# Optimizing a Trainium2 kernel written in Bass

```python
import math
import jax, jax.numpy as jnp
from jax import lax
import numpy as np

D_MODEL = 1024
BATCH = 1
SEQ = 256
DEPTH = 1

HEAD_DIM = 64
SB_HEADS = 8
MB_HEADS = 8
SB_WIDTH = SB_HEADS * HEAD_DIM
MB_WIDTH = MB_HEADS * HEAD_DIM
SB_QBLOCK = 128
MB_BLOCK = 256
MB_TOPK = 3
MB_QCHUNK = 64
REL_BUCKETS = 32
REL_MAX_DIST = 128
IN_WIDTH = 3 * SB_WIDTH + 3 * MB_WIDTH + 2 * D_MODEL
N_EXPERTS = 64
N_GROUPS = 8
TOPK_GROUPS = 4
TOPK_EXPERTS = 8
EXPERT_FF = 256
SHARED_FF = 256
ROUTED_SCALE = 2.5
MOE_ROW_BLOCK = 256
N_MOD = 6
EPS = 1e-6
NEG = -1e30


def rms_norm(x, g):
    x32 = x.astype(jnp.float32)
    y = x32 * lax.rsqrt(jnp.mean(x32 * x32, axis=-1, keepdims=True) + EPS)
    return (y * g.astype(jnp.float32)).astype(x.dtype)

def modulate(h, shift, scale):
    return h * (1.0 + scale[:, None, :]) + shift[:, None, :]

def split_heads(t, n_heads):
    b, s, _ = t.shape
    return t.reshape(b, s, n_heads, HEAD_DIM).transpose(0, 2, 1, 3)

def merge_heads(t):
    b, h, s, d = t.shape
    return t.transpose(0, 2, 1, 3).reshape(b, s, h * d)

def t5_bucket(dist):
    n = jnp.maximum(dist, 0)
    max_exact = REL_BUCKETS // 2
    nf = jnp.maximum(n, 1).astype(jnp.float32)
    large = max_exact + (jnp.log(nf / max_exact) / math.log(REL_MAX_DIST / max_exact)
                         * (REL_BUCKETS - max_exact)).astype(jnp.int32)
    large = jnp.minimum(large, REL_BUCKETS - 1)
    return jnp.where(n < max_exact, n, large)

def stick_breaking_attention(q, k, v):
    s_len = q.shape[2]
    scale = HEAD_DIM ** -0.5
    outs = []
    for i in range(s_len // SB_QBLOCK):
        q0 = i * SB_QBLOCK
        kend = q0 + SB_QBLOCK
        qb = q[:, :, q0:kend]
        kb = k[:, :, :kend]
        vb = v[:, :, :kend]
        z = jnp.einsum('bhqd,bhkd->bhqk', qb, kb).astype(jnp.float32) * scale
        qpos = q0 + jnp.arange(SB_QBLOCK)
        kpos = jnp.arange(kend)
        past = kpos[None, :] < qpos[:, None]
        log_beta = jax.nn.log_sigmoid(z)
        log_rest = jnp.where(past, jax.nn.log_sigmoid(-z), 0.0)
        log_skip = lax.cumsum(log_rest, axis=3, reverse=True) - log_rest
        a = jnp.where(past, jnp.exp(log_beta + log_skip), 0.0)
        outs.append(jnp.einsum('bhqk,bhkd->bhqd', a.astype(v.dtype), vb))
    return jnp.concatenate(outs, axis=2)

def moba_attention(q, k, v, rel_bias):
    b, h, s_len, dh = q.shape
    nb = -(-s_len // MB_BLOCK)
    sp = nb * MB_BLOCK
    pad = ((0, 0), (0, 0), (0, sp - s_len), (0, 0))
    kp = jnp.pad(k, pad)
    vp = jnp.pad(v, pad)
    kblk = kp.reshape(b, h, nb, MB_BLOCK, dh)
    vblk = vp.reshape(b, h, nb, MB_BLOCK, dh)
    kbar = jnp.mean(kblk.astype(jnp.float32), axis=3)
    topk = min(MB_TOPK, nb)
    scale = dh ** -0.5
    bi = jnp.arange(b)[:, None, None, None]
    hi = jnp.arange(h)[None, :, None, None]
    hi5 = hi[..., None]
    offs = jnp.arange(MB_BLOCK)

    def chunk(ci):
        q0 = ci * MB_QCHUNK
        qc = lax.dynamic_slice_in_dim(q, q0, MB_QCHUNK, axis=2)
        qpos = q0 + jnp.arange(MB_QCHUNK)
        blk = q0 // MB_BLOCK
        gate = jnp.einsum('bhqd,bhnd->bhqn', qc.astype(jnp.float32), kbar)
        gate = jnp.where(jnp.arange(nb) < blk, gate, NEG)
        _, sel = lax.top_k(gate, topk)
        valid = sel < blk
        ksel = kblk[bi, hi, sel]
        vsel = vblk[bi, hi, sel]
        kpos_sel = sel[..., None] * MB_BLOCK + offs
        bias_sel = rel_bias[hi5, t5_bucket(qpos[:, None, None] - kpos_sel)]
        s_sel = jnp.einsum('bhqd,bhqjnd->bhqjn', qc, ksel).astype(jnp.float32) * scale + bias_sel
        s_sel = jnp.where(valid[..., None], s_sel, NEG).reshape(b, h, MB_QCHUNK, topk * MB_BLOCK)
        k_own = lax.dynamic_slice_in_dim(kp, blk * MB_BLOCK, MB_BLOCK, axis=2)
        v_own = lax.dynamic_slice_in_dim(vp, blk * MB_BLOCK, MB_BLOCK, axis=2)
        dist = qpos[:, None] - (blk * MB_BLOCK + offs)[None, :]
        s_own = jnp.einsum('bhqd,bhnd->bhqn', qc, k_own).astype(jnp.float32) * scale
        s_own = jnp.where(dist >= 0, s_own + rel_bias[:, t5_bucket(dist)], NEG)
        p = jax.nn.softmax(jnp.concatenate([s_sel, s_own], axis=-1), axis=-1)
        p_sel = p[..., :topk * MB_BLOCK].reshape(b, h, MB_QCHUNK, topk, MB_BLOCK)
        p_own = p[..., topk * MB_BLOCK:]
        return (jnp.einsum('bhqjn,bhqjnd->bhqd', p_sel.astype(v.dtype), vsel)
                + jnp.einsum('bhqn,bhnd->bhqd', p_own.astype(v.dtype), v_own))

    outs = lax.map(chunk, jnp.arange(s_len // MB_QCHUNK))
    return outs.transpose(1, 2, 0, 3, 4).reshape(b, h, s_len, dh)

def swiglu(x, w_gate, w_up, w_down):
    return (jax.nn.silu(x @ w_gate) * (x @ w_up)) @ w_down

def moe_ffn(xt, w_router, router_bias, w_gate_e, w_up_e, w_down_e, w_gate_sh, w_up_sh, w_down_sh):
    t = xt.shape[0]
    scores = jax.nn.sigmoid((xt @ w_router).astype(jnp.float32))
    choice = scores + router_bias.astype(jnp.float32)
    grp = choice.reshape(t, N_GROUPS, N_EXPERTS // N_GROUPS)
    grp_score = jnp.sum(lax.top_k(grp, 2)[0], axis=-1)
    _, gidx = lax.top_k(grp_score, TOPK_GROUPS)
    gmask = jnp.any(gidx[..., None] == jnp.arange(N_GROUPS), axis=1)
    emask = jnp.repeat(gmask, N_EXPERTS // N_GROUPS, axis=1)
    _, eidx = lax.top_k(jnp.where(emask, choice, NEG), TOPK_EXPERTS)
    wts = jnp.take_along_axis(scores, eidx, axis=1)
    wts = wts / jnp.sum(wts, axis=-1, keepdims=True) * ROUTED_SCALE

    n_assign = t * TOPK_EXPERTS
    e_flat = eidx.reshape(n_assign)
    tok_flat = jnp.repeat(jnp.arange(t, dtype=jnp.int32), TOPK_EXPERTS)
    w_flat = wts.reshape(n_assign)
    order = jnp.argsort(e_flat)
    e_s = e_flat[order]
    counts = jnp.bincount(e_flat, length=N_EXPERTS)
    start = jnp.cumsum(counts) - counts
    pcounts = (counts + MOE_ROW_BLOCK - 1) // MOE_ROW_BLOCK * MOE_ROW_BLOCK
    pend = jnp.cumsum(pcounts)
    pstart = pend - pcounts
    dest = pstart[e_s] + (jnp.arange(n_assign) - start[e_s])
    n_blk = -(-n_assign // MOE_ROW_BLOCK) + N_EXPERTS
    n_rows = n_blk * MOE_ROW_BLOCK
    tok_buf = jnp.zeros((n_rows,), jnp.int32).at[dest].set(tok_flat[order])
    w_buf = jnp.zeros((n_rows,), jnp.float32).at[dest].set(w_flat[order])
    blk_expert = jnp.minimum(
        jnp.searchsorted(pend, jnp.arange(n_blk) * MOE_ROW_BLOCK, side='right'), N_EXPERTS - 1)

    def body(acc, bidx):
        rows = lax.dynamic_slice_in_dim(tok_buf, bidx * MOE_ROW_BLOCK, MOE_ROW_BLOCK)
        wr = lax.dynamic_slice_in_dim(w_buf, bidx * MOE_ROW_BLOCK, MOE_ROW_BLOCK)
        e = blk_expert[bidx]
        ye = swiglu(xt[rows], w_gate_e[e], w_up_e[e], w_down_e[e]) * wr[:, None]
        return acc.at[rows].add(ye.astype(acc.dtype)), None

    routed, _ = lax.scan(body, jnp.zeros_like(xt), jnp.arange(n_blk))
    return routed + swiglu(xt, w_gate_sh, w_up_sh, w_down_sh)

def first_inputs(seed: int = 0) -> dict:
    key = jax.random.key(seed)
    ks = jax.random.split(key, 24)
    f32 = jnp.float32
    L, D, E = DEPTH, D_MODEL, N_EXPERTS

    def nrm(k, shape, s):
        return jax.random.normal(k, shape, f32) * s

    return {
        "x": nrm(ks[0], (BATCH, SEQ, D), 1.0),
        "c": nrm(ks[1], (BATCH, D), 1.0),
        "norm1_g": 1.0 + nrm(ks[2], (L, D), 0.05),
        "norm2_g": 1.0 + nrm(ks[3], (L, D), 0.05),
        "w_ada": nrm(ks[4], (L, D, N_MOD * D), 0.5 * D ** -0.5),
        "b_ada": nrm(ks[5], (L, N_MOD * D), 0.02),
        "w_in": nrm(ks[6], (L, D, IN_WIDTH), D ** -0.5),
        "w_branch_sb": nrm(ks[7], (L, SB_WIDTH, D), SB_WIDTH ** -0.5),
        "w_branch_mb": nrm(ks[8], (L, MB_WIDTH, D), MB_WIDTH ** -0.5),
        "w_out": nrm(ks[9], (L, D, D), D ** -0.5),
        "w_router": nrm(ks[10], (L, D, E), D ** -0.5),
        "router_bias": nrm(ks[11], (L, E), 0.01),
        "w_gate_e": nrm(ks[12], (L, E, D, EXPERT_FF), D ** -0.5),
        "w_up_e": nrm(ks[13], (L, E, D, EXPERT_FF), D ** -0.5),
        "w_down_e": nrm(ks[14], (L, E, EXPERT_FF, D), EXPERT_FF ** -0.5),
        "w_gate_sh": nrm(ks[15], (L, D, SHARED_FF), D ** -0.5),
        "w_up_sh": nrm(ks[16], (L, D, SHARED_FF), D ** -0.5),
        "w_down_sh": nrm(ks[17], (L, SHARED_FF, D), SHARED_FF ** -0.5),
        "rel_bias": nrm(ks[18], (MB_HEADS, REL_BUCKETS), 0.5),
        "final_g": 1.0 + nrm(ks[19], (D,), 0.05),
    }

def first_block(x, c, norm1_g, norm2_g, w_ada, b_ada, w_in, w_branch_sb, w_branch_mb, w_out,
              w_router, router_bias, w_gate_e, w_up_e, w_down_e, w_gate_sh, w_up_sh, w_down_sh,
              rel_bias, final_g):
    b, s, d = x.shape
    cuts = [SB_WIDTH, 2 * SB_WIDTH, 3 * SB_WIDTH,
            3 * SB_WIDTH + MB_WIDTH, 3 * SB_WIDTH + 2 * MB_WIDTH, 3 * SB_WIDTH + 3 * MB_WIDTH,
            3 * SB_WIDTH + 3 * MB_WIDTH + D_MODEL]
    for l in range(DEPTH):
        mod = jax.nn.silu(c) @ w_ada[l] + b_ada[l]
        shift1, scale1, gate1, shift2, scale2, gate2 = jnp.split(mod, N_MOD, axis=-1)

        h = modulate(rms_norm(x, norm1_g[l]), shift1, scale1)
        proj = h @ w_in[l]
        q_sb, k_sb, v_sb, q_mb, k_mb, v_mb, g_sb, g_mb = jnp.split(proj, cuts, axis=-1)
        o_sb = stick_breaking_attention(split_heads(q_sb, SB_HEADS), split_heads(k_sb, SB_HEADS),
                                        split_heads(v_sb, SB_HEADS))
        o_mb = moba_attention(split_heads(q_mb, MB_HEADS), split_heads(k_mb, MB_HEADS),
                              split_heads(v_mb, MB_HEADS), rel_bias)
        merged = (jax.nn.sigmoid(g_sb) * (merge_heads(o_sb) @ w_branch_sb[l])
                  + jax.nn.sigmoid(g_mb) * (merge_heads(o_mb) @ w_branch_mb[l]))
        x = x + gate1[:, None, :] * (merged @ w_out[l])

        h2 = modulate(rms_norm(x, norm2_g[l]), shift2, scale2)
        y = moe_ffn(h2.reshape(b * s, d), w_router[l], router_bias[l], w_gate_e[l], w_up_e[l],
                    w_down_e[l], w_gate_sh[l], w_up_sh[l], w_down_sh[l]).reshape(b, s, d)
        x = x + gate2[:, None, :] * y
    return rms_norm(x, final_g)


D_CONV = D_MODEL
CONV_WIDTH = 3
MLA_HEADS = 8
QK_NOPE = 128
QK_ROPE = 64
V_HEAD = 128
Q_LORA = 256
KV_LORA = 128
ROPE_THETA = 10000.0
Q_BLOCK = 128
MEM_LEN = 256
MEM_HEADS = 4
MEM_HEAD_DIM = D_MODEL // MEM_HEADS
N_EXPERTS_2 = 16
EXPERT_FF_2 = 1024
CAPACITY_FACTOR = 2
IN_COLS = 3 * D_CONV + Q_LORA + KV_LORA + QK_ROPE + 2 * D_MODEL


def rmsnorm(x, g):
    xf = x.astype(jnp.float32)
    y = xf * lax.rsqrt(jnp.mean(xf * xf, axis=-1, keepdims=True) + EPS)
    return (y * g.astype(jnp.float32)).astype(x.dtype)

def rotary_tables(seq):
    inv = 1.0 / (ROPE_THETA ** (jnp.arange(0, QK_ROPE, 2, dtype=jnp.float32) / QK_ROPE))
    ang = jnp.arange(seq, dtype=jnp.float32)[:, None] * inv[None, :]
    return jnp.cos(ang), jnp.sin(ang)

def apply_rope(v, cos, sin):
    vf = v.astype(jnp.float32)
    v1, v2 = jnp.split(vf, 2, axis=-1)
    out = jnp.concatenate([v1 * cos - v2 * sin, v1 * sin + v2 * cos], axis=-1)
    return out.astype(v.dtype)

def short_conv(v, w, b):
    y = lax.conv_general_dilated(
        v, w[:, None, :].astype(v.dtype), window_strides=(1,), padding=((1, 1),),
        dimension_numbers=("NWC", "WIO", "NWC"), feature_group_count=v.shape[-1])
    return y + b.astype(v.dtype)

def mla_attention(q_nope, q_rope, k_nope, k_rope, v):
    b, s, h, _ = q_nope.shape
    nb = s // Q_BLOCK
    scale = (QK_NOPE + QK_ROPE) ** -0.5
    qn = q_nope.reshape(b, nb, Q_BLOCK, h, QK_NOPE).transpose(1, 0, 2, 3, 4)
    qr = q_rope.reshape(b, nb, Q_BLOCK, h, QK_ROPE).transpose(1, 0, 2, 3, 4)

    def block(args):
        qn_b, qr_b = args
        sc = (jnp.einsum("bqhd,bkhd->bhqk", qn_b, k_nope)
              + jnp.einsum("bqhr,bkr->bhqk", qr_b, k_rope))
        p = jax.nn.softmax(sc.astype(jnp.float32) * scale, axis=-1).astype(v.dtype)
        return jnp.einsum("bhqk,bkhd->bqhd", p, v)

    o = lax.map(block, (qn, qr))
    return o.transpose(1, 0, 2, 3, 4).reshape(b, s, h * V_HEAD)

def memory_cross_attention(h, m, w_q, w_kv, w_o):
    b, s, _ = h.shape
    ml = m.shape[1]
    q = (h @ w_q).reshape(b, s, MEM_HEADS, MEM_HEAD_DIM)
    kv = (m @ w_kv).reshape(b, ml, 2, MEM_HEADS, MEM_HEAD_DIM)
    k, v = kv[:, :, 0], kv[:, :, 1]
    sc = jnp.einsum("bqhd,bkhd->bhqk", q, k).astype(jnp.float32) * (MEM_HEAD_DIM ** -0.5)
    p = jax.nn.softmax(sc, axis=-1).astype(v.dtype)
    o = jnp.einsum("bhqk,bkhd->bqhd", p, v).reshape(b, s, MEM_HEADS * MEM_HEAD_DIM)
    return o @ w_o

def expert_choice_moe(h, w_router, w_gate, w_up, w_down):
    b, s, d = h.shape
    cap = max(1, CAPACITY_FACTOR * s // N_EXPERTS_2)
    aff = jax.nn.softmax((h @ w_router).astype(jnp.float32), axis=-1)
    gates, idx = lax.top_k(jnp.swapaxes(aff, 1, 2), cap)
    xg = jax.vmap(lambda hb, ib: hb[ib])(h, idx)
    a = jax.nn.silu(jnp.einsum("becd,edf->becf", xg, w_gate)) * jnp.einsum("becd,edf->becf", xg, w_up)
    yo = jnp.einsum("becf,efd->becd", a, w_down) * gates[..., None].astype(h.dtype)
    return jax.vmap(lambda ib, vb: jnp.zeros((s, d), vb.dtype).at[ib.reshape(-1)].add(vb.reshape(-1, d)))(idx, yo)

def second_inputs(seed: int = 0) -> dict:
    key = jax.random.key(seed)
    ks = jax.random.split(key, 32)

    def w(k, shape, fan_in):
        return jax.random.normal(k, shape, jnp.float32) * fan_in ** -0.5

    def g(k, shape):
        return 1.0 + 0.02 * jax.random.normal(k, shape, jnp.float32)

    def bias(k, shape):
        return 0.02 * jax.random.normal(k, shape, jnp.float32)

    L = DEPTH
    return {
        "x": jax.random.normal(ks[0], (BATCH, SEQ, D_MODEL), jnp.float32),
        "mem": jax.random.normal(ks[1], (BATCH, MEM_LEN, D_MODEL), jnp.float32),
        "norm_mix_g": g(ks[2], (L, D_MODEL)),
        "w_in": w(ks[3], (L, D_MODEL, IN_COLS), D_MODEL),
        "conv_w": w(ks[4], (L, CONV_WIDTH, D_CONV), CONV_WIDTH),
        "conv_b": bias(ks[5], (L, D_CONV)),
        "w_conv_out": w(ks[6], (L, D_CONV, D_MODEL), D_CONV),
        "q_norm_g": g(ks[7], (L, Q_LORA)),
        "w_uq": w(ks[8], (L, Q_LORA, MLA_HEADS * (QK_NOPE + QK_ROPE)), Q_LORA),
        "kv_norm_g": g(ks[9], (L, KV_LORA)),
        "w_ukv": w(ks[10], (L, KV_LORA, MLA_HEADS * (QK_NOPE + V_HEAD)), KV_LORA),
        "w_mla_out": w(ks[11], (L, MLA_HEADS * V_HEAD, D_MODEL), MLA_HEADS * V_HEAD),
        "b_gate": bias(ks[12], (L, 2 * D_MODEL)),
        "w_mix_out": w(ks[13], (L, D_MODEL, D_MODEL), D_MODEL),
        "norm_mem_g": g(ks[14], (L, D_MODEL)),
        "norm_memkv_g": g(ks[15], (L, D_MODEL)),
        "w_mem_q": w(ks[16], (L, D_MODEL, MEM_HEADS * MEM_HEAD_DIM), D_MODEL),
        "w_mem_kv": w(ks[17], (L, D_MODEL, 2 * MEM_HEADS * MEM_HEAD_DIM), D_MODEL),
        "w_mem_out": w(ks[18], (L, MEM_HEADS * MEM_HEAD_DIM, D_MODEL), MEM_HEADS * MEM_HEAD_DIM),
        "norm_moe_g": g(ks[19], (L, D_MODEL)),
        "w_router": w(ks[20], (L, D_MODEL, N_EXPERTS_2), D_MODEL),
        "w_exp_gate": w(ks[21], (L, N_EXPERTS_2, D_MODEL, EXPERT_FF_2), D_MODEL),
        "w_exp_up": w(ks[22], (L, N_EXPERTS_2, D_MODEL, EXPERT_FF_2), D_MODEL),
        "w_exp_down": w(ks[23], (L, N_EXPERTS_2, EXPERT_FF_2, D_MODEL), EXPERT_FF_2),
        "norm_final_g": g(ks[24], (D_MODEL,)),
    }

def second_block(x, mem, norm_mix_g, w_in, conv_w, conv_b, w_conv_out, q_norm_g, w_uq, kv_norm_g,
              w_ukv, w_mla_out, b_gate, w_mix_out, norm_mem_g, norm_memkv_g, w_mem_q, w_mem_kv,
              w_mem_out, norm_moe_g, w_router, w_exp_gate, w_exp_up, w_exp_down, norm_final_g):
    b, s, _ = x.shape
    cos, sin = rotary_tables(s)
    splits = list(np.cumsum([D_CONV, D_CONV, D_CONV, Q_LORA, KV_LORA, QK_ROPE]))
    for l in range(DEPTH):
        h = rmsnorm(x, norm_mix_g[l])
        u = h @ w_in[l]
        xc, gb, gc, cq, ckv, kr, glog = jnp.split(u, splits, axis=-1)
        y_conv = (gb * short_conv(gc * xc, conv_w[l], conv_b[l])) @ w_conv_out[l]
        q = (rmsnorm(cq, q_norm_g[l]) @ w_uq[l]).reshape(b, s, MLA_HEADS, QK_NOPE + QK_ROPE)
        q_nope, q_rope = q[..., :QK_NOPE], apply_rope(q[..., QK_NOPE:], cos[None, :, None, :], sin[None, :, None, :])
        kv = (rmsnorm(ckv, kv_norm_g[l]) @ w_ukv[l]).reshape(b, s, MLA_HEADS, QK_NOPE + V_HEAD)
        k_nope, v = kv[..., :QK_NOPE], kv[..., QK_NOPE:]
        k_rope = apply_rope(kr, cos[None], sin[None])
        y_mla = mla_attention(q_nope, q_rope, k_nope, k_rope, v) @ w_mla_out[l]
        gates = jax.nn.sigmoid((glog + b_gate[l]).astype(jnp.float32)).astype(x.dtype)
        g_conv, g_mla = gates[..., :D_MODEL], gates[..., D_MODEL:]
        x = x + (g_conv * y_conv + g_mla * y_mla) @ w_mix_out[l]
        x = x + memory_cross_attention(rmsnorm(x, norm_mem_g[l]), rmsnorm(mem, norm_memkv_g[l]),
                                       w_mem_q[l], w_mem_kv[l], w_mem_out[l])
        x = x + expert_choice_moe(rmsnorm(x, norm_moe_g[l]), w_router[l], w_exp_gate[l],
                                  w_exp_up[l], w_exp_down[l])
    return rmsnorm(x, norm_final_g)


def setup_inputs(seed=0):
    out = dict(first_inputs(seed))
    for name, value in second_inputs(seed + 1).items():
        if name != "x":
            out[name + "_2"] = value
    return out


def reference(
    x, c, norm1_g, norm2_g, w_ada, b_ada, w_in, w_branch_sb, w_branch_mb, w_out, w_router,
    router_bias, w_gate_e, w_up_e, w_down_e, w_gate_sh, w_up_sh, w_down_sh, rel_bias, final_g,
    mem_2, norm_mix_g_2, w_in_2, conv_w_2, conv_b_2, w_conv_out_2, q_norm_g_2, w_uq_2,
    kv_norm_g_2, w_ukv_2, w_mla_out_2, b_gate_2, w_mix_out_2, norm_mem_g_2, norm_memkv_g_2,
    w_mem_q_2, w_mem_kv_2, w_mem_out_2, norm_moe_g_2, w_router_2, w_exp_gate_2, w_exp_up_2,
    w_exp_down_2, norm_final_g_2,
):
    x = first_block(
        x, c, norm1_g, norm2_g, w_ada, b_ada, w_in, w_branch_sb, w_branch_mb, w_out, w_router,
        router_bias, w_gate_e, w_up_e, w_down_e, w_gate_sh, w_up_sh, w_down_sh, rel_bias,
        final_g,
    )
    return second_block(
        x, mem_2, norm_mix_g_2, w_in_2, conv_w_2, conv_b_2, w_conv_out_2, q_norm_g_2, w_uq_2,
        kv_norm_g_2, w_ukv_2, w_mla_out_2, b_gate_2, w_mix_out_2, norm_mem_g_2, norm_memkv_g_2,
        w_mem_q_2, w_mem_kv_2, w_mem_out_2, norm_moe_g_2, w_router_2, w_exp_gate_2, w_exp_up_2,
        w_exp_down_2, norm_final_g_2,
    )


_drawn_inputs = setup_inputs


def setup_inputs(seed=0):
    import zlib

    import numpy as np

    out = dict(_drawn_inputs(seed))
    spreads = {}
    factors = {'norm_mix_g_2': 2.917,
     'conv_b_2': 4.249,
     'q_norm_g_2': 8.0,
     'kv_norm_g_2': 8.0,
     'b_gate_2': 8.0,
     'norm_mem_g_2': 8.0,
     'norm_memkv_g_2': 8.0,
     'norm_moe_g_2': 10.209,
     'norm_final_g_2': 8.031}
    for name, (base, spread) in spreads.items():
        noise = np.random.default_rng([zlib.crc32(name.encode()), seed]).standard_normal(out[name].shape)
        drawn = base * np.exp(spread * noise) if base else spread * noise
        out[name] = __import__('jax').numpy.asarray(drawn.astype(out[name].dtype))
    for name, factor in factors.items():
        out[name] = (out[name] * factor).astype(out[name].dtype)
    return out
```

```python
import math
from contextlib import ExitStack

import numpy as np
import concourse.bass as bass
from concourse import mybir

F32 = mybir.dt.float32
F32R = mybir.dt.float32r
I32 = mybir.dt.int32
ALU = mybir.AluOpType
ACT = mybir.ActivationFunctionType
AX = mybir.AxisListType.X

P = 128
D = 1024
KT = D // P
T = 256
TT = T // P
EPS = 1e-6
NEG = -1e30
HEADS = 8
HD = 64
E1, FF1, SLOTS1 = 64, 256, 64
GROUPS, TOPK = 8, 8
PAIRS_PER_TURN = 2
TURNS1 = E1 // (2 * PAIRS_PER_TURN)
EXTRA = T * TOPK // SLOTS1
ITEMS = E1 + EXTRA + 4
FAR = 1.0e6
E2, FF2, CAP2 = 16, 1024, 32
TURNS2 = E2 // 4
MLA_NOPE, MLA_ROPE, MLA_V = 128, 64, 128
QL, KVL = 256, 128
MEMH = 4
RING, SLOT = 6, 4096
BANKS = 7
PAD = 383

VEC = {}
for _name, _rows in (("c", 8), ("b_ada", 48), ("norm1_g", 8), ("norm2_g", 8), ("final_g", 8), ("norm_mix_g_2", 8),
                     ("norm_mem_g_2", 8), ("norm_memkv_g_2", 8), ("norm_moe_g_2", 8), ("norm_final_g_2", 8)):
    VEC[_name] = (sum(n for _, n in VEC.values()), _rows)
VEC2 = {}
for _name, _rows in (("b_gate_2", 16), ("conv_w_2", 24), ("conv_b_2", 8), ("q_norm_g_2", 2), ("kv_norm_g_2", 1),
                     ("rel_bias", 8)):
    VEC2[_name] = (sum(n for _, n in VEC2.values()), _rows)

C_ID, C_BEFORE, C_ONES, C_BEFORE2, C_AFTER, C_IOTA, C_SEL, C_PIDX = 0, 128, 256, 384, 512, 640, 768, 769
C_WIDTH = 770
R_COS, R_SIN, R_PERM, R_WIDTH = 0, 256, 512, 640


def shape_tables():
    r = np.arange(P)
    cst = np.zeros((P, C_WIDTH), np.float32)
    cst[:, C_ID:C_ID + P] = np.eye(P)
    before = (r[:, None] < r[None, :]).astype(np.float32)
    cst[:, C_BEFORE:C_BEFORE + P] = before
    cst[:, C_ONES:C_ONES + P] = 1.0
    cst[:, C_BEFORE2:C_BEFORE2 + P] = before
    cst[:, C_AFTER:C_AFTER + P] = before.T
    cst[:, C_IOTA:C_IOTA + P] = r[None, :]
    cst[::32, C_SEL] = 1.0
    cst[:, C_PIDX] = r
    half = MLA_ROPE // 2
    inv = (1.0 / (10000.0 ** (np.arange(0, MLA_ROPE, 2, dtype=np.float32) / np.float32(MLA_ROPE)))).astype(np.float32)
    ang = np.arange(T, dtype=np.float32)[None, :] * inv[:, None]
    rope = np.zeros((P, R_WIDTH), np.float32)
    for b in range(0, P, MLA_ROPE):
        rope[b:b + half, R_COS:R_COS + T] = np.cos(ang)
        rope[b + half:b + MLA_ROPE, R_COS:R_COS + T] = np.cos(ang)
        rope[b:b + half, R_SIN:R_SIN + T] = -np.sin(ang)
        rope[b + half:b + MLA_ROPE, R_SIN:R_SIN + T] = np.sin(ang)
        for i in range(MLA_ROPE):
            rope[b + i, R_PERM + b + (i + half) % MLA_ROPE] = 1.0
    n = np.arange(T - 1, -1, -1)
    nf = np.maximum(n, 1).astype(np.float32)
    large = 16 + (np.log(nf / np.float32(16)) / np.float32(math.log(8.0)) * np.float32(16)).astype(np.int32)
    bucket = np.where(n < 16, n, np.minimum(large, 31))
    onehot = (np.arange(32)[:, None] == bucket[None, :]).astype(np.float32)
    return {"cst": cst, "rope": rope, "buckets": onehot}


ADA_FIRST, ADA = 4, 12
IN_A = {}
CHUNKS_A = [("w_ada", 512 * _j, 512, 8) for _j in range(ADA_FIRST)] + [("w_mem_kv_2", 512 * _j, 512, 8) for _j in range(4)]
for _c in range(10):
    IN_A[_c] = len(CHUNKS_A)
    CHUNKS_A += [("w_in", 512 * _c, 512, 8)]
    CHUNKS_A += [("w_ada", 512 * _j, 512, 8) for _j in range(ADA_FIRST + 2 * _c, min(ADA_FIRST + 2 * _c + 2, ADA))]
CHUNKS_A += [("w_branch_sb", 0, 1024, 4), ("w_branch_mb", 0, 1024, 4), ("w_out", 0, 512, 8), ("w_out", 512, 512, 8),
             ("shared_gu", 0, 0, 0), ("w_down_sh", 0, 1024, 2)]
CHUNKS_B = [("w_in_2", 3072, 448, 8), ("w_in_2", 0, 512, 8), ("w_in_2", 512, 512, 8), ("w_uq_2", 0, 1536, 2), ("w_ukv_2", 0, 2048, 1)]
CHUNKS_B += [("w_in_2", _c, 512, 8) for _c in (1024, 1536, 2048, 2560, 3520, 4032, 4544, 5056)]
CHUNKS_B += [(_w, _c, 512, 8) for _w in ("w_conv_out_2", "w_mla_out_2", "w_mix_out_2", "w_mem_q_2", "w_mem_out_2")
             for _c in (0, 512)]
NA, NB = len(CHUNKS_A), len(CHUNKS_B)

JOBS = ["vec"] + [f"memT{j}" for j in range(4)] + [f"xT{j}" for j in range(4)] + ["ms0", "ms1"]
JOBS += [f"ada{_j}" for _j in range(ADA_FIRST)] + [f"memkv{_g}_{_j}" for _g in range(4) for _j in range(2)]
JOBS += [f"rel{h}" for h in range(HEADS)]
for _c in range(6):
    JOBS += [f"in{_c}_{_j}" for _j in range(2)] + [f"ada{_j}" for _j in range(ADA_FIRST + 2 * _c, min(ADA_FIRST + 2 * _c + 2, ADA))]
for _s in range(HEADS + 2):
    if _s < HEADS:
        JOBS += [f"z{_s}", f"s{_s}", f"in{6 + _s // 2}_{_s % 2}"]
    if 1 <= _s <= HEADS:
        JOBS += [f"skip{_s - 1}", f"pT{_s - 1}"]
    if _s >= 2:
        JOBS += [f"av{_s - 2}"]
JOBS += [f"br{_b}_{_j}" for _j in range(4) for _b in ("s", "m")] + [f"out{j}" for j in range(4)] + ["ms2", "route1"]
JOBS += [f"hN{j}" for j in range(4)] + ["shg", "shu", "rank1", "count1", "start1", "tabT", "item", "eidx"]
JOBS += ["ms3", "ms4", "cq", "ckv"] + [f"xc{j}" for j in range(2)] + ["msq"] + [f"xc{j}" for j in range(2, 4)]
JOBS += [f"qn{j}" for j in range(4)] + [f"qr{j}" for j in range(2)] + [f"kn{j}" for j in range(4)] + \
        [f"v{j}" for j in range(4)] + [f"rot{j}" for j in range(3)]
for _s in range(HEADS + 2):
    if _s < HEADS:
        JOBS += [f"ls{_s}", f"fill{2 * _s}"]
    if 1 <= _s <= HEADS:
        JOBS += [f"lp{_s - 1}"]
    if _s < HEADS:
        JOBS += [f"fill{2 * _s + 1}"]
    if _s >= 2:
        JOBS += [f"lo{_s - 2}"]
JOBS += [f"conv{j}" for j in range(4)] + [f"mla{j}" for j in range(4)] + [f"mix{j}" for j in range(4)] + ["ms5"]
JOBS += [f"mq{j}" for j in range(4)]
for _s in range(MEMH + 1):
    if _s < MEMH:
        JOBS += [f"mS{_s}"]
    if _s >= 1:
        JOBS += [f"mP{_s - 1}", f"mO{_s - 1}"]
JOBS += [f"mo{j}" for j in range(4)] + ["ms6", "route2"] + [f"gN{j}" for j in range(4)]
JOBS += ["affT", "selT", "rank2"]
JOBS2 = ["ms7"] + [f"oN{j}" for j in range(4)]
AT = {name: (n % BANKS, n // BANKS) for n, name in enumerate(JOBS)}
for _n, _name in enumerate(JOBS2):
    AT[_name] = ((len(JOBS) + _n) % BANKS, (len(JOBS) + _n) // BANKS)
assert len(AT) == len(JOBS) + len(JOBS2)


def last_uses(names):
    return list({AT[n][0]: n for n in names}.values())


def build(nc, a, out):
    ctx = ExitStack()
    with ctx:
        def sb(name, shape, dt=F32):
            return ctx.enter_context(nc.sbuf_tensor(name, shape, dt))

        def sem(name):
            return ctx.enter_context(nc.semaphore(name))

        ring = sb("ring", [P, RING, SLOT])
        NBUF, BUF = 13, KT * T
        sb("arena_place", [P, NBUF * BUF])
        place = nc.sbuf_base - NBUF * BUF * 4
        arena = nc.alloc_sbuf_tensor_at("arena", [P, NBUF * BUF], F32, offset=place)
        arena_r = nc.alloc_sbuf_tensor_at("arena_r", [P, NBUF * BUF], F32R, offset=place)
        cst = sb("constants", [P, C_WIDTH])
        vec = sb("vectors", [P, 256])
        mod = sb("mod", [P, 48])
        items = sb("items", [P, 2, TT, ITEMS])
        small = sb("small", [P, 192])
        rbias = sb("router_bias_rows", [P, E1])
        tab_i = sb("item_table", [1, 64], I32)
        psum = ctx.enter_context(nc.psum_tensor("psum", [P, 8, 512], F32))
        bias_dram = nc.dram_tensor("bias_rows", (HEADS, P, PAD), F32, kind="Internal").ap()

        def buf(i, n=BUF, off=0):
            return arena[:, i * BUF + off:i * BUF + off + n]

        def buf_r(i, n=BUF, off=0):
            return arena_r[:, i * BUF + off:i * BUF + off + n]

        def tiles(i, n=KT):
            return buf(i, n * T).rearrange("p (k t) -> p k t", t=T)

        ident = cst[:, C_ID:C_ID + P]
        before = cst[:, C_BEFORE:C_BEFORE + P]
        after = cst[:, C_AFTER:C_AFTER + P]
        ones = cst[:, C_ONES:C_ONES + P]
        mask3 = cst[:, C_BEFORE:C_BEFORE + 3 * P]
        iota = cst[:, C_IOTA:C_IOTA + P]

        xT, hT = tiles(0), tiles(1)
        QK = tiles(2, 16)
        V1 = buf(4).rearrange("p (t f) -> p t f", t=TT)
        G1 = tiles(5, 16)
        OT = tiles(7)
        merged = tiles(2)
        memK, memV = tiles(11), buf(12).rearrange("p (t f) -> p t f", t=TT)
        xN, memN = (buf(i).rearrange("p (t f) -> p t f", t=TT) for i in (4, 5))
        memT = tiles(1)
        sq = [tiles(8), tiles(9)]
        vec_rows = buf(6, 256, 0).rearrange("p (a c) -> p a c", a=2)
        csil = buf(6, 8, 256)
        cs32 = buf(6, 256, 512).rearrange("p (k c) -> p k c", k=KT)
        ada_rows = [buf(6, 512, 1024), buf(6, 512, 1536)]
        relb = buf(7, HEADS * P).rearrange("p (h c) -> p h c", h=HEADS)
        onehot = buf(7, T, HEADS * P)
        bias_st = buf(2, HEADS * PAD).rearrange("p (h c) -> p h c", h=HEADS)
        biasT = buf(10).rearrange("p (h c) -> p h c", h=HEADS)
        W3 = 3 * P
        sc_L = buf(8, W3, 0)
        sc_lr = buf(8, W3, W3)
        sc_lb = [buf(8, W3, (2 + i) * W3) for i in range(2)]
        sc_a = [buf(8, W3, (4 + i) * W3) for i in range(2)]
        sc_p = [buf(8, W3, (6 + i) * W3) for i in range(2)]
        sc_pT = [buf(8, W3, (8 + i) * W3) for i in range(2)]
        mx1 = small[:, 0:4].rearrange("p (i t) -> p i t", i=2)
        sm1 = small[:, 4:8].rearrange("p (i t) -> p i t", i=2)
        rstd_lo = buf(8, 2 * T, 1024)

        def rstd_of(n):
            return buf(8, T, (n % 2) * T)

        gs = small[:, 8:24]
        wr1 = buf(10, KT * E1).rearrange("p (k e) -> p k e", k=KT)
        hN = buf(2).rearrange("p (t f) -> p t f", t=TT)
        hN_hi, hN_lo = (buf_r(i).rearrange("p (t f) -> p t f", t=TT) for i in (2, 3))
        hN_hi32 = buf_r(2).bitcast(F32).rearrange("p (t f) -> p t f", t=TT)
        xg1 = buf(8).rearrange("p (k c) -> p k c", k=KT)
        Pg1 = buf_r(5, 2 * T, 0).rearrange("p (t c) -> p t c", t=TT)
        Pg1_32 = buf_r(5, 2 * T, 0).bitcast(F32).rearrange("p (t c) -> p t c", t=TT)
        Pw1 = buf(5, 2 * T, 2 * T).rearrange("p (t c) -> p t c", t=TT)
        PT1 = [buf_r(5, T, (4 + i) * T) for i in range(2)]
        y_hi, y_lo = buf_r(6, D, 0), buf_r(6, D, D)
        y_hi32 = y_hi.bitcast(F32)
        sil1, aT1 = buf(10, 256, 1024), buf(10, 256, 1280)
        wslot = small[:, 48:50]
        xg = buf(3, KT * P).rearrange("p (k c) -> p k c", k=KT)
        shg_s, sha = tiles(4, 2), buf(4, 512, 512).rearrange("p (k t) -> p k t", t=T)
        rt = buf(7)
        Pg = buf(5, TT * P, 0).rearrange("p (t c) -> p t c", t=TT)
        Pw = buf(5, TT * P, 256).rearrange("p (t c) -> p t c", t=TT)
        PwT = buf(5, T, 512)
        gu_s = buf(5, 512, 1536)
        y_s = buf(6, D, 0)
        gates = tiles(2, 16)
        xcT, gbT = tiles(4), tiles(5)
        low = tiles(7)
        qnT, knT = tiles(6), tiles(8)
        vN = buf(9).rearrange("p (t f) -> p t f", t=TT)
        oT = qnT
        rope = buf(10, R_WIDTH)
        lsq = buf(9, 3 * T).rearrange("p (k t) -> p k t", t=T)
        spare = buf(5, 2 * T)
        at_p = [buf(10, 512, 0), buf(10, 512, 512)]
        at_pT = [buf(10, 512, 1024), buf(10, 512, 1536)]
        mx2 = small[:, 24:28].rearrange("p (i t) -> p i t", i=2)
        sm2 = small[:, 28:32].rearrange("p (i t) -> p i t", i=2)
        mqT, moT = tiles(8), tiles(9)
        wr2 = buf(5, KT * E2).rearrange("p (k e) -> p k e", k=KT)
        yn = tiles(4)
        rt2 = rt[:, 0:TT * E2].rearrange("p (t e) -> p t e", t=TT)
        sel2 = rt[:, 64:64 + TT * E2]
        sil2 = buf(6, 256, 1024)
        aT2 = [buf(4, 256, 256 * e).rearrange("p (k c) -> p k c", c=CAP2) for e in range(4)]
        zeros = buf(4, P, 1024)

        def vcol(name, k):
            table, off = (VEC, 0) if name in VEC else (VEC2, P)
            return vec[:, off + table[name][0] + k:off + table[name][0] + k + 1]

        def vcols(name):
            table, off = (VEC, 0) if name in VEC else (VEC2, P)
            return vec[:, off + table[name][0]:off + table[name][0] + table[name][1]]

        rows_in, x_in, mem_in, cst_in = sem("vector_rows_arrived"), sem("x_arrived"), sem("mem_arrived"), sem("constants_arrived")
        bias_out, bias_in = sem("bias_rows_written"), sem("bias_table_arrived")
        wr1_in, rope_in, wr2_in = sem("router1_arrived"), sem("rope_arrived"), sem("router2_arrived")
        out_done = sem("output_written")
        load_a = [sem(f"ring_slot{i}_loaded_a") for i in range(RING)]
        load_b = [sem(f"ring_slot{i}_loaded_b") for i in range(RING)]
        used_a, used_b = sem("chunks_used_a"), sem("chunks_used_b")
        bank_full = [sem(f"bank{i}_full") for i in range(BANKS)]
        bank_free = [sem(f"bank{i}_free") for i in range(BANKS)]
        squares_ready, mean_ready, rstd_ready, normed = (sem(n) for n in ("squares_ready", "mean_ready", "rstd_ready", "normed"))
        dve_step, act_step = sem("dve_step"), sem("act_step")
        rows_zeroed, csil_ready, cs32_ready, mod_full, mod_ready = (
            sem(n) for n in ("rows_zeroed", "c_silu_ready", "c_silu_wide_ready", "mod_columns_full", "mod_ready"))
        relb_ready, bias_staged = sem("rel_bias_wide_ready"), sem("bias_staged")
        sb_abs, sb_soft, sb_rest, sb_arg, sb_exp, sb_a = (
            sem(n) for n in ("sb_abs_ready", "sb_softplus_ready", "sb_log_rest_ready", "sb_log_a_ready", "sb_exp_ready", "sb_a_ready"))
        at_max, at_exp, at_p_ready = sem("softmax_max_ready"), sem("softmax_exp_ready"), sem("softmax_p_ready")
        gates_exp, gates_ready = sem("gates_exp_ready"), sem("gates_ready")
        merged_ready, x_ready = sem("merged_ready"), sem("residual_ready")
        act_func = sem("act_value_ready")
        sh_ready, route_ready = sem("shared_hidden_ready"), sem("routing_step_ready")
        table_ready = sem("item_table_ready")
        hn_high = sem("h_rows_high_ready")
        y_high0, y_high1, y_copied = sem("y0_high_ready"), sem("y1_high_ready"), sem("y_split")
        p_ready, gathered, g_copied = sem("onehot_ready"), sem("gathered"), sem("gather_copied")
        gu_copied, turned, sil_ready, aT_ready = sem("gu_copied"), sem("gu_transposed"), sem("silu_ready"), sem("hidden_ready")
        y0_done, pT_done, pT_copied, scattered = (sem(n) for n in ("y0_done", "onehot_transposed", "onehot_copied", "scattered"))
        acc_ready, acc_read = sem("accumulators_ready"), sem("accumulators_read")
        q_scaled, rope_done, conv_ready = sem("low_rank_normed"), sem("rotated"), sem("convolved")
        p2_ready, gathered2, g2_copied, pwT2_done, pwT2_copied, gu2_copied, turned2, sil2_ready, aT2_ready, y20_copied, y21_copied, scattered2 = (
            sem(n + "_moe2") for n in ("onehot_ready", "gathered", "gather_copied", "weights_transposed", "weights_copied", "gu_copied",
                                       "gu_transposed", "silu_ready", "hidden_ready", "y0_copied", "y1_copied", "scattered"))

        block = ctx.enter_context(nc.Block())

        def bank(name):
            return psum[:, AT[name][0], :]

        def full(eng, name):
            eng.wait_ge(bank_full[AT[name][0]], AT[name][1] + 1)
            return bank(name)

        def evacuated(eng, name):
            eng.wait_ge(bank_free[AT[name][0]], AT[name][1] + 1)

        def frees(ins, name):
            ins.then_inc(bank_free[AT[name][0]], 1)

        def slot_a(n):
            return ring[:, n % RING, :]

        def slot_b(n):
            return ring[:, (NA + n) % RING, :]

        CA = {c: n for n, c in enumerate(CHUNKS_A)}
        CB = {c: n for n, c in enumerate(CHUNKS_B)}

        @block.sync
        def _(sp):
            def load(ap, spec, done):
                name, c0, cols, k = spec
                if name == "shared_gu":
                    half = ap.rearrange("p (g k f) -> p g k f", g=2, k=KT)
                    sp.dma_start(half[:, 0], a["w_gate_sh"][0].rearrange("(k p) f -> p k f", p=P)).then_inc(done, 16)
                    sp.dma_start(half[:, 1], a["w_up_sh"][0].rearrange("(k p) f -> p k f", p=P)).then_inc(done, 16)
                else:
                    sp.dma_start(ap[:, 0:k * cols].rearrange("p (k c) -> p k c", k=k),
                                 a[name][0, :, c0:c0 + cols].rearrange("(k p) c -> p k c", p=P)).then_inc(done, 16)

            sp.dma_start(memN, a["mem_2"][0].rearrange("(t p) f -> p t f", p=P)).then_inc(mem_in, 16)
            sp.dma_start(xN, a["x"][0].rearrange("(t p) f -> p t f", p=P)).then_inc(x_in, 16)
            sp.wait_ge(cst_in, 48)
            sp.wait_ge(rows_in, 16 * (len(VEC) + len(VEC2)))
            for n, spec in enumerate(CHUNKS_A):
                if n >= RING:
                    sp.wait_ge(used_a, n - RING + 1)
                load(slot_a(n), spec, load_a[n % RING])

            def moe1_chunk(c, experts, done):
                s = (NA + c) % RING
                pair, what = c // 3, c % 3
                if what < 2:
                    e = experts[2 * pair + what]
                    dst = ring[:, s, :].rearrange("p (g k f) -> p g (k f)", g=2, k=KT)
                    for g, w in enumerate(("w_gate_e", "w_up_e")):
                        sp.dma_start(dst[:, g], a[w][0, e].rearrange("(p k) f -> p (k f)", p=P)).then_inc(done, 16)
                else:
                    dst = ring[:, s, :].rearrange("p (e k) -> p e k", e=2)
                    for j in range(2):
                        sp.dma_start(dst[:, j], a["w_down_e"][0, experts[2 * pair + j]].rearrange("(p k) f -> p (k f)", p=P))\
                          .then_inc(done, 16)

            with sp.Fori(0, TURNS1) as i:
                for c in range(6):
                    sp.wait_ge(used_a, i * 6 + (NA + c - RING + 1))
                    moe1_chunk(c, [i * 4 + j for j in range(4)], load_a[(NA + c) % RING])
            sp.wait_ge(table_ready, 1)
            extra = sp.value_load(tab_i[0:1, 32:33], min_val=0, max_val=EXTRA // 4)
            turns = sp.snap(extra + TURNS1)
            with sp.If(extra > 0):
                with sp.Fori(TURNS1, turns) as i:
                    es = [sp.value_load(tab_i[0:1, bass.ds(i * 4 + (j - E1), 1)], min_val=0, max_val=E1 - 1) for j in range(4)]
                    for c in range(6):
                        sp.wait_ge(used_a, i * 6 + (NA + c - RING + 1))
                        moe1_chunk(c, es, load_a[(NA + c) % RING])
            for n, spec in enumerate(CHUNKS_B):
                if n < RING:
                    sp.wait_ge(used_a, turns * 6 + (NA + n - RING + 1))
                else:
                    sp.wait_ge(used_b, n - RING + 1)
                load(slot_b(n), spec, load_b[(NA + n) % RING])
            with sp.Fori(0, TURNS2) as i:
                for c in range(24):
                    s = (NA + NB + c) % RING
                    sp.wait_ge(used_b, i * 24 + (NB + c - RING + 1))
                    if c < 16:
                        dst = ring[:, s, :].rearrange("p (g k) -> p g k", g=2)
                        for g, w in enumerate(("w_exp_gate_2", "w_exp_up_2")):
                            src = a[w][0, i * 4 + c // 4].rearrange("(p k) f -> p (k f)", p=P)
                            sp.dma_start(dst[:, g], src[:, (c % 4) * 2 * FF2:((c % 4) + 1) * 2 * FF2]).then_inc(load_b[s], 16)
                    else:
                        dst = ring[:, s, :].rearrange("p (e f) -> p e f", e=4)
                        for j in range(4):
                            sp.dma_start(dst[:, j], a["w_exp_down_2"][0, i * 4 + j, (c - 16) * P:(c - 15) * P, :])\
                              .then_inc(load_b[s], 16)
            for j in range(2):
                evacuated(sp, f"oN{2 * j + 1}")
                sp.dma_start(out[0, j * P:(j + 1) * P, :], buf(6, D, j * D)).then_inc(out_done, 16)
            sp.wait_ge(out_done, 32)

        PIECES_A = [2 if c[0] == "shared_gu" else 1 for c in CHUNKS_A]
        TURN1_SUM = [2, 2, 2, 2, 2, 2]

        def arrived_a(eng, n):
            eng.wait_ge(load_a[n % RING], 16 * sum(PIECES_A[m] for m in range(n % RING, n + 1, RING)))

        def arrived_moe1(eng, i, c):
            s = (NA + c) % RING
            base = sum(PIECES_A[m] for m in range(s, NA, RING))
            eng.wait_ge(load_a[s], i * 32 + 16 * (base + 2))

        def arrived_b(eng, n):
            s = (NA + n) % RING
            eng.wait_ge(load_b[s], 16 * (n // RING + 1))

        def arrived_moe2(eng, i, c):
            s = (NA + NB + c) % RING
            base = len([m for m in range(NB) if (NA + m) % RING == s])
            pieces = [2] * 16 + [4] * 8
            mine = [m for m in range(24) if (NA + NB + m) % RING == s]
            eng.wait_ge(load_b[s], i * (16 * sum(pieces[m] for m in mine)) + 16 * (base + sum(pieces[m] for m in mine if m <= c)))

        @block.gpsimd
        def _(pool):
            pool.dma_start(cst[:, :], a["cst"]).then_inc(cst_in, 16)
            pool.dma_start(rbias[:, :], a["router_bias"][0:1, :].to_broadcast([P, E1])).then_inc(cst_in, 16)
            pool.dma_start(onehot[0:32, :], a["buckets"]).then_inc(cst_in, 16)
            pool.wait_ge(bias_staged, 2 * HEADS)
            pool.dma_start(bias_dram.rearrange("h p c -> p h c"), bias_st).then_inc(bias_out, 16)
            pool.wait_ge(bias_out, 16)
            skew = bass.AP(bias_dram.tensor, P - 1, [[PAD - 1, P], [P * PAD, HEADS], [1, T]])
            pool.dma_start(biasT, skew).then_inc(bias_in, 16)
            evacuated(pool, "av7")
            pool.wait_ge(at_exp, HEADS)
            pool.dma_start(wr1, a["w_router"][0].rearrange("(k p) e -> p k e", p=P)).then_inc(wr1_in, 16)
            evacuated(pool, "route1")
            pool.dma_start(rope, a["rope"]).then_inc(rope_in, 16)
            evacuated(pool, "conv3")
            pool.dma_start(wr2, a["w_router_2"][0].rearrange("(k p) e -> p k e", p=P)).then_inc(wr2_in, 16)

        @block.scalar
        def _(act):
            A = nc.scalar.activation

            def copy_out(name, dst, src=None):
                src = full(act, name) if src is None else src
                frees(A(dst, src, ACT.Copy), name)

            act.wait_ge(rows_zeroed, 1)
            for table, half in ((VEC, 0), (VEC2, 1)):
                for name, (r0, n) in table.items():
                    src = a[name]
                    if name == "rel_bias":
                        act.dma_start(vec_rows[r0:r0 + n, half, 0:32], src).then_inc(rows_in, 16)
                        continue
                    if name == "conv_w_2":
                        src = src[0].rearrange("w (k c) -> (w k) c", c=P)
                    elif len(src.shape) == 1:
                        src = src.rearrange("(k c) -> k c", c=P)
                    else:
                        src = src[0].rearrange("(k c) -> k c", c=P)
                    act.dma_start(vec_rows[r0:r0 + n, half, :], src).then_inc(rows_in, 16)

            evacuated(act, "vec")
            A(csil, vcols("c"), ACT.Silu).then_inc(csil_ready, 1)
            for dst, nm in ((memT, "memT"), (xT, "xT")):
                for j in range(4):
                    copy_out(f"{nm}{j}", dst[:, 2 * j:2 * j + 2, :], full(act, f"{nm}{j}").rearrange("p (k t) -> p k t", t=T))

            def rms_act(n):
                act.wait_ge(mean_ready, n + 1)
                A(rstd_of(n), rstd_of(n), ACT.Ln).then_inc(act_step, 1)
                act.wait_ge(act_step, n + 1)
                A(rstd_of(n), rstd_of(n), ACT.Exp, scale=-0.5).then_inc(rstd_ready, 1)

            rms_act(0)
            rms_act(1)

            def ada_copy(n):
                if n >= 2:
                    act.wait_ge(mod_full, n - 1)
                copy_out(f"ada{n}", ada_rows[n % 2])

            for n in range(ADA_FIRST):
                ada_copy(n)
            for g in range(4):
                for j in range(2):
                    nm = f"memkv{g}_{j}"
                    if g < 2:
                        copy_out(nm, memK[:, 4 * g + 2 * j:4 * g + 2 * j + 2, :], full(act, nm).rearrange("p (k t) -> p k t", t=T))
                    else:
                        copy_out(nm, memV[:, j, 512 * (g - 2):512 * (g - 1)])
            act.wait_ge(bias_staged, HEADS)
            for h in range(HEADS):
                ps = full(act, f"rel{h}")
                frees(A(bias_st[:, h, 0:T], ps[:, 0:T], ACT.Copy), f"rel{h}")
                evacuated(act, f"rel{h}")
                act.sem_inc(bias_staged, 1)
            for c in range(6):
                for j in range(2):
                    nm = f"in{c}_{j}"
                    if c in (0, 1, 3, 4):
                        m = 4 * (c - (c > 2)) + 2 * j
                        if m < 12:
                            act.wait_ge(bias_out, 16)
                        copy_out(nm, QK[:, m:m + 2, :], full(act, nm).rearrange("p (k t) -> p k t", t=T))
                    else:
                        copy_out(nm, V1[:, j, 512 * (c // 3):512 * (c // 3) + 512])
                for n in range(ADA_FIRST + 2 * c, min(ADA_FIRST + 2 * c + 2, ADA)):
                    ada_copy(n)
            for s in range(HEADS + 2):
                if s < HEADS:
                    ps = full(act, f"z{s}")
                    if s >= 1:
                        act.wait_ge(sb_rest, s)
                    A(sc_L, ps[:, 0:W3], ACT.Abs, scale=HD ** -0.5).then_inc(sb_abs, 1)
                    act.wait_ge(sb_abs, 3 * s + 1)
                    A(sc_L, sc_L, ACT.Exp, scale=-1.0).then_inc(sb_abs, 1)
                    act.wait_ge(sb_abs, 3 * s + 2)
                    act.wait_ge(cst_in, 48)
                    A(sc_L, sc_L, ACT.Ln, bias=ones[:, 0:1]).then_inc(sb_abs, 1)
                    act.wait_ge(at_max, s + 1)
                    A(sc_p[s % 2][:, 0:P], sc_p[s % 2][:, 0:P], ACT.Exp, bias=mx1[:, s % 2, 0:1],
                      accum_out=sm1[:, s % 2, 0:1])
                    A(sc_p[s % 2][:, P:W3], sc_p[s % 2][:, P:W3], ACT.Exp, bias=mx1[:, s % 2, 1:2],
                      accum_out=sm1[:, s % 2, 1:2]).then_inc(at_exp, 1)
                    nm = f"in{6 + s // 2}_{s % 2}"
                    copy_out(nm, G1[:, 2 * s:2 * s + 2, :], full(act, nm).rearrange("p (k t) -> p k t", t=T))
                if 1 <= s <= HEADS:
                    h = s - 1
                    act.wait_ge(sb_arg, s)
                    A(sc_a[h % 2], sc_a[h % 2], ACT.Exp).then_inc(sb_exp, 1)
                    copy_out(f"pT{h}", sc_pT[h % 2], full(act, f"pT{h}")[:, 0:W3])
                if s >= 2:
                    h = s - 2
                    r = 64 * (h % 2)
                    ps = full(act, f"av{h}")
                    frees(A(OT[r:r + 64, h // 2::4, :], ps[r:r + 64, :].rearrange("p (b t) -> p b t", b=2), ACT.Copy), f"av{h}")
            evacuated(act, "in9_1")
            for q in range(4):
                A(G1[:, 4 * q:4 * q + 4, :], G1[:, 4 * q:4 * q + 4, :], ACT.Exp, scale=-1.0).then_inc(gates_exp, 1)
            rms_act(2)
            for k in range(KT):
                if k == 0:
                    act.wait_ge(normed, 3)
                A(hT[:, k, :], hT[:, k, :], ACT.Identity, bias=mod[:, 24 + k:25 + k]).then_inc(act_func, 1)
            act.wait_ge(route_ready, 1)
            A(rt[:, 0:P], rt[:, 0:P], ACT.Exp, scale=-1.0).then_inc(act_func, 1)
            for j in range(4):
                nm = f"hN{j}"
                if j == 0:
                    evacuated(act, "out3")
                t, half = j // 2, j % 2
                dst = hN_hi[:, t, :].rearrange("p (k c) -> p c k", k=KT)[:, 64 * half:64 * half + 64, :]
                A(dst, full(act, nm).rearrange("p (c k) -> p c k", k=KT), ACT.Copy).then_inc(hn_high, 1)
            frees(A(shg_s, full(act, "shg").rearrange("p (k t) -> p k t", t=T), ACT.Silu), "shg")

            act.wait_ge(table_ready, 1)
            extra = act.value_load(tab_i[0:1, 32:33], min_val=0, max_val=EXTRA // 4)
            turns1 = act.snap(extra + TURNS1)
            with act.Fori(0, turns1) as i:
                for j in range(PAIRS_PER_TURN):
                    act.wait_ge(used_a, i * 6 + (NA + 3 * j + 2))
                    A(gu_s, psum[:, 5, :], ACT.Copy).then_inc(gu_copied, 1)
                    act.wait_ge(turned, i * 2 + (j + 1))
                    act.wait_ge(aT_ready, i * 2 + (j + 1))
                    A(sil1, psum[:, 6, 0:256], ACT.Silu).then_inc(sil_ready, 1)
                    act.wait_ge(pT_copied, i * 2 + (j + 1))
                    act.wait_ge(y0_done, i * 2 + (j + 1))
                    A(y_hi[:, 0:512], psum[:, 4, :], ACT.Copy, scale=wslot[:, j:j + 1]).then_inc(y_high0, 1)
                    act.wait_ge(used_a, i * 6 + (NA + 3 * j + 3))
                    A(y_hi[:, 512:D], psum[:, 7, :], ACT.Copy, scale=wslot[:, j:j + 1]).then_inc(y_high1, 1)

            rms_act(3)
            rms_act(4)
            for nm, dst in (("cq", low[:, 0:2, :]), ("ckv", low[:, 2:4, :])):
                copy_out(nm, dst, full(act, nm).rearrange("p (k t) -> p k t", t=T))
            for j in range(2):
                copy_out(f"xc{j}", xcT[:, 2 * j:2 * j + 2, :], full(act, f"xc{j}").rearrange("p (k t) -> p k t", t=T))
            act.wait_ge(q_scaled, 1)
            A(rstd_lo, rstd_lo, ACT.Ln).then_inc(act_func, 1)
            act.wait_ge(act_func, 10)
            A(rstd_lo, rstd_lo, ACT.Exp, scale=-0.5).then_inc(act_func, 1)
            for j in range(2, 4):
                copy_out(f"xc{j}", xcT[:, 2 * j:2 * j + 2, :], full(act, f"xc{j}").rearrange("p (k t) -> p k t", t=T))
            for j in range(4):
                if j == 0:
                    act.wait_ge(normed, 5)
                copy_out(f"qn{j}", qnT[:, 2 * j:2 * j + 2, :], full(act, f"qn{j}").rearrange("p (k t) -> p k t", t=T))
            for j in range(2):
                copy_out(f"qr{j}", low[:, 4 + 2 * j:6 + 2 * j, :], full(act, f"qr{j}").rearrange("p (k t) -> p k t", t=T))
            for j in range(4):
                copy_out(f"kn{j}", knT[:, 2 * j:2 * j + 2, :], full(act, f"kn{j}").rearrange("p (k t) -> p k t", t=T))
            for j in range(4):
                if j == 0:
                    act.wait_ge(q_scaled, 2)
                copy_out(f"v{j}", vN[:, j // 2, 512 * (j % 2):512 * (j % 2) + 512])
            for s in range(HEADS + 2):
                if s < HEADS:
                    act.wait_ge(at_max, HEADS + s + 1)
                    for t in range(TT):
                        ins = A(at_p[s % 2][:, t * T:(t + 1) * T], bank(f"ls{s}")[:, t * T:(t + 1) * T], ACT.Exp,
                                bias=mx2[:, s % 2, t:t + 1], scale=(MLA_NOPE + MLA_ROPE) ** -0.5,
                                accum_out=sm2[:, s % 2, t:t + 1])
                    frees(ins, f"ls{s}")

                def fill(n):
                    nm = f"fill{n}"
                    if n < 4:
                        copy_out(nm, gbT[:, 2 * n:2 * n + 2, :], full(act, nm).rearrange("p (k t) -> p k t", t=T))
                    elif n >= 8:
                        ps = full(act, nm)
                        for t in range(2):
                            m = 2 * (n - 8) + t
                            ins = A(gates[:, m, :], ps[:, t * T:(t + 1) * T], ACT.Exp, scale=-1.0,
                                    bias=small[:, 32 + m:33 + m])
                        frees(ins, nm)
                if s < HEADS:
                    fill(2 * s)
                if 1 <= s <= HEADS:
                    copy_out(f"lp{s - 1}", at_pT[(s - 1) % 2])
                if s < HEADS:
                    fill(2 * s + 1)
                if s >= 2:
                    copy_out(f"lo{s - 2}", oT[:, s - 2, :], full(act, f"lo{s - 2}")[:, 0:T])
            rms_act(5)
            for j in range(4):
                copy_out(f"mq{j}", mqT[:, 2 * j:2 * j + 2, :], full(act, f"mq{j}").rearrange("p (k t) -> p k t", t=T))
            for s in range(MEMH + 1):
                if s < MEMH:
                    act.wait_ge(at_max, 2 * HEADS + s + 1)
                    for t in range(TT):
                        ins = A(at_p[s % 2][:, t * T:(t + 1) * T], bank(f"mS{s}")[:, t * T:(t + 1) * T], ACT.Exp,
                                bias=mx2[:, s % 2, t:t + 1], scale=T ** -0.5, accum_out=sm2[:, s % 2, t:t + 1])
                    frees(ins, f"mS{s}")
                if s >= 1:
                    copy_out(f"mP{s - 1}", at_pT[(s - 1) % 2])
                    copy_out(f"mO{s - 1}", moT[:, 2 * s - 2:2 * s, :], full(act, f"mO{s - 1}").rearrange("p (k t) -> p k t", t=T))
            rms_act(6)
            act.wait_ge(at_max, 2 * HEADS + MEMH + 1)
            for t in range(TT):
                ins = A(rt2[:, t, :], bank("route2")[:, t * E2:(t + 1) * E2], ACT.Exp, bias=mx2[:, 0, t:t + 1],
                        accum_out=sm2[:, 0, t:t + 1])
            frees(ins, "route2")
            for j in range(4):
                nm = f"gN{j}"
                t, half = j // 2, j % 2
                dst = hN[:, t, :].rearrange("p (k c) -> p c k", k=KT)[:, 64 * half:64 * half + 64, :]
                frees(A(dst, full(act, nm).rearrange("p (c k) -> p c k", k=KT), ACT.Copy), nm)
            act.sem_inc(y20_copied, 1)
            with act.Fori(0, TURNS2) as i:
                for e in range(4):
                    act.wait_ge(used_b, i * 24 + (NB + 4 * e + 4))
                    A(gu_s, psum[:, 5 + 2 * (e % 2), :], ACT.Copy).then_inc(gu2_copied, 1)
                    act.wait_ge(turned2, i * 4 + (e + 1))
                    act.wait_ge(aT2_ready, i * 4 + (e + 1))
                    A(sil2.rearrange("p (f c) -> p f c", c=64),
                      psum[:, 6, :].rearrange("p (f c) -> p f c", c=P)[:, :, 0:64], ACT.Silu).then_inc(sil2_ready, 1)
                act.wait_ge(used_b, i * 24 + (NB + 24))
                act.wait_ge(scattered2, i + 1)
                A(y_s[:, 0:512], psum[:, 5, :], ACT.Copy).then_inc(y20_copied, 1)
            rms_act(7)

        @block.vector
        def _(dve):
            V = nc.vector
            steps = [0]

            def step(ins):
                ins.then_inc(dve_step, 1)
                steps[0] += 1
                return steps[0]

            def after_step(n=None):
                dve.wait_ge(dve_step, steps[0] if n is None else n)

            V.memset(vec_rows, 0.0).then_inc(rows_zeroed, 1)
            ps = full(dve, "vec")
            frees(V.tensor_copy(vec[:, :], ps[:, 0:256]), "vec")
            evacuated(dve, "vec")
            dve.wait_ge(csil_ready, 1)
            dve.wait_ge(cst_in, 48)
            for k in range(KT):
                ins = V.tensor_scalar(cs32[:, k, :], ones[:, 0:32], csil[:, k:k + 1], None, ALU.mult)
            ins.then_inc(cs32_ready, 1)
            for h in range(HEADS):
                ins = V.tensor_scalar(relb[0:32, h, :], ones[0:32, :], vcol("rel_bias", h)[0:32, :], None, ALU.mult)
            ins.then_inc(relb_ready, 1)
            for h in range(HEADS):
                V.memset(bias_st[:, h, T:PAD], NEG).then_inc(bias_staged, 1)
            step(V.tensor_scalar(small[:, 32:48], vcols("b_gate_2"), -1.0, None, ALU.mult))

            def squares(n, src, sqb):
                V.tensor_tensor(sqb[:, 0:4, :], src[:, 0:4, :], src[:, 0:4, :], ALU.mult).then_inc(squares_ready, 1)
                V.tensor_tensor(sqb[:, 4:8, :], src[:, 4:8, :], src[:, 4:8, :], ALU.mult).then_inc(squares_ready, 1)

            def mean(n):
                name = f"ms{n}"
                ps = full(dve, name)
                frees(V.tensor_scalar(rstd_of(n), ps[:, 0:T], 1.0 / D, EPS, ALU.mult, ALU.add), name)
                evacuated(dve, name)
                dve.sem_inc(mean_ready, 1)

            def scaled(n, dst, src, gain):
                dve.wait_ge(rstd_ready, n + 1)
                for k in range(KT):
                    ins = V.scalar_tensor_tensor(dst[:, k, :], src[:, k, :], gain(k), rstd_of(n), ALU.mult, ALU.mult)
                return ins

            for j in range(4):
                evacuated(dve, f"memT{j}")
            squares(0, memT, sq[0])
            for j in range(4):
                evacuated(dve, f"xT{j}")
            squares(1, xT, sq[1])
            mean(0)
            mean(1)
            scaled(0, memT, memT, lambda k: vcol("norm_memkv_g_2", k)).then_inc(normed, 1)
            NF = 4 * ADA_FIRST
            dve.wait_ge(mod_full, ADA_FIRST)
            V.tensor_tensor(mod[:, 0:NF], psum[:, 7, 0:NF], vcols("b_ada")[:, 0:NF], ALU.add).then_inc(mod_ready, 1)
            dve.wait_ge(mod_ready, 1)
            step(V.scalar_tensor_tensor(gs[:, 0:8], mod[:, 8:16], 1.0, vcols("norm1_g"), ALU.add, ALU.mult))
            after_step()
            evacuated(dve, "memkv3_1")
            step(scaled(1, hT, xT, lambda k: gs[:, k:k + 1]))
            after_step()
            for k in range(KT):
                ins = V.tensor_scalar(hT[:, k, :], hT[:, k, :], mod[:, k:k + 1], None, ALU.add)
            ins.then_inc(normed, 1)

            for s in range(HEADS + 2):
                if s < HEADS:
                    h = s
                    ps = full(dve, f"z{h}")
                    dve.wait_ge(sb_abs, 3 * h + 1)
                    step(V.tensor_scalar(sc_lb[h % 2], ps[:, 0:W3], HD ** -0.5, 0.0, ALU.mult, ALU.min))
                    z = ps
                    ps = full(dve, f"s{h}")
                    if h == 0:
                        dve.wait_ge(bias_in, 16)
                    if h >= 2:
                        full(dve, f"pT{h - 2}")
                    p = sc_p[h % 2]
                    V.scalar_tensor_tensor(p[:, 0:P], ps[:, 0:P], HD ** -0.5, biasT[:, h, P:T], ALU.mult, ALU.add)
                    frees(V.scalar_tensor_tensor(p[:, P:W3], ps[:, P:W3], HD ** -0.5, biasT[:, h, :], ALU.mult, ALU.add), f"s{h}")
                    evacuated(dve, f"s{h}")
                    V.tensor_reduce(mx1[:, h % 2, 0:1], p[:, 0:P], AX, ALU.max, negate=True)
                    V.tensor_reduce(mx1[:, h % 2, 1:2], p[:, P:W3], AX, ALU.max, negate=True).then_inc(at_max, 1)
                    after_step()
                    dve.wait_ge(sb_abs, 3 * h + 3)
                    step(V.tensor_tensor(sc_lb[h % 2], sc_lb[h % 2], sc_L, ALU.subtract))
                    after_step()
                    if h >= 1:
                        full(dve, f"skip{h - 1}")
                    frees(V.scalar_tensor_tensor(sc_lr, z[:, 0:W3], -(HD ** -0.5), sc_lb[h % 2], ALU.mult, ALU.add), f"z{h}")
                    evacuated(dve, f"z{h}")
                    V.tensor_tensor(sc_lr, sc_lr, mask3, ALU.mult).then_inc(sb_rest, 1)
                if 1 <= s <= HEADS:
                    h = s - 1
                    ps = full(dve, f"skip{h}")
                    if h >= 2:
                        full(dve, f"av{h - 2}")
                    frees(V.tensor_tensor(sc_a[h % 2], sc_lb[h % 2], ps[:, 0:W3], ALU.add), f"skip{h}")
                    evacuated(dve, f"skip{h}")
                    dve.sem_inc(sb_arg, 1)
                if s < HEADS:
                    h = s
                    dve.wait_ge(at_exp, h + 1)
                    step(V.reciprocal(sm1[:, h % 2, :], sm1[:, h % 2, :]))
                    after_step()
                    p = sc_p[h % 2]
                    V.tensor_scalar(p[:, 0:P], p[:, 0:P], sm1[:, h % 2, 0:1], None, ALU.mult)
                    V.tensor_scalar(p[:, P:W3], p[:, P:W3], sm1[:, h % 2, 1:2], None, ALU.mult).then_inc(at_p_ready, 1)
                if 1 <= s <= HEADS:
                    h = s - 1
                    dve.wait_ge(sb_exp, h + 1)
                    V.tensor_tensor(sc_a[h % 2], sc_a[h % 2], mask3, ALU.mult).then_inc(sb_a, 1)
            for q in range(4):
                dve.wait_ge(gates_exp, q + 1)
                g = G1[:, 4 * q:4 * q + 4, :]
                step(V.tensor_scalar(g, g, 1.0, None, ALU.add))
                after_step()
                step(V.reciprocal(g, g))
            after_step()
            dve.wait_ge(mod_full, ADA)
            step(V.tensor_tensor(mod[:, NF:48], psum[:, 7, NF:48], vcols("b_ada")[:, NF:48], ALU.add))
            after_step()
            step(V.scalar_tensor_tensor(gs[:, 8:16], mod[:, 32:40], 1.0, vcols("norm2_g"), ALU.add, ALU.mult))
            after_step()
            for j in range(4):
                ps = full(dve, f"brs_{j}").rearrange("p (k t) -> p k t", t=T)
                frees(V.tensor_tensor(merged[:, 2 * j:2 * j + 2, :], ps, G1[:, 2 * j:2 * j + 2, :], ALU.mult), f"brs_{j}")
                ps = full(dve, f"brm_{j}").rearrange("p (k t) -> p k t", t=T)
                frees(V.tensor_tensor(G1[:, 8 + 2 * j:10 + 2 * j, :], ps, G1[:, 8 + 2 * j:10 + 2 * j, :], ALU.mult), f"brm_{j}")
                evacuated(dve, f"brs_{j}")
                evacuated(dve, f"brm_{j}")
                V.tensor_tensor(merged[:, 2 * j:2 * j + 2, :], merged[:, 2 * j:2 * j + 2, :], G1[:, 8 + 2 * j:10 + 2 * j, :],
                                ALU.add).then_inc(merged_ready, 1)

            def residual(name, m0, gate):
                ps = full(dve, name)
                for t in range(2):
                    ins = V.scalar_tensor_tensor(xT[:, m0 + t, :], ps[:, t * T:(t + 1) * T], gate(m0 + t), xT[:, m0 + t, :],
                                                 ALU.mult, ALU.add)
                frees(ins, name)

            for j in range(4):
                residual(f"out{j}", 2 * j, lambda m: mod[:, 16 + m:17 + m])
            for j in range(4):
                evacuated(dve, f"out{j}")
            squares(2, xT, sq[1])
            mean(2)
            scaled(2, hT, xT, lambda k: gs[:, 8 + k:9 + k]).then_inc(normed, 1)

            def rows_low(j):
                t, half = j // 2, j % 2
                v = lambda ap: ap[:, t, :].rearrange("p (k c) -> p c k", k=KT)[:, 64 * half:64 * half + 64, :]
                ps = full(dve, f"hN{j}")
                dve.wait_ge(hn_high, j + 1)
                frees(V.tensor_tensor(v(hN_lo), ps.rearrange("p (c k) -> p c k", k=KT), v(hN_hi32), ALU.subtract), f"hN{j}")

            lg = rt[:, 0:P]
            sc = rt[:, P:2 * P]
            ch = rt[:, 2 * P:3 * P]
            gsc = rt[:, 3 * P:3 * P + 16]
            gtop = rt[:, 400:416]
            gm = rt[:, 416:432]
            mch = rt[:, 512:640]
            rep = rt[:, 640:768]
            top = rt[:, 768:784]
            sel = rt[:, 896:1024]
            wts = rt[:, 1024:1152]
            rk = rt[:, 1152:1280]
            t8 = rt[:, 1280:1408]
            den = rt[:, 1408:1412]
            ps = full(dve, "route1")
            frees(V.tensor_copy(lg, ps[:, 0:P]), "route1")
            evacuated(dve, "route1")
            dve.sem_inc(route_ready, 1)
            dve.wait_ge(act_func, 9)
            step(V.tensor_scalar(lg, lg, 1.0, None, ALU.add))
            after_step()
            step(V.reciprocal(sc, lg))
            after_step()
            for t in range(TT):
                step(V.tensor_tensor(ch[:, t * E1:(t + 1) * E1], sc[:, t * E1:(t + 1) * E1], rbias[:, :], ALU.add))
            after_step()
            for g in range(TT * GROUPS):
                step(V.max(t8[:, 8 * g:8 * g + 8], ch[:, 8 * g:8 * g + 8]))
            after_step()
            tv = t8.rearrange("p (g i) -> p g i", i=8)
            step(V.tensor_tensor(gsc.rearrange("p (g i) -> p g i", i=1), tv[:, :, 0:1], tv[:, :, 1:2], ALU.add))
            after_step()
            for t in range(TT):
                step(V.max(gtop[:, 8 * t:8 * t + 8], gsc[:, 8 * t:8 * t + 8]))
            after_step()
            for t in range(TT):
                step(V.memset(gtop[:, 8 * t + 4:8 * t + 8], 3e38))
            after_step()
            for t in range(TT):
                step(V.match_replace(gm[:, 8 * t:8 * t + 8], gtop[:, 8 * t:8 * t + 8], gsc[:, 8 * t:8 * t + 8], -3e38))
            after_step()
            step(V.tensor_scalar(gm, gm, -3e38, None, ALU.is_equal))
            after_step()
            step(V.tensor_scalar(gsc, gm, -1.0, 1e30, ALU.add, ALU.mult))
            after_step()
            grouped = lambda ap: ap.rearrange("p (g i) -> p g i", i=8)
            spread = lambda ap: ap.unsqueeze(2).to_broadcast([P, 16, 8])
            step(V.tensor_tensor(grouped(mch), grouped(ch), spread(gm), ALU.mult))
            after_step()
            step(V.tensor_tensor(grouped(mch), grouped(mch), spread(gsc), ALU.add))
            after_step()
            for t in range(TT):
                step(V.max(top[:, 8 * t:8 * t + 8], mch[:, t * E1:(t + 1) * E1]))
            after_step()
            for t in range(TT):
                step(V.match_replace(rep[:, t * E1:(t + 1) * E1], top[:, 8 * t:8 * t + 8], mch[:, t * E1:(t + 1) * E1], -3e38))
            after_step()
            V.tensor_scalar(sel, rep, -3e38, None, ALU.is_equal).then_inc(route_ready, 1)
            dve.wait_ge(route_ready, 2)
            for t in range(TT):
                e = slice(t * E1, (t + 1) * E1)
                step(V.tensor_tensor(wts[:, e], sc[:, e], sel[:, e], ALU.mult))
            after_step()
            step(V.tensor_reduce(den[:, 0:2], wts.rearrange("p (t e) -> p t e", t=TT), AX, ALU.add))
            after_step()
            step(V.reciprocal(den[:, 2:4], den[:, 0:2]))
            after_step()
            for t in range(TT):
                e = slice(t * E1, (t + 1) * E1)
                step(V.tensor_scalar(wts[:, e], wts[:, e], den[:, 2 + t:3 + t], 2.5, ALU.mult, ALU.mult))
            for j in range(4):
                rows_low(j)
            ps = full(dve, "rank1")
            frees(V.scalar_tensor_tensor(rk, ps[:, 0:P], FAR, sel, ALU.add, ALU.mult), "rank1")
            evacuated(dve, "rank1")
            after_step()
            dve.sem_inc(route_ready, 1)
            for t in range(TT):
                step(V.tensor_scalar(items[:, 0, t, 0:E1], rk[:, t * E1:(t + 1) * E1], -FAR, None, ALU.add))
                step(V.tensor_copy(items[:, 1, t, 0:E1], wts[:, t * E1:(t + 1) * E1]))
            step(V.memset(items[:, 0, :, E1 + EXTRA:ITEMS], -FAR))
            step(V.memset(items[:, 1, :, E1 + EXTRA:ITEMS], 0.0))
            cnt, ex, tmp = (rt[0:64, 1416 + i:1417 + i] for i in range(3))
            st, en = (rt[0:64, 1420 + i:1421 + i] for i in range(2))
            OH, CH, ge = (rt[0:64, 1440 + 32 * i:1472 + 32 * i] for i in range(3))
            ps = full(dve, "count1")
            frees(V.tensor_copy(cnt, ps[0:64, 0:1]), "count1")
            evacuated(dve, "count1")
            step(V.tensor_scalar(ex, cnt, float(SLOTS1), None, ALU.is_gt))
            after_step()
            for j in range(2, T // SLOTS1):
                step(V.tensor_scalar(tmp, cnt, float(SLOTS1 * j), None, ALU.is_gt))
                after_step()
                step(V.tensor_tensor(ex, ex, tmp, ALU.add))
                after_step()
            dve.sem_inc(route_ready, 1)
            ps = full(dve, "start1")
            frees(V.tensor_copy(st, ps[0:64, 0:1]), "start1")
            evacuated(dve, "start1")
            step(V.tensor_tensor(en, st, ex, ALU.add))
            after_step()
            step(V.tensor_scalar(ge, iota[0:64, 0:32], en, None, ALU.is_ge))
            step(V.tensor_scalar(OH, iota[0:64, 0:32], st, None, ALU.is_ge))
            after_step()
            step(V.tensor_tensor(OH, OH, ge, ALU.subtract))
            step(V.tensor_scalar(CH, iota[0:64, 0:32], st, 1.0, ALU.subtract, ALU.add))
            after_step()
            step(V.scalar_tensor_tensor(CH, CH, -float(SLOTS1), OH, ALU.mult, ALU.mult))
            after_step()
            ps = full(dve, "tabT")
            rT = buf(8, 512, 512)
            frees(V.tensor_copy(rT[0:64, :], ps[0:64, :]), "tabT")
            evacuated(dve, "tabT")
            dve.sem_inc(route_ready, 1)
            ps = full(dve, "item")
            iv = ps[:, 0:128].rearrange("p (w t s) -> p w t s", w=2, t=TT)
            step(V.tensor_scalar(items[:, 0, :, E1:E1 + EXTRA], iv[:, 0], -FAR, None, ALU.add))
            frees(V.tensor_copy(items[:, 1, :, E1:E1 + EXTRA], iv[:, 1]), "item")
            after_step()
            evacuated(dve, "item")
            ps = full(dve, "eidx")
            frow = rt[0:1, 1600:1664]
            step(V.memset(frow, 0.0))
            after_step()
            step(V.tensor_copy(frow[:, 0:32], ps[0:1, 0:32]))
            frees(V.tensor_copy(rt[0:1, 1670:1671], ps[0:1, 32:33]), "eidx")
            evacuated(dve, "eidx")
            i4 = iota[0:1, 0:32].rearrange("p (a b) -> p a b", b=4)[:, :, 0:1]
            step(V.tensor_scalar(rt[0:1, 1680:1688].rearrange("p (a b) -> p a b", b=1), i4, rt[0:1, 1670:1671], None, ALU.is_lt))
            after_step()
            step(V.tensor_reduce(frow[:, 32:33], rt[0:1, 1680:1688], AX, ALU.add))
            after_step()
            V.tensor_copy(tab_i[:, :], frow).then_inc(table_ready, 1)
            ps = full(dve, "shu").rearrange("p (k t) -> p k t", t=T)
            evacuated(dve, "shg")
            frees(V.tensor_tensor(sha, shg_s, ps, ALU.mult), "shu")

            dve.wait_ge(table_ready, 1)
            extra = dve.value_load(tab_i[0:1, 32:33], min_val=0, max_val=EXTRA // 4)
            turns1 = dve.snap(extra + TURNS1)

            def onehots(col0):
                for t in range(TT):
                    for j in range(4):
                        r = items[:, 0, t, bass.ds(col0 + j, 1)]
                        w = items[:, 1, t, bass.ds(col0 + j, 1)]
                        c = slice(SLOTS1 * j, SLOTS1 * (j + 1))
                        V.tensor_scalar(Pg1[:, t, c], iota[:, 0:SLOTS1], r, None, ALU.is_equal)
                        ins = V.tensor_scalar(Pw1[:, t, c], iota[:, 0:SLOTS1], r, w, ALU.is_equal, ALU.mult)
                ins.then_inc(p_ready, 1)

            def gather_copy(quarter, count):
                dve.wait_ge(gathered, count)
                V.tensor_copy(xg1[:, 2 * quarter:2 * quarter + 2, :],
                              psum[:, 4 + 3 * (quarter % 2), :].rearrange("p (k c) -> p k c", k=2)).then_inc(g_copied, 1)

            def transposed_copy(pair, count):
                dve.wait_ge(pT_done, count)
                V.tensor_copy(wslot[:, pair:pair + 1], psum[:, 6, T:T + 1])
                V.tensor_copy(PT1[pair], psum[:, 6, 0:T]).then_inc(pT_copied, 1)

            V.memset(buf_r(6).bitcast(F32), 0.0)
            dve.sem_inc(aT_ready, 1)
            onehots(0)
            V.memset(PT1[1].bitcast(F32), 0.0).then_inc(y_copied, 1)
            for q in range(4):
                gather_copy(q, q + 1)
            transposed_copy(0, 1)
            with dve.Fori(0, turns1) as i:
                for j in range(PAIRS_PER_TURN):
                    if j == 1:
                        gather_copy(0, i * 4 + 5)
                        gather_copy(1, i * 4 + 6)
                    dve.wait_ge(sil_ready, i * 2 + (j + 1))
                    V.tensor_tensor(aT1, sil1, psum[:, 6, 256:512], ALU.mult).then_inc(aT_ready, 1)
                    if j == 1:
                        gather_copy(2, i * 4 + 7)
                        gather_copy(3, i * 4 + 8)
                    dve.wait_ge(y_high0, i * 2 + (j + 1))
                    V.scalar_tensor_tensor(y_lo[:, 0:512], psum[:, 4, :], wslot[:, j:j + 1], y_hi32[:, 0:512], ALU.mult, ALU.subtract)
                    transposed_copy((j + 1) % 2, i * 2 + (j + 2))
                    dve.wait_ge(y_high1, i * 2 + (j + 1))
                    V.scalar_tensor_tensor(y_lo[:, 512:D], psum[:, 7, :], wslot[:, j:j + 1], y_hi32[:, 512:D], ALU.mult, ALU.subtract)\
                     .then_inc(y_copied, 1)
                    if j == 0:
                        onehots(i * 4 + 4)
            dve.wait_ge(scattered, turns1 * 2 + 1)

            def add_accumulated(gate):
                for m in range(KT):
                    ps = psum[:, m // 2, (m % 2) * T:(m % 2) * T + T]
                    if gate is None:
                        ins = V.tensor_tensor(xT[:, m, :], ps, xT[:, m, :], ALU.add)
                    else:
                        ins = V.scalar_tensor_tensor(xT[:, m, :], ps, gate(m), xT[:, m, :], ALU.mult, ALU.add)
                ins.then_inc(acc_read, 1)

            add_accumulated(lambda m: mod[:, 40 + m:41 + m])
            dve.wait_ge(acc_read, 1)
            squares(3, xT, sq[1])
            mean(3)
            x_out = scaled(3, xT, xT, lambda k: vcol("final_g", k))
            x_out.then_inc(normed, 1)
            dve.wait_ge(normed, 4)
            squares(4, xT, sq[1])
            mean(4)
            scaled(4, hT, xT, lambda k: vcol("norm_mix_g_2", k)).then_inc(normed, 1)

            evacuated(dve, "cq")
            evacuated(dve, "ckv")
            dve.wait_ge(normed, 5)
            V.tensor_tensor(lsq, low[:, 0:3, :], low[:, 0:3, :], ALU.mult).then_inc(squares_ready, 1)
            ps = full(dve, "msq")
            step(V.tensor_scalar(rstd_lo[:, 0:T], ps[:, 0:T], 1.0 / QL, EPS, ALU.mult, ALU.add))
            frees(V.tensor_scalar(rstd_lo[:, T:2 * T], ps[:, T:2 * T], 1.0 / KVL, EPS, ALU.mult, ALU.add), "msq")
            after_step()
            evacuated(dve, "msq")
            dve.sem_inc(q_scaled, 1)
            dve.wait_ge(act_func, 11)
            for k in range(2):
                V.scalar_tensor_tensor(low[:, k, :], low[:, k, :], vcol("q_norm_g_2", k), rstd_lo[:, 0:T], ALU.mult, ALU.mult)
            V.scalar_tensor_tensor(low[:, 2, :], low[:, 2, :], vcol("kv_norm_g_2", 0), rstd_lo[:, T:2 * T],
                                   ALU.mult, ALU.mult).then_inc(q_scaled, 1)
            dve.wait_ge(rope_in, 16)
            cosT, sinT = rope[:, R_COS:R_COS + T], rope[:, R_SIN:R_SIN + T]
            for j in range(3):
                ps = full(dve, f"rot{j}")
                ms = (4 + 2 * j, 5 + 2 * j) if j < 2 else (3,)
                for n, m in enumerate(ms):
                    step(V.tensor_tensor(low[:, m, :], low[:, m, :], cosT, ALU.mult))
                    ins = V.tensor_tensor(spare[:, n * T:(n + 1) * T], ps[:, n * T:(n + 1) * T], sinT, ALU.mult)
                frees(ins, f"rot{j}")
                after_step()
                evacuated(dve, f"rot{j}")
                for n, m in enumerate(ms):
                    ins = V.tensor_tensor(low[:, m, :], low[:, m, :], spare[:, n * T:(n + 1) * T], ALU.add)
                ins.then_inc(rope_done, 1)
                dve.wait_ge(rope_done, j + 1)

            def softmax_max(name, h, scale):
                ps = full(dve, name)
                step(V.tensor_reduce(mx2[:, h % 2, :], ps.rearrange("p (t k) -> p t k", t=TT), AX, ALU.max, negate=True))
                after_step()
                V.tensor_scalar(mx2[:, h % 2, :], mx2[:, h % 2, :], scale, None, ALU.mult).then_inc(at_max, 1)

            def softmax_norm(name, h):
                evacuated(dve, name)
                step(V.reciprocal(sm2[:, h % 2, :], sm2[:, h % 2, :]))
                after_step()
                p = at_p[h % 2]
                V.tensor_scalar(p[:, 0:T], p[:, 0:T], sm2[:, h % 2, 0:1], None, ALU.mult)
                V.tensor_scalar(p[:, T:2 * T], p[:, T:2 * T], sm2[:, h % 2, 1:2], None, ALU.mult).then_inc(at_p_ready, 1)

            def conv_tile(k):
                y, v = low[:, k % 2, :], xcT[:, k, :]
                step(V.tensor_scalar(y, v, vcol("conv_w_2", 8 + k), vcol("conv_b_2", k), ALU.mult, ALU.add))
                after_step()
                step(V.scalar_tensor_tensor(y[:, 1:T], v[:, 0:T - 1], vcol("conv_w_2", k), y[:, 1:T], ALU.mult, ALU.add))
                after_step()
                step(V.scalar_tensor_tensor(y[:, 0:T - 1], v[:, 1:T], vcol("conv_w_2", 16 + k), y[:, 0:T - 1], ALU.mult, ALU.add))
                after_step()
                V.tensor_tensor(gbT[:, k, :], y, gbT[:, k, :], ALU.mult).then_inc(conv_ready, 1)

            for s in range(HEADS):
                softmax_max(f"ls{s}", s, (MLA_NOPE + MLA_ROPE) ** -0.5)
                softmax_norm(f"ls{s}", s)
                for n in (2 * s, 2 * s + 1):
                    if 4 <= n < 8:
                        m = 2 * (n - 4)
                        ps = full(dve, f"fill{n}").rearrange("p (k t) -> p k t", t=T)
                        frees(V.tensor_tensor(xcT[:, m:m + 2, :], ps, xcT[:, m:m + 2, :], ALU.mult), f"fill{n}")
                        evacuated(dve, f"fill{n}")
                        evacuated(dve, f"fill{n - 4}")
                        conv_tile(m)
                        conv_tile(m + 1)
            for q in range(4):
                for n in range(2 * q, 2 * q + 2):
                    evacuated(dve, f"fill{8 + n}")
                g = gates[:, 4 * q:4 * q + 4, :]
                step(V.tensor_scalar(g, g, 1.0, None, ALU.add))
                after_step()
                step(V.reciprocal(g, g))
            after_step()
            for j in range(4):
                ps = full(dve, f"conv{j}").rearrange("p (k t) -> p k t", t=T)
                frees(V.tensor_tensor(yn[:, 2 * j:2 * j + 2, :], ps, gates[:, 2 * j:2 * j + 2, :], ALU.mult), f"conv{j}")
            for j in range(4):
                ps = full(dve, f"mla{j}").rearrange("p (k t) -> p k t", t=T)
                g = gates[:, 8 + 2 * j:10 + 2 * j, :]
                frees(V.tensor_tensor(g, ps, g, ALU.mult), f"mla{j}")
                evacuated(dve, f"mla{j}")
                evacuated(dve, f"conv{j}")
                V.tensor_tensor(yn[:, 2 * j:2 * j + 2, :], yn[:, 2 * j:2 * j + 2, :], g, ALU.add).then_inc(merged_ready, 1)

            def plain_residual(name, m0):
                ps = full(dve, name).rearrange("p (k t) -> p k t", t=T)
                frees(V.tensor_tensor(xT[:, m0:m0 + 2, :], ps, xT[:, m0:m0 + 2, :], ALU.add), name)

            for j in range(4):
                plain_residual(f"mix{j}", 2 * j)
            for j in range(4):
                evacuated(dve, f"mix{j}")
            squares(5, xT, sq[1])
            mean(5)
            scaled(5, hT, xT, lambda k: vcol("norm_mem_g_2", k)).then_inc(normed, 1)
            for s in range(MEMH):
                softmax_max(f"mS{s}", s, T ** -0.5)
                softmax_norm(f"mS{s}", s)
            for j in range(4):
                plain_residual(f"mo{j}", 2 * j)
            for j in range(4):
                evacuated(dve, f"mo{j}")
            squares(6, xT, sq[1])
            mean(6)
            scaled(6, hT, xT, lambda k: vcol("norm_moe_g_2", k)).then_inc(normed, 1)
            ps = full(dve, "route2")
            V.tensor_reduce(mx2[:, 0, :], ps[:, 0:TT * E2].rearrange("p (t e) -> p t e", t=TT), AX, ALU.max,
                            negate=True).then_inc(at_max, 1)
            evacuated(dve, "route2")
            step(V.reciprocal(sm2[:, 0, :], sm2[:, 0, :]))
            after_step()
            for t in range(TT):
                ins = V.tensor_scalar(rt2[:, t, :], rt2[:, t, :], sm2[:, 0, t:t + 1], None, ALU.mult)
            ins.then_inc(route_ready, 1)
            dve.wait_ge(route_ready, 6)
            ps = full(dve, "affT")
            aff = [rt[0:E2, 256:512], rt[0:E2, 512:768]]
            t8b = rt[0:E2, 768:776]
            frees(V.tensor_copy(aff[0], ps[0:E2, 0:T]), "affT")
            evacuated(dve, "affT")
            for r in range(CAP2 // 8):
                step(V.max(t8b, aff[r % 2]))
                after_step()
                step(V.match_replace(aff[(r + 1) % 2], t8b, aff[r % 2], -1.0))
                after_step()
            V.tensor_scalar(aff[1], aff[0], 0.0, None, ALU.is_lt).then_inc(route_ready, 1)
            ps = full(dve, "selT")
            frees(V.tensor_copy(sel2, ps[:, 0:TT * E2]), "selT")
            evacuated(dve, "selT")
            dve.sem_inc(route_ready, 1)
            step(V.tensor_tensor(items[:, 1, :, 0:E2], rt2, sel2.rearrange("p (t e) -> p t e", t=TT), ALU.mult))
            ps = full(dve, "rank2")
            frees(V.scalar_tensor_tensor(rk[:, 0:TT * E2], ps[:, 0:TT * E2], FAR, sel2, ALU.add, ALU.mult), "rank2")
            evacuated(dve, "rank2")
            after_step()
            step(V.tensor_scalar(items[:, 0, :, 0:E2], rk[:, 0:TT * E2].rearrange("p (t e) -> p t e", t=TT), -FAR, None, ALU.add))
            after_step()
            V.memset(zeros, 0.0).then_inc(route_ready, 1)
            for ahead in (g2_copied, aT2_ready, y21_copied):
                dve.sem_inc(ahead, 1)
            with dve.Fori(0, TURNS2) as i:
                dve.wait_ge(pwT2_done, i + 1)
                for t in range(TT):
                    for j in range(4):
                        r = items[:, 0, t, bass.ds(i * 4 + j, 1)]
                        w = items[:, 1, t, bass.ds(i * 4 + j, 1)]
                        c = slice(CAP2 * j, CAP2 * (j + 1))
                        V.tensor_scalar(Pg[:, t, c], iota[:, 0:CAP2], r, None, ALU.is_equal)
                        ins = V.tensor_scalar(Pw[:, t, c], iota[:, 0:CAP2], r, w, ALU.is_equal, ALU.mult)
                ins.then_inc(p2_ready, 1)
                for half in range(2):
                    dve.wait_ge(gathered2, i * 2 + (half + 1))
                    V.tensor_copy(xg[:, 4 * half:4 * half + 4, :], psum[:, 4, :].rearrange("p (k c) -> p k c", k=4))\
                     .then_inc(g2_copied, 1)
                dve.wait_ge(pwT2_done, i + 2)
                V.tensor_copy(PwT, psum[:, 6, 0:T]).then_inc(pwT2_copied, 1)
                for e in range(4):
                    dve.wait_ge(sil2_ready, i * 4 + (e + 1))
                    V.tensor_tensor(aT2[e].rearrange("p (h f) c -> p f h c", h=2),
                                    sil2.rearrange("p (f h c) -> p f h c", f=4, h=2),
                                    psum[:, 6, :].rearrange("p (f g h c) -> p f g h c", f=4, g=2, h=2)[:, :, 1], ALU.mult)\
                     .then_inc(aT2_ready, 1)
                dve.wait_ge(used_b, i * 24 + (NB + 24))
                dve.wait_ge(scattered2, i + 1)
                V.tensor_copy(y_s[:, 512:D], psum[:, 7, :]).then_inc(y21_copied, 1)
            dve.wait_ge(scattered2, TURNS2 + 1)
            add_accumulated(None)
            dve.wait_ge(acc_read, 2)
            squares(7, xT, sq[1])
            mean(7)
            scaled(7, hT, xT, lambda k: vcol("norm_final_g_2", k)).then_inc(normed, 1)
            oN = buf(6).rearrange("p (t f) -> p t f", t=TT)
            for j in range(4):
                ps = full(dve, f"oN{j}")
                frees(V.tensor_copy(oN[:, j // 2, 512 * (j % 2):512 * (j % 2) + 512], ps), f"oN{j}")

        @block.tensor
        def _(pe):
            mm = nc.tensor.matmul
            turn = nc.tensor.transpose
            opened = []

            def start(name):
                opened.append(name)
                b, use = AT[name]
                if use:
                    pe.wait_ge(bank_free[b], use)
                return bank(name)

            def done(ins, name):
                ins.then_inc(bank_full[AT[name][0]], 1)

            def project(name, w, src, m, uses=None):
                ps = start(name)
                nk = w.shape[1]
                for t in range(2):
                    for k in range(nk):
                        ins = mm(ps[:, t * T:(t + 1) * T], w[:, k, (m + t) * P:(m + t + 1) * P], src[:, k, :],
                                 start=(k == 0), stop=(k == nk - 1))
                done(ins, name)

            def project_rows(name, w, src, t, cols=512):
                ps = start(name)
                nk = w.shape[1]
                for k in range(nk):
                    ins = mm(ps[:, 0:cols], src[:, k, t * P:(t + 1) * P], w[:, k, 0:cols], start=(k == 0), stop=(k == nk - 1))
                done(ins, name)

            def mean_square(n, sqb):
                ps = start(f"ms{n}")
                base = 2 * n + (n > 4)
                for k in range(KT):
                    if k % 4 == 0:
                        pe.wait_ge(squares_ready, base + k // 4 + 1)
                    ins = mm(ps[:, 0:T], ones, sqb[:, k, :], start=(k == 0), stop=(k == KT - 1))
                done(ins, f"ms{n}")

            def chunk_a(n, cols):
                arrived_a(pe, n)
                k = CHUNKS_A[n][3]
                return slot_a(n)[:, 0:k * cols].rearrange("p (k c) -> p k c", k=k)

            def chunk_b(n, cols):
                arrived_b(pe, n)
                k = CHUNKS_B[n][3]
                return slot_b(n)[:, 0:k * cols].rearrange("p (k c) -> p k c", k=k)

            def used(sem_):
                pe.sem_inc(sem_, 1)

            pe.wait_ge(cst_in, 48)
            pe.wait_ge(rows_in, 16 * (len(VEC) + len(VEC2)))
            pe.wait_ge(rows_zeroed, 1)
            ps = start("vec")
            for h in range(2):
                ins = turn(ps[:, h * P:(h + 1) * P], vec_rows[:, h, :], ident)
            done(ins, "vec")
            for src, arrival, nm in ((memN, mem_in, "memT"), (xN, x_in, "xT")):
                pe.wait_ge(arrival, 16)
                for j in range(4):
                    ps = start(f"{nm}{j}")
                    for k in range(2):
                        for t in range(TT):
                            ins = turn(ps[:, k * T + t * P:k * T + (t + 1) * P], src[:, t, (2 * j + k) * P:(2 * j + k + 1) * P], ident)
                    done(ins, f"{nm}{j}")
            mean_square(0, sq[0])
            mean_square(1, sq[1])
            pe.wait_ge(cs32_ready, 1)
            sel_col = cst[:, C_SEL:C_SEL + 1]

            def columns(n):
                evacuated(pe, f"ada{n}")
                for b in range(4):
                    m = 4 * n + b
                    ins = mm(psum[:, 7, m:m + 1], ada_rows[n % 2][:, b * P:(b + 1) * P], sel_col, start=True, stop=True)
                ins.then_inc(mod_full, 1)

            def modulation(n, place):
                w = chunk_a(place, 512)
                ps = start(f"ada{n}")
                for k in range(2):
                    for q in range(4):
                        ins = mm(ps[32 * q:32 * q + 32, :], cs32[:, 2 * q + k, :], w[:, 2 * q + k, :],
                                 start=(k == 0), stop=(k == 1))
                done(ins, f"ada{n}")
                full(pe, f"ada{n}")
                used(used_a)
                if n == ADA_FIRST:
                    pe.wait_ge(mod_ready, 1)
                elif n >= 1:
                    columns(n - 1)

            for n in range(ADA_FIRST):
                modulation(n, n)
            for g in range(4):
                w = chunk_a(ADA_FIRST + g, 512)
                if g == 0:
                    pe.wait_ge(normed, 1)
                for j in range(2):
                    if g < 2:
                        project(f"memkv{g}_{j}", w, memT, 2 * j)
                    else:
                        project_rows(f"memkv{g}_{j}", w, memT, j)
                    if g == 0 and j == 0:
                        columns(ADA_FIRST - 1)
                full(pe, f"memkv{g}_1")
                used(used_a)
            pe.wait_ge(relb_ready, 1)
            for h in range(HEADS):
                ps = start(f"rel{h}")
                done(mm(ps[:, 0:T], relb[0:32, h, :], onehot[0:32, :], start=True, stop=True), f"rel{h}")

            n0 = IN_A[9] - 9
            pe.wait_ge(normed, 2)
            for c in range(6):
                w = chunk_a(IN_A[c], 512)
                for j in range(2):
                    if c in (2, 5):
                        project_rows(f"in{c}_{j}", w, hT, j)
                    else:
                        project(f"in{c}_{j}", w, hT, 2 * j)
                full(pe, f"in{c}_1")
                used(used_a)
                for i, n in enumerate(range(ADA_FIRST + 2 * c, min(ADA_FIRST + 2 * c + 2, ADA))):
                    modulation(n, IN_A[c] + 1 + i)
            columns(ADA - 1)
            for j in range(2):
                for c in range(6):
                    evacuated(pe, f"in{c}_{j}")
            for s in range(HEADS + 2):
                if s < HEADS:
                    h, r = s, 64 * (s % 2)
                    ps = start(f"z{h}")
                    q, k = QK[r:r + 64, h // 2, :], QK[r:r + 64, 4 + h // 2, :]
                    mm(ps[:, 0:T], k[:, 0:P], q, start=True, stop=True)
                    done(mm(ps[:, T:T + P], k[:, P:T], q[:, P:T], start=True, stop=True), f"z{h}")
                    ps = start(f"s{h}")
                    q, k = QK[r:r + 64, 8 + h // 2, :], QK[r:r + 64, 12 + h // 2, :]
                    mm(ps[:, 0:P], q[:, 0:P], k[:, 0:P], start=True, stop=True)
                    done(mm(ps[:, P:W3], q[:, P:T], k, start=True, stop=True), f"s{h}")
                    c = 6 + s // 2
                    if s % 2 == 0:
                        w_g = chunk_a(IN_A[c], 512)
                    project(f"in{c}_{s % 2}", w_g, hT, 2 * (s % 2))
                    if s % 2:
                        full(pe, f"in{c}_1")
                        used(used_a)
                if 1 <= s <= HEADS:
                    h = s - 1
                    pe.wait_ge(sb_rest, h + 1)
                    ps = start(f"skip{h}")
                    mm(ps[:, 0:T], after, sc_lr[:, 0:T], start=True, stop=False, skip_group_check=True)
                    mm(ps[:, P:T], ones, sc_lr[:, T:W3], start=False, stop=False, skip_group_check=True)
                    done(mm(ps[:, T:W3], after, sc_lr[:, T:W3], start=False, stop=True, skip_group_check=True), f"skip{h}")
                    pe.wait_ge(at_p_ready, h + 1)
                    ps = start(f"pT{h}")
                    p = sc_p[h % 2]
                    turn(ps[:, 0:P], p[:, 0:P], ident)
                    turn(ps[:, P:T], p[:, P:T], ident)
                    done(turn(ps[:, T:W3], p[:, T:W3], ident), f"pT{h}")
                if s >= 2:
                    h, r = s - 2, 64 * (s % 2)
                    ps = start(f"av{h}")
                    pe.wait_ge(sb_a, h + 1)
                    evacuated(pe, f"pT{h}")
                    for b, pr in ((0, sc_a[h % 2]), (1, sc_pT[h % 2])):
                        o = b * T
                        v = V1[:, :, b * 512 + h * HD:b * 512 + (h + 1) * HD]
                        mm(ps[r:r + 64, o:o + T], v[:, 0, :], pr[:, 0:T], start=True, stop=False, skip_group_check=True)
                        ins = mm(ps[r:r + 64, o + P:o + T], v[:, 1, :], pr[:, T:W3], start=False, stop=True, skip_group_check=True)
                    done(ins, f"av{h}")
            evacuated(pe, "av6")
            evacuated(pe, "av7")
            ws = chunk_a(n0 + 10, 1024)
            wm = chunk_a(n0 + 11, 1024)
            for j in range(4):
                project(f"brs_{j}", ws, OT[:, 0:4, :], 2 * j)
                project(f"brm_{j}", wm, OT[:, 4:8, :], 2 * j)
            full(pe, "brm_3")
            used(used_a)
            used(used_a)
            for j in range(4):
                if j % 2 == 0:
                    w = chunk_a(n0 + 12 + j // 2, 512)
                if j == 0:
                    pe.wait_ge(merged_ready, 4)
                project(f"out{j}", w, merged, 2 * (j % 2))
                if j % 2:
                    full(pe, f"out{j}")
                    used(used_a)
            mean_square(2, sq[1])
            pe.wait_ge(wr1_in, 16)
            pe.wait_ge(act_func, KT)
            ps = start("route1")
            for t in range(TT):
                for k in range(KT):
                    ins = mm(ps[:, t * E1:(t + 1) * E1], hT[:, k, t * P:(t + 1) * P], wr1[:, k, :], start=(k == 0), stop=(k == KT - 1))
            done(ins, "route1")

            def rows_of_h(prefix):
                for j in range(4):
                    ps = start(f"{prefix}{j}")
                    t, half = j // 2, j % 2
                    for k in range(4):
                        ins = turn(ps[:, k * P:(k + 1) * P], hT[:, 4 * half + k, t * P:(t + 1) * P], ident)
                    done(ins, f"{prefix}{j}")

            rows_of_h("hN")
            arrived_a(pe, n0 + 14)
            w = slot_a(n0 + 14).rearrange("p (g k f) -> p g k f", g=2, k=KT)
            project("shg", w[:, 0], hT, 0)
            project("shu", w[:, 1], hT, 0)
            full(pe, "shu")
            used(used_a)
            pe.wait_ge(route_ready, 2)
            sel = rt[:, 896:1024]
            ps = start("rank1")
            mm(ps[:, 0:E1], before, sel[:, 0:E1], start=True, stop=True)
            mm(ps[:, E1:2 * E1], ones, sel[:, 0:E1], start=True, stop=False)
            done(mm(ps[:, E1:2 * E1], before, sel[:, E1:2 * E1], start=False, stop=True), "rank1")
            ps = start("count1")
            mm(ps[0:64, 0:1], sel[:, 0:E1], ones[:, 0:1], start=True, stop=False)
            done(mm(ps[0:64, 0:1], sel[:, E1:2 * E1], ones[:, 0:1], start=False, stop=True), "count1")
            pe.wait_ge(route_ready, 4)
            ps = start("start1")
            done(mm(ps[0:64, 0:1], before[0:64, 0:64], rt[0:64, 1417:1418], start=True, stop=True), "start1")
            ps = start("tabT")
            rk, wts = rt[:, 1152:1280], rt[:, 1024:1152]
            for i, src in enumerate((rk, wts)):
                for t in range(TT):
                    ins = turn(ps[0:64, i * T + t * P:i * T + (t + 1) * P], src[:, t * E1:(t + 1) * E1], ident)
            done(ins, "tabT")
            pe.wait_ge(route_ready, 5)
            rT = buf(8, 512, 512)
            OH, CH = rt[0:64, 1440:1472], rt[0:64, 1472:1504]
            ps = start("item")
            for t in range(TT):
                mm(ps[:, t * 32:(t + 1) * 32], rT[0:64, t * P:(t + 1) * P], OH, start=True, stop=False)
                mm(ps[:, t * 32:(t + 1) * 32], ones[0:64, :], CH, start=False, stop=True)
            for t in range(TT):
                ins = mm(ps[:, 64 + t * 32:64 + (t + 1) * 32], rT[0:64, T + t * P:T + (t + 1) * P], OH, start=True, stop=True)
            done(ins, "item")
            ps = start("eidx")
            mm(ps[0:1, 0:32], cst[0:64, C_PIDX:C_PIDX + 1], OH, start=True, stop=True)
            done(mm(ps[0:1, 32:33], rt[0:64, 1417:1418], ones[0:64, 0:1], start=True, stop=True), "eidx")

            wd = chunk_a(n0 + 15, 1024)
            for nm in last_uses(opened):
                evacuated(pe, nm)
            acc = lambda m: psum[:, m // 2, (m % 2) * T:(m % 2) * T + T]
            for m in range(KT):
                for k in range(2):
                    ins = mm(acc(m), wd[:, k, m * P:(m + 1) * P], sha[:, k, :], start=(k == 0 and m % 2 == 0), stop=False,
                             skip_group_check=True)
            ins.then_inc(acc_ready, 1)
            pe.wait_ge(acc_ready, 1)
            used(used_a)

            for nm in ("hN0", "hN1", "hN2", "hN3"):
                evacuated(pe, nm)
            pe.wait_ge(table_ready, 1)
            extra = pe.value_load(tab_i[0:1, 32:33], min_val=0, max_val=EXTRA // 4)
            turns1 = pe.snap(extra + TURNS1)

            def scatter1(pair, m0, m1):
                for m in range(m0, m1):
                    for y in (y_hi, y_lo):
                        ins = mm(acc(m), y[:, m * P:(m + 1) * P], PT1[pair], start=False, stop=False, skip_group_check=True)
                return ins

            def gather1(quarter):
                for k in range(2):
                    for t in range(TT):
                        for h in (hN_hi, hN_lo):
                            kk = 2 * quarter + k
                            ins = mm(psum[:, 4 + 3 * (quarter % 2), k * T:(k + 1) * T], h[:, t, kk * P:(kk + 1) * P], Pg1[:, t, :],
                                     start=(t == 0 and h is hN_hi), stop=(t == TT - 1 and h is hN_lo))
                ins.then_inc(gathered, 1)

            def onehot_turn(pair):
                for t in range(TT):
                    turn(psum[:, 6, t * P:(t + 1) * P], Pg1_32[:, t, pair * P:(pair + 1) * P], ident)
                for t in range(TT):
                    ins = mm(psum[:, 6, T:T + 1], Pw1[:, t, pair * P:(pair + 1) * P], ones[:, 0:1], start=(t == 0), stop=(t == TT - 1))
                ins.then_inc(pT_done, 1)

            pe.wait_ge(p_ready, 1)
            gather1(0)
            gather1(1)
            for q in (2, 3):
                pe.wait_ge(g_copied, q - 1)
                gather1(q)
            onehot_turn(0)
            with pe.Fori(0, turns1) as i:
                for j in range(PAIRS_PER_TURN):
                    c = 3 * j
                    arrived_moe1(pe, i, c)
                    arrived_moe1(pe, i, c + 1)
                    pe.wait_ge(g_copied, i * 4 + 4)
                    ws = [ring[:, (NA + c + e) % RING, :].rearrange("p (g k f) -> p g k f", g=2, k=KT) for e in range(2)]
                    for k in range(KT):
                        for e in range(2):
                            ins = mm(psum[64 * e:64 * e + 64, 5, :], xg1[:, k, P * j + 64 * e:P * j + 64 * e + 64], ws[e][:, :, k, :],
                                     start=(k == 0), stop=(k == KT - 1))
                    ins.then_inc(used_a, 2)
                    pe.wait_ge(y_copied, i * 2 + (j + 1))
                    if j == 0:
                        scatter1(1, 0, 4)
                    else:
                        pe.wait_ge(p_ready, i + 2)
                        gather1(0)
                    pe.wait_ge(gu_copied, i * 2 + (j + 1))
                    pe.wait_ge(pT_copied, i * 2 + (j + 1))
                    for b in range(4):
                        src = gu_s[:, 256 * (b // 2) + b % 2:256 * (b // 2) + 256:2]
                        ins = turn(psum[:, 6, b * P:(b + 1) * P], src, ident)
                    ins.then_inc(turned, 1)
                    if j == 0:
                        scatter1(1, 4, 8).then_inc(scattered, 1)
                    else:
                        gather1(1)
                        pe.wait_ge(g_copied, i * 4 + 5)
                        gather1(2)
                        scatter1(0, 0, 8).then_inc(scattered, 1)
                        pe.wait_ge(g_copied, i * 4 + 6)
                        gather1(3)
                    pe.wait_ge(aT_ready, i * 2 + (j + 2))
                    arrived_moe1(pe, i, c + 2)
                    wd = ring[:, (NA + c + 2) % RING, :].rearrange("p (e k f) -> p e k f", e=2, k=2)
                    for half in range(2):
                        if j == 1:
                            pe.wait_ge(g_copied, i * 4 + (7 + half))
                        b = 4 + 3 * half
                        for k in range(2):
                            for e in range(2):
                                ins = mm(psum[64 * e:64 * e + 64, b, :], aT1[:, k * P + 64 * e:k * P + 64 * e + 64],
                                         wd[:, e, k, half * 512:(half + 1) * 512], start=(k == 0), stop=(k == 1))
                        ins.then_inc(used_a if half else y0_done, 1)
                    onehot_turn((j + 1) % 2)
            pe.wait_ge(y_copied, turns1 * 2 + 1)
            scatter1(1, 0, 8).then_inc(scattered, 1)

            pe.wait_ge(acc_read, 1)
            mean_square(3, sq[1])
            mean_square(4, sq[1])
            pe.wait_ge(normed, 5)
            w = chunk_b(0, 448)
            project("cq", w, hT, 0)
            ps = start("ckv")
            for k in range(KT):
                mm(ps[:, 0:T], w[:, k, QL:QL + KVL], hT[:, k, :], start=(k == 0), stop=(k == KT - 1))
            for k in range(KT):
                for r in (0, 64):
                    ins = mm(ps[r:r + 64, T:2 * T], w[:, k, QL + KVL:448], hT[:, k, :], start=(k == 0), stop=(k == KT - 1))
            done(ins, "ckv")
            full(pe, "ckv")
            used(used_b)
            for c in range(2):
                w = chunk_b(1 + c, 512)
                for j in range(2):
                    project(f"xc{2 * c + j}", w, hT, 2 * j)
                full(pe, f"xc{2 * c + 1}")
                used(used_b)
                if c == 0:
                    pe.wait_ge(squares_ready, 11)
                    ps = start("msq")
                    for k in range(2):
                        mm(ps[:, 0:T], ones, lsq[:, k, :], start=(k == 0), stop=(k == 1))
                    done(mm(ps[:, T:2 * T], ones, lsq[:, 2, :], start=True, stop=True), "msq")
            pe.wait_ge(q_scaled, 2)
            w = chunk_b(3, 1536)
            HQ = MLA_NOPE + MLA_ROPE
            for j in range(4):
                ps = start(f"qn{j}")
                for t in range(2):
                    for k in range(2):
                        c0 = (2 * j + t) * HQ
                        ins = mm(ps[:, t * T:(t + 1) * T], w[:, k, c0:c0 + MLA_NOPE], low[:, k, :], start=(k == 0), stop=(k == 1))
                done(ins, f"qn{j}")
            for j in range(2):
                ps = start(f"qr{j}")
                for t in range(2):
                    for k in range(2):
                        for r in range(2):
                            c0 = (4 * j + 2 * t + r) * HQ + MLA_NOPE
                            ins = mm(ps[64 * r:64 * r + 64, t * T:(t + 1) * T], w[:, k, c0:c0 + MLA_ROPE], low[:, k, :],
                                     start=(k == 0), stop=(k == 1))
                done(ins, f"qr{j}")
            full(pe, "qr1")
            used(used_b)
            w = chunk_b(4, 2048)
            HK = MLA_NOPE + MLA_V
            for j in range(4):
                ps = start(f"kn{j}")
                for t in range(2):
                    c0 = (2 * j + t) * HK
                    ins = mm(ps[:, t * T:(t + 1) * T], w[:, 0, c0:c0 + MLA_NOPE], low[:, 2, :], start=True, stop=True)
                done(ins, f"kn{j}")
            wv = w[:, 0, :].rearrange("p (h c) -> p h c", c=HK)
            for j in range(4):
                ps = start(f"v{j}")
                done(mm(ps, low[:, 2, (j // 2) * P:(j // 2 + 1) * P], wv[:, 4 * (j % 2):4 * (j % 2) + 4, MLA_NOPE:HK],
                        start=True, stop=True), f"v{j}")
            full(pe, "v3")
            used(used_b)
            pe.wait_ge(rope_in, 16)
            perm = rope[:, R_PERM:R_PERM + P]
            for j in range(3):
                ps = start(f"rot{j}")
                if j < 2:
                    evacuated(pe, f"qr{j}")
                for n, m in enumerate((4 + 2 * j, 5 + 2 * j) if j < 2 else (3,)):
                    ins = mm(ps[:, n * T:(n + 1) * T], perm, low[:, m, :], start=True, stop=True)
                done(ins, f"rot{j}")
            pe.wait_ge(rope_done, 3)
            for j in range(4):
                evacuated(pe, f"qn{j}")
                evacuated(pe, f"kn{j}")
                evacuated(pe, f"v{j}")

            def fill(n):
                nonlocal w_f
                if n % 2 == 0:
                    w_f = chunk_b(5 + n // 2, 512)
                project(f"fill{n}", w_f, hT2, 2 * (n % 2))
                if n % 2:
                    full(pe, f"fill{n}")
                    used(used_b)

            w_f = None
            hT2 = hT
            for s in range(HEADS + 2):
                if s < HEADS:
                    ps = start(f"ls{s}")
                    r = 64 * (s % 2)
                    for t in range(TT):
                        mm(ps[:, t * T:(t + 1) * T], qnT[:, s, t * P:(t + 1) * P], knT[:, s, :], start=True, stop=False)
                        ins = mm(ps[:, t * T:(t + 1) * T], low[r:r + 64, 4 + s // 2, t * P:(t + 1) * P], low[r:r + 64, 3, :],
                                 start=False, stop=True)
                    done(ins, f"ls{s}")
                    fill(2 * s)
                if 1 <= s <= HEADS:
                    h = s - 1
                    pe.wait_ge(at_p_ready, HEADS + h + 1)
                    ps = start(f"lp{h}")
                    for k in range(TT):
                        for t in range(TT):
                            ins = turn(ps[:, k * T + t * P:k * T + (t + 1) * P], at_p[h % 2][:, t * T + k * P:t * T + (k + 1) * P], ident)
                    done(ins, f"lp{h}")
                if s < HEADS:
                    fill(2 * s + 1)
                if s >= 2:
                    h = s - 2
                    ps = start(f"lo{h}")
                    evacuated(pe, f"lp{h}")
                    for k in range(TT):
                        ins = mm(ps[:, 0:T], vN[:, k, h * MLA_V:(h + 1) * MLA_V], at_pT[h % 2][:, k * T:(k + 1) * T],
                                 start=(k == 0), stop=(k == TT - 1))
                    done(ins, f"lo{h}")
            pe.wait_ge(conv_ready, KT)
            n = 13
            for nm, src in (("conv", gbT), ("mla", oT), ("mix", yn)):
                if nm == "mla":
                    for h in range(HEADS):
                        evacuated(pe, f"lo{h}")
                if nm == "mix":
                    pe.wait_ge(merged_ready, 8)
                for j in range(4):
                    if j % 2 == 0:
                        w = chunk_b(n, 512)
                        n += 1
                    project(f"{nm}{j}", w, src, 2 * (j % 2))
                    if j % 2:
                        full(pe, f"{nm}{j}")
                        used(used_b)
            mean_square(5, sq[1])
            pe.wait_ge(normed, 6)
            for j in range(4):
                if j % 2 == 0:
                    w = chunk_b(n, 512)
                    n += 1
                project(f"mq{j}", w, hT, 2 * (j % 2))
                if j % 2:
                    full(pe, f"mq{j}")
                    used(used_b)
            for j in range(4):
                evacuated(pe, f"mq{j}")
            for s in range(MEMH + 1):
                if s < MEMH:
                    ps = start(f"mS{s}")
                    for t in range(TT):
                        for k in range(2):
                            ins = mm(ps[:, t * T:(t + 1) * T], mqT[:, 2 * s + k, t * P:(t + 1) * P], memK[:, 2 * s + k, :],
                                     start=(k == 0), stop=(k == 1))
                    done(ins, f"mS{s}")
                if s >= 1:
                    h = s - 1
                    pe.wait_ge(at_p_ready, 2 * HEADS + h + 1)
                    ps = start(f"mP{h}")
                    for k in range(TT):
                        for t in range(TT):
                            ins = turn(ps[:, k * T + t * P:k * T + (t + 1) * P], at_p[h % 2][:, t * T + k * P:t * T + (k + 1) * P], ident)
                    done(ins, f"mP{h}")
                    ps = start(f"mO{h}")
                    evacuated(pe, f"mP{h}")
                    for m in range(2):
                        for k in range(TT):
                            ins = mm(ps[:, m * T:(m + 1) * T], memV[:, k, (2 * h + m) * P:(2 * h + m + 1) * P],
                                     at_pT[h % 2][:, k * T:(k + 1) * T], start=(k == 0), stop=(k == TT - 1))
                    done(ins, f"mO{h}")
            for h in range(MEMH):
                evacuated(pe, f"mO{h}")
            for j in range(4):
                if j % 2 == 0:
                    w = chunk_b(n, 512)
                    n += 1
                project(f"mo{j}", w, moT, 2 * (j % 2))
                if j % 2:
                    full(pe, f"mo{j}")
                    used(used_b)
            assert n == NB
            mean_square(6, sq[1])
            pe.wait_ge(wr2_in, 16)
            pe.wait_ge(normed, 7)
            ps = start("route2")
            for t in range(TT):
                for k in range(KT):
                    ins = mm(ps[:, t * E2:(t + 1) * E2], hT[:, k, t * P:(t + 1) * P], wr2[:, k, :], start=(k == 0), stop=(k == KT - 1))
            done(ins, "route2")
            rows_of_h("gN")
            pe.wait_ge(route_ready, 6)
            ps = start("affT")
            for t in range(TT):
                ins = turn(ps[0:E2, t * P:(t + 1) * P], rt2[:, t, :], ident)
            done(ins, "affT")
            pe.wait_ge(route_ready, 7)
            ps = start("selT")
            for t in range(TT):
                ins = turn(ps[:, t * E2:(t + 1) * E2], rt[0:E2, 512 + t * P:512 + (t + 1) * P], ident[0:E2, 0:E2])
            done(ins, "selT")
            pe.wait_ge(route_ready, 8)
            ps = start("rank2")
            mm(ps[:, 0:E2], before, sel2[:, 0:E2], start=True, stop=True)
            mm(ps[:, E2:2 * E2], ones, sel2[:, 0:E2], start=True, stop=False)
            done(mm(ps[:, E2:2 * E2], before, sel2[:, E2:2 * E2], start=False, stop=True), "rank2")
            for nm in last_uses(opened):
                evacuated(pe, nm)
            for nm in ("gN0", "gN1", "gN2", "gN3"):
                evacuated(pe, nm)
            pe.wait_ge(route_ready, 9)

            def gather(half, done_sem):
                for k in range(4):
                    for t in range(TT):
                        kk = 4 * half + k
                        ins = mm(psum[:, 4, k * P:(k + 1) * P], hN[:, t, kk * P:(kk + 1) * P], Pg[:, t, :],
                                 start=(t == 0), stop=(t == TT - 1))
                ins.then_inc(done_sem, 1)

            def weights_turn(done_sem):
                for t in range(TT):
                    ins = turn(psum[:, 6, t * P:(t + 1) * P], Pw[:, t, :], ident)
                ins.then_inc(done_sem, 1)

            def scatter(m0, wT):
                for m in range(m0, m0 + 4):
                    ins = mm(acc(m), y_s[:, m * P:(m + 1) * P], wT, start=False, stop=False, skip_group_check=True)
                return ins

            pe.sem_inc(pwT2_done, 1)
            pe.sem_inc(scattered2, 1)
            for m in range(0, KT, 2):
                mm(psum[:, m // 2, :], zeros, cst[:, 0:512], start=True, stop=False, skip_group_check=True)
            with pe.Fori(0, TURNS2) as i:
                pe.wait_ge(p2_ready, i + 1)
                pe.wait_ge(g2_copied, i * 2 + 1)
                gather(0, gathered2)
                pe.wait_ge(g2_copied, i * 2 + 2)
                gather(1, gathered2)
                weights_turn(pwT2_done)
                pe.wait_ge(g2_copied, i * 2 + 3)
                for e in range(4):
                    b = 5 + 2 * (e % 2)
                    if e == 0:
                        pe.wait_ge(y20_copied, i + 1)
                    if e == 1:
                        pe.wait_ge(y21_copied, i + 1)
                    for c in range(4 * e, 4 * e + 4):
                        arrived_moe2(pe, i, c)
                        w = ring[:, (NA + NB + c) % RING, :].rearrange("p (g k f) -> p g k f", g=2, k=2)
                        for k in range(2):
                            for q in range(4):
                                kk = 2 * (c % 4) + k
                                ins = mm(psum[32 * q:32 * q + 32, b, :], xg[:, kk, CAP2 * e:CAP2 * (e + 1)],
                                         w[:, q // 2, k, (q % 2) * 512:(q % 2 + 1) * 512], start=(kk == 0), stop=(kk == KT - 1))
                        ins.then_inc(used_b, 1)
                    pe.wait_ge(gu2_copied, i * 4 + (e + 1))
                    if e == 0:
                        pe.wait_ge(pwT2_copied, i + 1)
                    else:
                        pe.wait_ge(aT2_ready, i * 4 + (e + 1))
                    for f in range(4):
                        ins = turn(psum[:, 6, f * P:(f + 1) * P], gu_s[:, f * P:(f + 1) * P], ident)
                    ins.then_inc(turned2, 1)
                pe.wait_ge(aT2_ready, i * 4 + 5)
                for c in range(16, 24):
                    arrived_moe2(pe, i, c)
                    w = ring[:, (NA + NB + c) % RING, :].rearrange("p (e f) -> p e f", e=4)
                    k = c - 16
                    for half in range(2):
                        for e in range(4):
                            ins = mm(psum[32 * e:32 * e + 32, 5 + 2 * half, :], aT2[e][:, k, :],
                                     w[:, e, half * 512:(half + 1) * 512], start=(k == 0), stop=(k == KT - 1))
                    ins.then_inc(used_b, 1)
                pe.wait_ge(y20_copied, i + 2)
                scatter(0, PwT)
                pe.wait_ge(y21_copied, i + 2)
                scatter(4, PwT).then_inc(scattered2, 1)
            pe.wait_ge(acc_read, 2)
            mean_square(7, sq[1])
            pe.wait_ge(normed, 8)
            for j in range(4):
                ps = start(f"oN{j}")
                t, half = j // 2, j % 2
                for k in range(4):
                    ins = turn(ps[:, k * P:(k + 1) * P], hT[:, 4 * half + k, t * P:(t + 1) * P], ident)
                done(ins, f"oN{j}")
            assert opened == JOBS + JOBS2, [x for x in zip(opened, JOBS + JOBS2) if x[0] != x[1]][:3]


_OUTS = [((1, T, D), "float32")]


def kernel(**inputs):
    import numpy as _np
    import concourse.bacc as _bacc
    from concourse import mybir as _mybir
    from concourse.bass_utils import run_bass_kernel_spmd as _run

    nc = _bacc.Bacc("TRN2", target_bir_lowering=False, num_devices=1)
    arrays, aps = {}, {}
    for name, value in {**inputs, **shape_tables()}.items():
        x = _np.ascontiguousarray(value)
        arrays[f"in_{name}_dram"] = x
        aps[name] = nc.dram_tensor(f"in_{name}_dram", x.shape, _mybir.dt.from_np(x.dtype), kind="ExternalInput").ap()
    out = nc.dram_tensor("out_0_dram", _OUTS[0][0], _mybir.dt.from_np(_np.dtype(_OUTS[0][1])), kind="ExternalOutput").ap()
    build(nc, aps, out)
    r = _run(nc, [arrays], core_ids=[0])
    return r.results[0]["out_0_dram"]
```

```python
import math
from contextlib import ExitStack

import numpy as np
import concourse.bass as bass
from concourse import mybir

F32 = mybir.dt.float32
F32R = mybir.dt.float32r
I32 = mybir.dt.int32
ALU = mybir.AluOpType
ACT = mybir.ActivationFunctionType
AX = mybir.AxisListType.X

P = 128
D = 1024
KT = D // P
T = 256
TT = T // P
EPS = 1e-6
NEG = -1e30
HEADS = 8
HD = 64
E1, FF1, SLOTS1 = 64, 256, 64
GROUPS, TOPK = 8, 8
PAIRS_PER_TURN = 2
TURNS1 = E1 // (2 * PAIRS_PER_TURN)
EXTRA = T * TOPK // SLOTS1
ITEMS = E1 + EXTRA + 4
FAR = 1.0e6
E2, FF2, CAP2 = 16, 1024, 32
TURNS2 = E2 // 4
MLA_NOPE, MLA_ROPE, MLA_V = 128, 64, 128
QL, KVL = 256, 128
MEMH = 4
RING, SLOT = 6, 4096
BANKS = 7
PAD = 383

VEC = {}
for _name, _rows in (("c", 8), ("b_ada", 48), ("norm1_g", 8), ("norm2_g", 8), ("final_g", 8), ("norm_mix_g_2", 8),
                     ("norm_mem_g_2", 8), ("norm_memkv_g_2", 8), ("norm_moe_g_2", 8), ("norm_final_g_2", 8)):
    VEC[_name] = (sum(n for _, n in VEC.values()), _rows)
VEC2 = {}
for _name, _rows in (("b_gate_2", 16), ("conv_w_2", 24), ("conv_b_2", 8), ("q_norm_g_2", 2), ("kv_norm_g_2", 1),
                     ("rel_bias", 8)):
    VEC2[_name] = (sum(n for _, n in VEC2.values()), _rows)

C_ID, C_BEFORE, C_ONES, C_BEFORE2, C_AFTER, C_IOTA, C_SEL, C_PIDX, C_SUM1, C_SUM2 = 0, 128, 256, 384, 512, 640, 768, 769, 770, 834
C_WIDTH = 850
R_COS, R_SIN, R_PERM, R_WIDTH = 0, 256, 512, 640


def shape_tables():
    r = np.arange(P)
    cst = np.zeros((P, C_WIDTH), np.float32)
    cst[:, C_ID:C_ID + P] = np.eye(P)
    before = (r[:, None] < r[None, :]).astype(np.float32)
    cst[:, C_BEFORE:C_BEFORE + P] = before
    cst[:, C_ONES:C_ONES + P] = 1.0
    cst[:, C_BEFORE2:C_BEFORE2 + P] = before
    cst[:, C_AFTER:C_AFTER + P] = before.T
    cst[:, C_IOTA:C_IOTA + P] = r[None, :]
    cst[::32, C_SEL] = 1.0
    cst[:, C_PIDX] = r
    cst[r, C_SUM1 + r % E1] = 1.0
    cst[r[r % 32 < E2], C_SUM2 + r[r % 32 < E2] % 32] = 1.0
    half = MLA_ROPE // 2
    inv = (1.0 / (10000.0 ** (np.arange(0, MLA_ROPE, 2, dtype=np.float32) / np.float32(MLA_ROPE)))).astype(np.float32)
    ang = np.arange(T, dtype=np.float32)[None, :] * inv[:, None]
    rope = np.zeros((P, R_WIDTH), np.float32)
    for b in range(0, P, MLA_ROPE):
        rope[b:b + half, R_COS:R_COS + T] = np.cos(ang)
        rope[b + half:b + MLA_ROPE, R_COS:R_COS + T] = np.cos(ang)
        rope[b:b + half, R_SIN:R_SIN + T] = -np.sin(ang)
        rope[b + half:b + MLA_ROPE, R_SIN:R_SIN + T] = np.sin(ang)
        for i in range(MLA_ROPE):
            rope[b + i, R_PERM + b + (i + half) % MLA_ROPE] = 1.0
    n = np.arange(T - 1, -1, -1)
    nf = np.maximum(n, 1).astype(np.float32)
    large = 16 + (np.log(nf / np.float32(16)) / np.float32(math.log(8.0)) * np.float32(16)).astype(np.int32)
    bucket = np.where(n < 16, n, np.minimum(large, 31))
    onehot = (np.arange(32)[:, None] == bucket[None, :]).astype(np.float32)
    return {"cst": cst, "rope": rope, "buckets": onehot}


ADA_FIRST, ADA = 4, 12
IN_A = {}
START = "aakaakkk"
CHUNKS_A = [("w_ada" if _x == "a" else "w_mem_kv_2", 512 * START[:_i].count(_x), 512, 8) for _i, _x in enumerate(START)]
for _c in range(10):
    IN_A[_c] = len(CHUNKS_A)
    CHUNKS_A += [("w_in", 512 * _c, 512, 8)]
    CHUNKS_A += [("w_ada", 512 * _j, 512, 8) for _j in range(ADA_FIRST + _c, min(ADA_FIRST + _c + 1, ADA))]
CHUNKS_A += [("w_branch_sb", 0, 1024, 4), ("w_branch_mb", 0, 1024, 4), ("w_out", 0, 512, 8), ("w_out", 512, 512, 8),
             ("shared_gu", 0, 0, 0), ("w_down_sh", 0, 1024, 2)]
CHUNKS_B = [("w_in_2", 3072, 512, 8), ("w_in_2", 0, 512, 8), ("w_in_2", 512, 512, 8), ("w_uq_2", 0, 1536, 2), ("w_ukv_2", 0, 2048, 1)]
CHUNKS_B += [("w_in_2", _c, 512, 8) for _c in (1024, 1536, 2048, 2560, 3520, 4032, 4544, 5056)]
CHUNKS_B += [(_w, _c, 512, 8) for _w in ("w_conv_out_2", "w_mla_out_2", "w_mix_out_2", "w_mem_q_2", "w_mem_out_2")
             for _c in (0, 512)]
WHOLE = ("w_ada", "shared_gu", "w_down_sh", "w_uq_2", "w_ukv_2")


def slots_of(chunks, base):
    at, m = [], base
    for c in chunks:
        at.append(m)
        m += 1 if c[0] in WHOLE else 2
    return at, m


SLOT_A, NA = slots_of(CHUNKS_A, 0)
SLOT_B, NAB = slots_of(CHUNKS_B, NA)
NB = NAB - NA
SPLIT = [("a", n) for n, c in enumerate(CHUNKS_A) if c[0] not in WHOLE] + \
        [("b", n) for n, c in enumerate(CHUNKS_B) if c[0] not in WHOLE]
SPLIT_AT = {x: k for k, x in enumerate(SPLIT)}

JOBS = ["vec"] + [f"memT{j}" for j in range(4)] + [f"xT{j}" for j in range(4)] + ["ms0", "ms1"]
for _i, _x in enumerate(START):
    _n = START[:_i].count(_x)
    JOBS += [f"ada{_n}"] if _x == "a" else [f"memkv{_n}_{_j}" for _j in range(2)] + [f"rel{2 * _n + _j}" for _j in range(2)]
for _c in range(6):
    JOBS += [f"in{_c}_{_j}" for _j in range(2)] + [f"ada{_j}" for _j in range(ADA_FIRST + _c, min(ADA_FIRST + _c + 1, ADA))]
for _s in range(HEADS + 2):
    if _s < HEADS:
        JOBS += [f"z{_s}", f"s{_s}", f"in{6 + _s // 2}_{_s % 2}"] + ([f"ada{ADA_FIRST + 6 + _s // 2}"] if _s in (1, 3) else [])
    if 1 <= _s <= HEADS:
        JOBS += [f"skip{_s - 1}", f"pT{_s - 1}"]
    if _s >= 2:
        JOBS += [f"av{_s - 2}"]
JOBS += [f"br{_b}_{_j}" for _j in range(4) for _b in ("s", "m")] + [f"again{j}" for j in range(4)] + ["out0", "out1", "out2", "ms2", "out3", "logit1"]
JOBS += ["hN0", "route1", "hN1", "hN2", "hN3", "shg", "shu", "rank1", "count1", "start1", "tabT", "item", "eidx"]
JOBS += ["ms3", "ms4", "cq", "ckv"] + [f"xc{j}" for j in range(2)] + ["msq"] + [f"xc{j}" for j in range(2, 4)]
JOBS += [f"qn{j}" for j in range(4)] + [f"qr{j}" for j in range(2)] + [f"kn{j}" for j in range(4)] + \
        [f"v{j}" for j in range(4)] + [f"rot{j}" for j in range(3)]
for _s in range(HEADS + 2):
    if _s < HEADS:
        JOBS += [f"ls{_s}", f"fill{2 * _s}"]
    if 1 <= _s <= HEADS:
        JOBS += [f"lp{_s - 1}"]
    if _s < HEADS:
        JOBS += [f"fill{2 * _s + 1}"]
    if _s >= 2:
        JOBS += [f"lo{_s - 2}"]
JOBS += [f"conv{j}" for j in range(4)] + [f"mla{j}" for j in range(4)] + ["mix0", "mix1", "mix2", "ms5", "mix3"]
JOBS += [f"mq{j}" for j in range(4)]
JOBS += ["mS0", "mS1"]
for _s in range(MEMH):
    JOBS += [f"mP{_s}"] + ([f"mS{_s + 2}"] if _s + 2 < MEMH else []) + [f"mO{_s}"]
JOBS += ["mo0", "mo1", "mo2", "ms6", "mo3", "logit2", "gN0", "route2", "gN1", "gN2", "gN3"]
JOBS += ["affT", "selT", "rank2"]
JOBS2 = ["ms7", "oN0", "rstdT", "oN1", "oN2", "oN3"]
AT, _next = {}, 0
for _name in JOBS + JOBS2:
    while _name in ("ms3", "ms7") and _next % BANKS <= 3:
        _next += 1
    AT[_name] = (_next % BANKS, sum(b == _next % BANKS for b, _ in AT.values()))
    _next += 1
assert len(AT) == len(JOBS) + len(JOBS2)


def last_uses(names):
    return list({AT[n][0]: n for n in names}.values())


def build(nc, a, out):
    ctx = ExitStack()
    with ctx:
        def sb(name, shape, dt=F32):
            return ctx.enter_context(nc.sbuf_tensor(name, shape, dt))

        def sem(name):
            return ctx.enter_context(nc.semaphore(name))

        ring_place = nc.sbuf_base
        sb("ring_place", [P, RING * SLOT + 8])
        ring_place += -ring_place % 32
        ring = nc.alloc_sbuf_tensor_at("ring", [P, RING, SLOT], F32, offset=ring_place)
        ring_r = nc.alloc_sbuf_tensor_at("ring_r", [P, RING, SLOT], F32R, offset=ring_place)
        NBUF, BUF = 13, KT * T
        sb("arena_place", [P, NBUF * BUF])
        place = nc.sbuf_base - NBUF * BUF * 4
        arena = nc.alloc_sbuf_tensor_at("arena", [P, NBUF * BUF], F32, offset=place)
        arena_r = nc.alloc_sbuf_tensor_at("arena_r", [P, NBUF * BUF], F32R, offset=place)
        cst = sb("constants", [P, C_WIDTH])
        vec = sb("vectors", [P, 256])
        mod = sb("mod", [P, 48])
        items = sb("items", [P, 2, TT, ITEMS])
        small = sb("small", [P, 192])
        rbias = sb("router_bias_rows", [P, E1])
        tab_i = sb("item_table", [1, 64], I32)
        psum = ctx.enter_context(nc.psum_tensor("psum", [P, 8, 512], F32))
        bias_dram = nc.dram_tensor("bias_rows", (HEADS, P, PAD), F32, kind="Internal").ap()

        def buf(i, n=BUF, off=0):
            return arena[:, i * BUF + off:i * BUF + off + n]

        def buf_r(i, n=BUF, off=0):
            return arena_r[:, i * BUF + off:i * BUF + off + n]

        def tiles(i, n=KT):
            return buf(i, n * T).rearrange("p (k t) -> p k t", t=T)

        ident = cst[:, C_ID:C_ID + P]
        before = cst[:, C_BEFORE:C_BEFORE + P]
        after = cst[:, C_AFTER:C_AFTER + P]
        ones = cst[:, C_ONES:C_ONES + P]
        mask3 = cst[:, C_BEFORE:C_BEFORE + 3 * P]
        iota = cst[:, C_IOTA:C_IOTA + P]

        xT, hT = tiles(0), tiles(1)
        QK = tiles(2, 16)
        V1 = buf(4).rearrange("p (t f) -> p t f", t=TT)
        G1 = tiles(5, 16)
        OT = tiles(7)
        merged = tiles(2)
        memK, memV = tiles(11), buf(12).rearrange("p (t f) -> p t f", t=TT)
        xN, memN = (buf(i).rearrange("p (t f) -> p t f", t=TT) for i in (4, 5))
        memT = tiles(10)
        sq, sq_g = [tiles(8), tiles(9)], tiles(7)
        vec_rows = buf(6, 256, 0).rearrange("p (a c) -> p a c", a=2)
        csil = buf(6, 8, 256)
        cs32 = buf(6, 256, 512).rearrange("p (k c) -> p k c", k=KT)
        ada_rows = [buf(6, 512, 1024), buf(6, 512, 1536)]
        relb = buf(3, HEADS * P, 1024).rearrange("p (h c) -> p h c", h=HEADS)
        onehot = buf(6, T, 768)
        bias_st = buf(2, HEADS * PAD).rearrange("p (h c) -> p h c", h=HEADS)
        biasT = buf(10).rearrange("p (h c) -> p h c", h=HEADS)
        W3 = 3 * P
        sc_L = buf(8, W3, 0)
        sc_lr = buf(8, W3, W3)
        sc_lb = [buf(8, W3, (2 + i) * W3) for i in range(2)]
        sc_a = [buf(8, W3, (4 + i) * W3) for i in range(2)]
        sc_p = [buf(8, W3, (6 + i) * W3) for i in range(2)]
        sc_pT = [buf(8, W3, (8 + i) * W3) for i in range(2)]
        mx1 = small[:, 0:4].rearrange("p (i t) -> p i t", i=2)
        sm1 = small[:, 4:8].rearrange("p (i t) -> p i t", i=2)
        rstd_lo = buf(8, 2 * T, 1024)

        def rstd_of(n):
            return buf(8, T, (n % 2) * T)

        gs = small[:, 8:24]
        wr1 = buf(10, KT * E1).rearrange("p (k e) -> p k e", k=KT)
        hN = buf(2).rearrange("p (t f) -> p t f", t=TT)
        hN_hi, hN_lo = (buf_r(i).rearrange("p (t f) -> p t f", t=TT) for i in (2, 3))
        hN_hi32 = buf_r(2).bitcast(F32).rearrange("p (t f) -> p t f", t=TT)
        xg1 = buf(8).rearrange("p (k c) -> p k c", k=KT)
        Pg1 = buf_r(5, 2 * T, 0).rearrange("p (t c) -> p t c", t=TT)
        Pg1_32 = buf_r(5, 2 * T, 0).bitcast(F32).rearrange("p (t c) -> p t c", t=TT)
        Pw1 = buf(5, 2 * T, 2 * T).rearrange("p (t c) -> p t c", t=TT)
        PT1 = [buf_r(5, T, (4 + i) * T) for i in range(2)]
        y_hi, y_lo = buf_r(6, D, 0), buf_r(6, D, D)
        y_hi32 = y_hi.bitcast(F32)
        sil1, aT1 = buf(10, 256, 1024), buf(10, 256, 1280)
        wslot = small[:, 48:50]
        xg = buf(3, KT * P).rearrange("p (k c) -> p k c", k=KT)
        shg_s, sha = tiles(4, 2), buf(4, 512, 512).rearrange("p (k t) -> p k t", t=T)
        rt = buf(7)
        Pg = buf(5, TT * P, 0).rearrange("p (t c) -> p t c", t=TT)
        Pw = buf(5, TT * P, 256).rearrange("p (t c) -> p t c", t=TT)
        PwT = buf(5, T, 512)
        gu_s = buf(5, 512, 1536)
        y_s = buf(6, D, 0)
        g_conv, g_mla = tiles(4), tiles(3)
        xcT, gbT = tiles(4), tiles(5)
        low = tiles(7)
        qnT, knT = tiles(6), tiles(8)
        vN = buf(9).rearrange("p (t f) -> p t f", t=TT)
        oT = qnT
        rope = buf(10, R_WIDTH)
        lsq = buf(9, 3 * T).rearrange("p (k t) -> p k t", t=T)
        spare = buf(5, 2 * T)
        at_p = [buf(10, 512, 0), buf(10, 512, 512)]
        at_pT = [buf(10, 512, 1024), buf(10, 512, 1536)]
        mx2 = small[:, 24:28].rearrange("p (i t) -> p i t", i=2)
        sm2 = small[:, 28:32].rearrange("p (i t) -> p i t", i=2)
        mqT, moT = tiles(8), tiles(9)
        wr2_flat = buf(5, KT * E2 + 16)
        wr2 = buf(5, KT * E2).rearrange("p (k e) -> p k e", k=KT)
        yn = tiles(4)
        partial = rt[:, 1536:1536 + T]
        rt2 = rt[:, 0:TT * E2].rearrange("p (t e) -> p t e", t=TT)
        sel2 = rt[:, 64:64 + TT * E2]
        sil2 = buf(6, 256, 1024)
        aT2 = [buf(4, 256, 256 * e).rearrange("p (k c) -> p k c", c=CAP2) for e in range(4)]
        zeros = buf(4, P, 1024)
        oN = buf(6).rearrange("p (t f) -> p t f", t=TT)
        rstd_col = small[:, 0:2]

        def tiles_r(i):
            return buf_r(i).rearrange("p (k t) -> p k t", t=T)

        PARTS = {"mem": (tiles_r(7), tiles_r(10)), "h1": (tiles_r(0), tiles_r(1)), "O": (tiles_r(8), tiles_r(7)),
                 "merged": (tiles_r(9), tiles_r(2)), "h4": (tiles_r(2), tiles_r(1)), "conv": (tiles_r(2), tiles_r(5)),
                 "mla": (tiles_r(1), tiles_r(6)), "yn": (tiles_r(2), tiles_r(4)), "h5": (tiles_r(2), tiles_r(1)),
                 "mo": (tiles_r(3), tiles_r(9))}
        WHOLE_X = {"mem": memT, "h1": hT, "O": OT, "merged": merged, "h4": hT, "conv": gbT, "mla": oT, "yn": yn, "h5": hT, "mo": moT}
        PART_AT = {x: i for i, x in enumerate(PARTS)}

        def vcol(name, k):
            table, off = (VEC, 0) if name in VEC else (VEC2, P)
            return vec[:, off + table[name][0] + k:off + table[name][0] + k + 1]

        def vcols(name):
            table, off = (VEC, 0) if name in VEC else (VEC2, P)
            return vec[:, off + table[name][0]:off + table[name][0] + table[name][1]]

        rows_in, x_in, mem_in, cst_in = sem("vector_rows_arrived"), sem("x_arrived"), sem("mem_arrived"), sem("constants_arrived")
        bias_out, bias_in = sem("bias_rows_written"), sem("bias_table_arrived")
        wr1_in, rope_in, wr2_in = sem("router1_arrived"), sem("rope_arrived"), sem("router2_arrived")
        out_done = sem("output_written")
        load_a = [sem(f"ring_slot{i}_loaded_a") for i in range(RING)]
        load_b = [sem(f"ring_slot{i}_loaded_b") for i in range(RING)]
        used_a, used_b = sem("chunks_used_a"), sem("chunks_used_b")
        bank_full = [sem(f"bank{i}_full") for i in range(BANKS)]
        bank_free = [sem(f"bank{i}_free") for i in range(BANKS)]
        squares_ready, mean_ready, rstd_ready, normed = (sem(n) for n in ("squares_ready", "mean_ready", "rstd_ready", "normed"))
        dve_step, act_step = sem("dve_step"), sem("act_step")
        rows_zeroed, csil_ready, cs32_ready, mod_full, mod_ready = (
            sem(n) for n in ("rows_zeroed", "c_silu_ready", "c_silu_wide_ready", "mod_columns_full", "mod_ready"))
        relb_ready, bias_staged = sem("rel_bias_wide_ready"), sem("bias_staged")
        sb_abs, sb_soft, sb_rest, sb_arg, sb_exp, sb_a = (
            sem(n) for n in ("sb_abs_ready", "sb_softplus_ready", "sb_log_rest_ready", "sb_log_a_ready", "sb_exp_ready", "sb_a_ready"))
        at_max, at_exp, at_p_ready = sem("softmax_max_ready"), sem("softmax_exp_ready"), sem("softmax_p_ready")
        gates_ready = sem("gates_ready")
        merged_ready, x_ready = sem("merged_ready"), sem("residual_ready")
        act_func = sem("act_value_ready")
        w_high, w_low = sem("weights_high_ready"), sem("weights_low_ready")
        x_high, x_low = sem("activation_high_ready"), sem("activation_low_ready")
        again_in = sem("x_arrived_again")
        sh_ready, route_ready = sem("shared_hidden_ready"), sem("routing_step_ready")
        table_ready = sem("item_table_ready")
        hn_high = sem("h_rows_high_ready")
        y_high0, y_high1, y_copied = sem("y0_high_ready"), sem("y1_high_ready"), sem("y_split")
        p_ready, gathered, g_copied = sem("onehot_ready"), sem("gathered"), sem("gather_copied")
        gu_copied, turned, sil_ready, aT_ready = sem("gu_copied"), sem("gu_transposed"), sem("silu_ready"), sem("hidden_ready")
        y0_done, pT_done, pT_copied, scattered = (sem(n) for n in ("y0_done", "onehot_transposed", "onehot_copied", "scattered"))
        acc_ready, acc_read = sem("accumulators_ready"), sem("accumulators_read")
        zeros_ready = sem("zeros_ready")
        act_squares = sem("squares_by_scalar_ready")
        gained, dve_gained = sem("first_half_times_gain"), sem("second_half_times_gain")
        q_scaled, rope_done, conv_ready = sem("low_rank_normed"), sem("rotated"), sem("convolved")
        p2_ready, gathered2, g2_copied, pwT2_done, pwT2_copied, gu2_copied, turned2, sil2_ready, aT2_ready, y20_copied, y21_copied, scattered2 = (
            sem(n + "_moe2") for n in ("onehot_ready", "gathered", "gather_copied", "weights_transposed", "weights_copied", "gu_copied",
                                       "gu_transposed", "silu_ready", "hidden_ready", "y0_copied", "y1_copied", "scattered"))

        block = ctx.enter_context(nc.Block())

        def bank(name):
            return psum[:, AT[name][0], :]

        def full(eng, name):
            eng.wait_ge(bank_full[AT[name][0]], AT[name][1] + 1)
            return bank(name)

        def evacuated(eng, name):
            eng.wait_ge(bank_free[AT[name][0]], AT[name][1] + 1)

        def frees(ins, name):
            ins.then_inc(bank_free[AT[name][0]], 1)

        def where(chunk_id):
            part, n = chunk_id
            chunks, at, base, loads = (CHUNKS_A, SLOT_A, 0, load_a) if part == "a" else (CHUNKS_B, SLOT_B, NA, load_b)
            s = at[n] % RING
            return s, loads[s], 16 * sum(pieces(chunks[m]) for m in range(n + 1) if at[m] % RING == s)

        def pieces(spec):
            return 2 if spec[0] == "shared_gu" or spec[:3] == ("w_in_2", 3072, 512) else 1

        def split_views(k, q):
            s = where(SPLIT[k])[0]
            c = slice(q * SLOT // 4, (q + 1) * SLOT // 4)
            return ring[:, s, c], ring_r[:, s, c], ring_r[:, (s + 1) % RING, c]

        @block.sync
        def _(sp):
            def load(ap, spec, done):
                name, c0, cols, k = spec
                if spec[:3] == ("w_in_2", 3072, 512):
                    dst = ap.rearrange("p (k c) -> p k c", k=k)
                    src = a[name][0].rearrange("(k p) c -> p k c", p=P)
                    sp.dma_start(dst[:, :, 0:448], src[:, :, 3072:3520]).then_inc(done, 16)
                    sp.dma_start(dst[:, :, 448:512], src[:, :, 3456:3520]).then_inc(done, 16)
                elif name == "shared_gu":
                    half = ap.rearrange("p (g k f) -> p g k f", g=2, k=KT)
                    sp.dma_start(half[:, 0], a["w_gate_sh"][0].rearrange("(k p) f -> p k f", p=P)).then_inc(done, 16)
                    sp.dma_start(half[:, 1], a["w_up_sh"][0].rearrange("(k p) f -> p k f", p=P)).then_inc(done, 16)
                else:
                    sp.dma_start(ap[:, 0:k * cols].rearrange("p (k c) -> p k c", k=k),
                                 a[name][0, :, c0:c0 + cols].rearrange("(k p) c -> p k c", p=P)).then_inc(done, 16)

            sp.dma_start(memN, a["mem_2"][0].rearrange("(t p) f -> p t f", p=P)).then_inc(mem_in, 16)
            sp.dma_start(xN, a["x"][0].rearrange("(t p) f -> p t f", p=P)).then_inc(x_in, 16)
            sp.wait_ge(cst_in, 48)
            sp.wait_ge(rows_in, 16 * (len(VEC) + len(VEC2)))
            for n, spec in enumerate(CHUNKS_A):
                if SLOT_A[n] >= RING:
                    sp.wait_ge(used_a, SLOT_A[n] - RING + 1)
                load(ring[:, SLOT_A[n] % RING, :], spec, load_a[SLOT_A[n] % RING])

            def moe1_chunk(c, experts, done):
                s = (NA + c) % RING
                pair, what = c // 3, c % 3
                if what < 2:
                    e = experts[2 * pair + what]
                    dst = ring[:, s, :].rearrange("p (g k f) -> p g (k f)", g=2, k=KT)
                    for g, w in enumerate(("w_gate_e", "w_up_e")):
                        sp.dma_start(dst[:, g], a[w][0, e].rearrange("(p k) f -> p (k f)", p=P)).then_inc(done, 16)
                else:
                    dst = ring[:, s, :].rearrange("p (e k) -> p e k", e=2)
                    for j in range(2):
                        sp.dma_start(dst[:, j], a["w_down_e"][0, experts[2 * pair + j]].rearrange("(p k) f -> p (k f)", p=P))\
                          .then_inc(done, 16)

            with sp.Fori(0, TURNS1) as i:
                for c in range(6):
                    sp.wait_ge(used_a, i * 6 + (NA + c - RING + 1))
                    moe1_chunk(c, [i * 4 + j for j in range(4)], load_a[(NA + c) % RING])
            sp.wait_ge(table_ready, 1)
            extra = sp.value_load(tab_i[0:1, 32:33], min_val=0, max_val=EXTRA // 4)
            turns = sp.snap(extra + TURNS1)
            with sp.If(extra > 0):
                with sp.Fori(TURNS1, turns) as i:
                    es = [sp.value_load(tab_i[0:1, bass.ds(i * 4 + (j - E1), 1)], min_val=0, max_val=E1 - 1) for j in range(4)]
                    for c in range(6):
                        sp.wait_ge(used_a, i * 6 + (NA + c - RING + 1))
                        moe1_chunk(c, es, load_a[(NA + c) % RING])
            for n, spec in enumerate(CHUNKS_B):
                m = SLOT_B[n] - NA
                if m < RING:
                    sp.wait_ge(used_a, turns * 6 + (NA + m - RING + 1))
                else:
                    sp.wait_ge(used_b, m - RING + 1)
                load(ring[:, SLOT_B[n] % RING, :], spec, load_b[SLOT_B[n] % RING])
            with sp.Fori(0, TURNS2) as i:
                for c in range(24):
                    s = (NA + NB + c) % RING
                    sp.wait_ge(used_b, i * 24 + (NB + c - RING + 1))
                    if c < 16:
                        dst = ring[:, s, :].rearrange("p (g k) -> p g k", g=2)
                        for g, w in enumerate(("w_exp_gate_2", "w_exp_up_2")):
                            src = a[w][0, i * 4 + c // 4].rearrange("(p k) f -> p (k f)", p=P)
                            sp.dma_start(dst[:, g], src[:, (c % 4) * 2 * FF2:((c % 4) + 1) * 2 * FF2]).then_inc(load_b[s], 16)
                    else:
                        dst = ring[:, s, :].rearrange("p (e f) -> p e f", e=4)
                        for j in range(4):
                            sp.dma_start(dst[:, j], a["w_exp_down_2"][0, i * 4 + j, (c - 16) * P:(c - 15) * P, :])\
                              .then_inc(load_b[s], 16)
            for j in range(4):
                t, half = j // 2, slice(512 * (j % 2), 512 * (j % 2) + 512)
                evacuated(sp, f"oN{j}")
                sp.dma_start(out[0, t * P:(t + 1) * P, half], oN[:, t, half]).then_inc(out_done, 16)
            sp.wait_ge(out_done, 64)

        def arrived(eng, chunk_id):
            _, done, value = where(chunk_id)
            eng.wait_ge(done, value)

        def arrived_moe1(eng, i, c):
            s = (NA + c) % RING
            base = sum(pieces(CHUNKS_A[m]) for m in range(len(CHUNKS_A)) if SLOT_A[m] % RING == s)
            eng.wait_ge(load_a[s], i * 32 + 16 * (base + 2))

        def arrived_moe2(eng, i, c):
            s = (NA + NB + c) % RING
            base = sum(pieces(CHUNKS_B[m]) for m in range(len(CHUNKS_B)) if SLOT_B[m] % RING == s)
            parts = [2] * 16 + [4] * 8
            mine = [m for m in range(24) if (NA + NB + m) % RING == s]
            eng.wait_ge(load_b[s], i * (16 * sum(parts[m] for m in mine)) + 16 * (base + sum(parts[m] for m in mine if m <= c)))

        @block.gpsimd
        def _(pool):
            pool.dma_start(cst[:, :], a["cst"]).then_inc(cst_in, 16)
            pool.dma_start(rbias[:, :], a["router_bias"][0:1, :].to_broadcast([P, E1])).then_inc(cst_in, 16)
            pool.dma_start(onehot[0:32, :], a["buckets"]).then_inc(cst_in, 16)
            pool.wait_ge(bias_staged, 2 * HEADS)
            pool.dma_start(bias_dram.rearrange("h p c -> p h c"), bias_st).then_inc(bias_out, 16)
            pool.wait_ge(bias_out, 16)
            skew = bass.AP(bias_dram.tensor, P - 1, [[PAD - 1, P], [P * PAD, HEADS], [1, T]])
            pool.dma_start(biasT, skew).then_inc(bias_in, 16)
            evacuated(pool, "av7")
            pool.dma_start(xN, a["x"][0].rearrange("(t p) f -> p t f", p=P)).then_inc(again_in, 16)
            pool.wait_ge(at_exp, HEADS)
            pool.dma_start(wr1, a["w_router"][0].rearrange("(k p) e -> p k e", p=P)).then_inc(wr1_in, 16)
            evacuated(pool, "route1")
            pool.dma_start(rope, a["rope"]).then_inc(rope_in, 16)
            pool.wait_ge(x_low, 4 * PART_AT["yn"] + 4)
            evacuated(pool, "mix0")
            pool.dma_start(wr2, a["w_router_2"][0].rearrange("(k p) e -> p k e", p=P)).then_inc(wr2_in, 16)

        @block.scalar
        def _(act):
            A = nc.scalar.activation

            def copy_out(name, dst, src=None):
                src = full(act, name) if src is None else src
                frees(A(dst, src, ACT.Copy), name)

            turns_a = [None]

            def high(k, quarters=range(4)):
                if k >= len(SPLIT):
                    return
                for q in quarters:
                    if q == 0:
                        arrived(act, SPLIT[k])
                        part, n = SPLIT[k]
                        m = (SLOT_A if part == "a" else SLOT_B)[n] + 1
                        if part == "a":
                            if m >= RING:
                                act.wait_ge(used_a, m - RING + 1)
                        elif m - NA < RING:
                            act.wait_ge(used_a, turns_a[0] * 6 + (m - RING + 1))
                        else:
                            act.wait_ge(used_b, m - NA - RING + 1)
                    whole, _, hi = split_views(k, q)
                    A(hi, whole, ACT.Copy).then_inc(w_high, 1)

            def x_high_part(name, half):
                for q in (4 * half, 4 * half + 2):
                    k = slice(q, q + 2)
                    A(PARTS[name][0][:, k, :], WHOLE_X[name][:, k, :], ACT.Copy).then_inc(x_high, 1)

            def normed_high(name, n):
                for half in range(2):
                    act.wait_ge(normed, 2 * n + half + 1)
                    x_high_part(name, half)

            act.wait_ge(rows_zeroed, 1)
            for table, half in ((VEC, 0), (VEC2, 1)):
                for name, (r0, n) in table.items():
                    src = a[name]
                    if name == "rel_bias":
                        act.dma_start(vec_rows[r0:r0 + n, half, 0:32], src).then_inc(rows_in, 16)
                        continue
                    if name == "conv_w_2":
                        src = src[0].rearrange("w (k c) -> (w k) c", c=P)
                    elif len(src.shape) == 1:
                        src = src.rearrange("(k c) -> k c", c=P)
                    else:
                        src = src[0].rearrange("(k c) -> k c", c=P)
                    act.dma_start(vec_rows[r0:r0 + n, half, :], src).then_inc(rows_in, 16)

            evacuated(act, "vec")
            A(csil, vcols("c"), ACT.Silu).then_inc(csil_ready, 1)
            for dst, nm in ((memT, "memT"), (xT, "xT")):
                for j in range(4):
                    copy_out(f"{nm}{j}", dst[:, 2 * j:2 * j + 2, :], full(act, f"{nm}{j}").rearrange("p (k t) -> p k t", t=T))

            def rms_act(n):
                act.wait_ge(mean_ready, n + 1)
                A(rstd_of(n), rstd_of(n), ACT.Ln).then_inc(act_step, 1)
                act.wait_ge(act_step, n + 1)
                A(rstd_of(n), rstd_of(n), ACT.Exp, scale=-0.5).then_inc(rstd_ready, 1)

            rms_act(0)
            rms_act(1)

            def ada_copy(n):
                if n >= 2:
                    act.wait_ge(mod_full, n - 1)
                copy_out(f"ada{n}", ada_rows[n % 2])

            for i, x in enumerate(START):
                g = START[:i].count(x)
                if x == "a":
                    ada_copy(g)
                    continue
                if g == 0:
                    normed_high("mem", 0)
                    high(0)
                high(g + 1)
                for j in range(2):
                    nm = f"memkv{g}_{j}"
                    if g < 2:
                        copy_out(nm, memK[:, 4 * g + 2 * j:4 * g + 2 * j + 2, :], full(act, nm).rearrange("p (k t) -> p k t", t=T))
                    else:
                        copy_out(nm, memV[:, j, 512 * (g - 2):512 * (g - 1)])
                if g == 0:
                    act.wait_ge(bias_staged, HEADS)
                for h in (2 * g, 2 * g + 1):
                    ps = full(act, f"rel{h}")
                    frees(A(bias_st[:, h, 0:T], ps[:, 0:T], ACT.Copy), f"rel{h}")
                    evacuated(act, f"rel{h}")
                    act.sem_inc(bias_staged, 1)
            normed_high("h1", 1)
            for c in range(6):
                high(5 + c)
                for j in range(2):
                    nm = f"in{c}_{j}"
                    if c in (0, 1, 3, 4):
                        m = 4 * (c - (c > 2)) + 2 * j
                        if m < 12:
                            act.wait_ge(bias_out, 16)
                        copy_out(nm, QK[:, m:m + 2, :], full(act, nm).rearrange("p (k t) -> p k t", t=T))
                    else:
                        copy_out(nm, V1[:, j, 512 * (c // 3):512 * (c // 3) + 512])
                ada_copy(ADA_FIRST + c)
            for s in range(HEADS + 2):
                if s < HEADS:
                    high(11 + s // 2, (2 * (s % 2), 2 * (s % 2) + 1))
                    ps = full(act, f"z{s}")
                    if s >= 1:
                        act.wait_ge(sb_rest, s)
                    A(sc_L, ps[:, 0:W3], ACT.Abs, scale=HD ** -0.5).then_inc(sb_abs, 1)
                    act.wait_ge(sb_abs, 3 * s + 1)
                    A(sc_L, sc_L, ACT.Exp, scale=-1.0).then_inc(sb_abs, 1)
                    act.wait_ge(sb_abs, 3 * s + 2)
                    act.wait_ge(cst_in, 48)
                    A(sc_L, sc_L, ACT.Ln, bias=ones[:, 0:1]).then_inc(sb_abs, 1)
                    act.wait_ge(at_max, s + 1)
                    A(sc_p[s % 2][:, 0:P], sc_p[s % 2][:, 0:P], ACT.Exp, bias=mx1[:, s % 2, 0:1],
                      accum_out=sm1[:, s % 2, 0:1])
                    A(sc_p[s % 2][:, P:W3], sc_p[s % 2][:, P:W3], ACT.Exp, bias=mx1[:, s % 2, 1:2],
                      accum_out=sm1[:, s % 2, 1:2]).then_inc(at_exp, 1)
                    nm = f"in{6 + s // 2}_{s % 2}"
                    copy_out(nm, G1[:, 2 * s:2 * s + 2, :], full(act, nm).rearrange("p (k t) -> p k t", t=T))
                    if s in (1, 3):
                        ada_copy(ADA_FIRST + 6 + s // 2)
                if 1 <= s <= HEADS:
                    h = s - 1
                    act.wait_ge(sb_arg, s)
                    A(sc_a[h % 2], sc_a[h % 2], ACT.Exp).then_inc(sb_exp, 1)
                    copy_out(f"pT{h}", sc_pT[h % 2], full(act, f"pT{h}")[:, 0:W3])
                if s >= 2:
                    h = s - 2
                    r = 64 * (h % 2)
                    ps = full(act, f"av{h}")
                    frees(A(OT[r:r + 64, h // 2::4, :], ps[r:r + 64, :].rearrange("p (b t) -> p b t", b=2), ACT.Copy), f"av{h}")
                if s == HEADS:
                    high(15, (0, 1))
            evacuated(act, "av7")
            evacuated(act, "av6")
            full(act, "pT7")
            x_high_part("O", 0)
            x_high_part("O", 1)
            high(15, (2, 3))
            evacuated(act, "in9_1")
            for q in (0, 2, 1, 3):
                A(G1[:, 4 * q:4 * q + 4, :], G1[:, 4 * q:4 * q + 4, :], ACT.Sigmoid).then_inc(gates_ready, 1)
            for half in range(2):
                act.wait_ge(merged_ready, 2 * half + 2)
                if half == 0:
                    high(16)
                x_high_part("merged", half)
            for j in range(4):
                copy_out(f"again{j}", xT[:, 2 * j:2 * j + 2, :], full(act, f"again{j}").rearrange("p (k t) -> p k t", t=T))
            high(17)
            rms_act(2)
            for k in range(KT):
                if k % 4 == 0:
                    act.wait_ge(normed, 4 + k // 4 + 1)
                A(hT[:, k, :], hT[:, k, :], ACT.Identity, bias=mod[:, 24 + k:25 + k]).then_inc(act_func, 1)
            act.wait_ge(route_ready, 1)
            A(rt[:, 0:P], rt[:, 0:P], ACT.Exp, scale=-1.0).then_inc(act_func, 1)
            for j in range(4):
                nm = f"hN{j}"
                if j == 0:
                    evacuated(act, "out3")
                t, half = j // 2, j % 2
                dst = hN_hi[:, t, :].rearrange("p (k c) -> p c k", k=KT)[:, 64 * half:64 * half + 64, :]
                A(dst, full(act, nm).rearrange("p (c k) -> p c k", k=KT), ACT.Copy).then_inc(hn_high, 1)
            frees(A(shg_s, full(act, "shg").rearrange("p (k t) -> p k t", t=T), ACT.Silu), "shg")

            act.wait_ge(table_ready, 1)
            extra = act.value_load(tab_i[0:1, 32:33], min_val=0, max_val=EXTRA // 4)
            turns1 = act.snap(extra + TURNS1)
            turns_a[0] = turns1
            with act.Fori(0, turns1) as i:
                for j in range(PAIRS_PER_TURN):
                    act.wait_ge(used_a, i * 6 + (NA + 3 * j + 2))
                    A(gu_s, psum[:, 5, :], ACT.Copy).then_inc(gu_copied, 1)
                    act.wait_ge(turned, i * 2 + (j + 1))
                    act.wait_ge(aT_ready, i * 2 + (j + 1))
                    A(sil1, psum[:, 6, 0:256], ACT.Silu).then_inc(sil_ready, 1)
                    act.wait_ge(pT_copied, i * 2 + (j + 1))
                    act.wait_ge(y0_done, i * 2 + (j + 1))
                    A(y_hi[:, 0:512], psum[:, 4, :], ACT.Copy, scale=wslot[:, j:j + 1]).then_inc(y_high0, 1)
                    act.wait_ge(used_a, i * 6 + (NA + 3 * j + 3))
                    A(y_hi[:, 512:D], psum[:, 7, :], ACT.Copy, scale=wslot[:, j:j + 1]).then_inc(y_high1, 1)

            kb = SPLIT_AT[("b", 0)]
            for j in range(4):
                act.wait_ge(acc_read, j + 1)
                A(sq[1][:, 2 * j:2 * j + 2, :], xT[:, 2 * j:2 * j + 2, :], ACT.Square).then_inc(act_squares, 1)
            high(kb, (0, 1))
            rms_act(3)
            high(kb, (2, 3))
            rms_act(4)
            normed_high("h4", 4)
            high(kb + 1)
            for nm, dst in (("cq", low[:, 0:2, :]), ("ckv", low[:, 2:4, :])):
                copy_out(nm, dst, full(act, nm).rearrange("p (k t) -> p k t", t=T))
            high(kb + 2)
            for j in range(2):
                copy_out(f"xc{j}", xcT[:, 2 * j:2 * j + 2, :], full(act, f"xc{j}").rearrange("p (k t) -> p k t", t=T))
            act.wait_ge(q_scaled, 1)
            A(rstd_lo, rstd_lo, ACT.Ln).then_inc(act_func, 1)
            act.wait_ge(act_func, 10)
            A(rstd_lo, rstd_lo, ACT.Exp, scale=-0.5).then_inc(act_func, 1)
            for j in range(2, 4):
                copy_out(f"xc{j}", xcT[:, 2 * j:2 * j + 2, :], full(act, f"xc{j}").rearrange("p (k t) -> p k t", t=T))
            for j in range(4):
                copy_out(f"qn{j}", qnT[:, 2 * j:2 * j + 2, :], full(act, f"qn{j}").rearrange("p (k t) -> p k t", t=T))
            for j in range(2):
                copy_out(f"qr{j}", low[:, 4 + 2 * j:6 + 2 * j, :], full(act, f"qr{j}").rearrange("p (k t) -> p k t", t=T))
            for j in range(4):
                copy_out(f"kn{j}", knT[:, 2 * j:2 * j + 2, :], full(act, f"kn{j}").rearrange("p (k t) -> p k t", t=T))
            for j in range(4):
                if j == 0:
                    act.wait_ge(q_scaled, 2)
                copy_out(f"v{j}", vN[:, j // 2, 512 * (j % 2):512 * (j % 2) + 512])
            high(kb + 3)
            for s in range(HEADS + 2):
                if s < HEADS:
                    act.wait_ge(at_max, HEADS + s + 1)
                    for t in range(TT):
                        ins = A(at_p[s % 2][:, t * T:(t + 1) * T], bank(f"ls{s}")[:, t * T:(t + 1) * T], ACT.Exp,
                                bias=mx2[:, s % 2, t:t + 1], scale=(MLA_NOPE + MLA_ROPE) ** -0.5,
                                accum_out=sm2[:, s % 2, t:t + 1])
                    frees(ins, f"ls{s}")

                def fill(n):
                    nm = f"fill{n}"
                    if n < 4:
                        copy_out(nm, gbT[:, 2 * n:2 * n + 2, :], full(act, nm).rearrange("p (k t) -> p k t", t=T))
                    elif n >= 8:
                        ps = full(act, nm)
                        for t in range(2):
                            m = 2 * (n - 8) + t
                            g, k = (g_conv, m) if m < 8 else (g_mla, m - 8)
                            if n == 8:
                                act.wait_ge(conv_ready, KT)
                            ins = A(g[:, k, :], ps[:, t * T:(t + 1) * T], ACT.Identity, bias=vcol("b_gate_2", m))
                        frees(ins, nm)
                if s < HEADS:
                    high(kb + 4 + s, (0, 1))
                    fill(2 * s)
                if 1 <= s <= HEADS:
                    copy_out(f"lp{s - 1}", at_pT[(s - 1) % 2])
                if s < HEADS:
                    high(kb + 4 + s, (2, 3))
                    fill(2 * s + 1)
                if s >= 2:
                    copy_out(f"lo{s - 2}", oT[:, s - 2, :], full(act, f"lo{s - 2}")[:, 0:T])
            x_high_part("conv", 0)
            x_high_part("conv", 1)
            high(kb + 12)
            evacuated(act, "lo7")
            evacuated(act, "fill15")
            x_high_part("mla", 0)
            x_high_part("mla", 1)
            for g in (g_conv, g_mla):
                for half in range(2):
                    A(g[:, 4 * half:4 * half + 4, :], g[:, 4 * half:4 * half + 4, :], ACT.Sigmoid).then_inc(gates_ready, 1)
            high(kb + 13)
            high(kb + 14)
            act.wait_ge(merged_ready, 6)
            x_high_part("yn", 0)
            high(kb + 15)
            act.wait_ge(merged_ready, 8)
            x_high_part("yn", 1)
            high(kb + 16)
            high(kb + 17)
            rms_act(5)
            normed_high("h5", 5)
            high(kb + 18)
            high(kb + 19)
            for j in range(4):
                copy_out(f"mq{j}", mqT[:, 2 * j:2 * j + 2, :], full(act, f"mq{j}").rearrange("p (k t) -> p k t", t=T))
            def memory_exp(s):
                act.wait_ge(at_max, 2 * HEADS + s + 1)
                for t in range(TT):
                    ins = A(at_p[s % 2][:, t * T:(t + 1) * T], bank(f"mS{s}")[:, t * T:(t + 1) * T], ACT.Exp,
                            bias=mx2[:, s % 2, t:t + 1], scale=T ** -0.5, accum_out=sm2[:, s % 2, t:t + 1])
                frees(ins, f"mS{s}")

            memory_exp(0)
            memory_exp(1)
            for s in range(MEMH):
                copy_out(f"mP{s}", at_pT[s % 2])
                if s + 2 < MEMH:
                    memory_exp(s + 2)
                copy_out(f"mO{s}", moT[:, 2 * s:2 * s + 2, :], full(act, f"mO{s}").rearrange("p (k t) -> p k t", t=T))
            evacuated(act, "mO3")
            x_high_part("mo", 0)
            x_high_part("mo", 1)
            high(kb + 20)
            rms_act(6)
            act.wait_ge(at_max, 2 * HEADS + MEMH + 1)
            for t in range(TT):
                ins = A(rt2[:, t, :], bank("route2")[:, t * E2:(t + 1) * E2], ACT.Exp, bias=mx2[:, 0, t:t + 1],
                        accum_out=sm2[:, 0, t:t + 1])
            frees(ins, "route2")
            for j in range(4):
                nm = f"gN{j}"
                t, half = j // 2, j % 2
                dst = hN[:, t, :].rearrange("p (k c) -> p c k", k=KT)[:, 64 * half:64 * half + 64, :]
                frees(A(dst, full(act, nm).rearrange("p (c k) -> p c k", k=KT), ACT.Copy), nm)
            act.sem_inc(y20_copied, 1)
            with act.Fori(0, TURNS2) as i:
                for e in range(4):
                    act.wait_ge(used_b, i * 24 + (NB + 4 * e + 4))
                    A(gu_s, psum[:, 5 + 2 * (e % 2), :], ACT.Copy).then_inc(gu2_copied, 1)
                    act.wait_ge(turned2, i * 4 + (e + 1))
                    act.wait_ge(aT2_ready, i * 4 + (e + 1))
                    A(sil2.rearrange("p (f c) -> p f c", c=64),
                      psum[:, 6, :].rearrange("p (f c) -> p f c", c=P)[:, :, 0:64], ACT.Silu).then_inc(sil2_ready, 1)
                act.wait_ge(used_b, i * 24 + (NB + 24))
                act.wait_ge(scattered2, i + 1)
                A(y_s[:, 0:512], psum[:, 5, :], ACT.Copy).then_inc(y20_copied, 1)
            for j in range(4):
                act.wait_ge(acc_read, 5 + j)
                A(sq[1][:, 2 * j:2 * j + 2, :], xT[:, 2 * j:2 * j + 2, :], ACT.Square).then_inc(act_squares, 1)
                if j < 2:
                    for k in (2 * j, 2 * j + 1):
                        ins = A(hT[:, k, :], xT[:, k, :], ACT.Copy, scale=vcol("norm_final_g_2", k))
            ins.then_inc(gained, 1)
            A(rstd_col, full(act, "rstdT")[:, 0:T].rearrange("p (t c) -> p t c", t=TT)[:, :, 0], ACT.Ln).then_inc(act_step, 1)
            act.wait_ge(act_step, 8)
            frees(A(rstd_col, rstd_col, ACT.Exp, scale=-0.5), "rstdT")
            evacuated(act, "rstdT")
            for j in (1, 3):
                frees(A(oN[:, j // 2, 512:D], full(act, f"oN{j}"), ACT.Copy, scale=rstd_col[:, j // 2:j // 2 + 1]), f"oN{j}")

        @block.vector
        def _(dve):
            V = nc.vector
            steps = [0]

            def step(ins):
                ins.then_inc(dve_step, 1)
                steps[0] += 1
                return steps[0]

            def after_step(n=None):
                dve.wait_ge(dve_step, steps[0] if n is None else n)

            def low_part(k, quarters=range(4)):
                if k >= len(SPLIT):
                    return
                for q in quarters:
                    dve.wait_ge(w_high, 4 * k + q + 1)
                    whole, lo, hi = split_views(k, q)
                    V.tensor_tensor(lo, whole, hi.bitcast(F32), ALU.subtract).then_inc(w_low, 1)

            def x_low_part(name, half):
                hi, lo = PARTS[name]
                for q in (4 * half, 4 * half + 2):
                    k = slice(q, q + 2)
                    dve.wait_ge(x_high, 4 * PART_AT[name] + q // 2 + 1)
                    V.tensor_tensor(lo[:, k, :], WHOLE_X[name][:, k, :], hi[:, k, :].bitcast(F32), ALU.subtract).then_inc(x_low, 1)

            V.memset(vec_rows, 0.0).then_inc(rows_zeroed, 1)
            ps = full(dve, "vec")
            frees(V.tensor_copy(vec[:, :], ps[:, 0:256]), "vec")
            evacuated(dve, "vec")
            dve.wait_ge(csil_ready, 1)
            dve.wait_ge(cst_in, 48)
            for k in range(KT):
                ins = V.tensor_scalar(cs32[:, k, :], ones[:, 0:32], csil[:, k:k + 1], None, ALU.mult)
            ins.then_inc(cs32_ready, 1)
            for h in range(HEADS):
                ins = V.tensor_scalar(relb[0:32, h, :], ones[0:32, :], vcol("rel_bias", h)[0:32, :], None, ALU.mult)
            ins.then_inc(relb_ready, 1)
            for h in range(HEADS):
                V.memset(bias_st[:, h, T:PAD], NEG).then_inc(bias_staged, 1)
            g_sq, g_both = small[:, 32:40], small[:, 40:48]
            step(V.tensor_tensor(g_both, vcols("final_g"), vcols("norm_mix_g_2"), ALU.mult))
            step(V.tensor_tensor(g_sq, vcols("final_g"), vcols("final_g"), ALU.mult))

            def squares(src, sqb, j, gain_sq=None):
                if gain_sq is None:
                    k = slice(2 * j, 2 * j + 2)
                    V.tensor_tensor(sqb[:, k, :], src[:, k, :], src[:, k, :], ALU.mult).then_inc(squares_ready, 1)
                    return
                for k in (2 * j, 2 * j + 1):
                    ins = V.scalar_tensor_tensor(sqb[:, k, :], src[:, k, :], gain_sq[:, k:k + 1], src[:, k, :], ALU.mult, ALU.mult)
                ins.then_inc(squares_ready, 1)

            def mean(n):
                name = f"ms{n}"
                ps = full(dve, name)
                frees(V.tensor_scalar(rstd_of(n), ps[:, 0:T], 1.0 / D, EPS, ALU.mult, ALU.add), name)
                evacuated(dve, name)
                dve.sem_inc(mean_ready, 1)

            def scaled(n, dst, src, gain, shift=None):
                dve.wait_ge(rstd_ready, n + 1)
                for k in range(KT):
                    ins = V.scalar_tensor_tensor(dst[:, k, :], src[:, k, :], gain(k), rstd_of(n), ALU.mult, ALU.mult)
                    if shift is not None:
                        step(ins)
                    elif k % 4 == 3:
                        ins.then_inc(normed, 1)
                if shift is not None:
                    after_step()
                    for k in range(KT):
                        ins = V.tensor_scalar(dst[:, k, :], dst[:, k, :], shift(k), None, ALU.add)
                        if k % 4 == 3:
                            ins.then_inc(normed, 1)

            for j in range(4):
                evacuated(dve, f"memT{j}")
                squares(memT, sq[0], j)
            for j in range(4):
                evacuated(dve, f"xT{j}")
                squares(xT, sq[1], j)
            mean(0)
            mean(1)
            scaled(0, memT, memT, lambda k: vcol("norm_memkv_g_2", k))
            x_low_part("mem", 0)
            x_low_part("mem", 1)
            low_part(0)
            low_part(1)
            NF = 4 * ADA_FIRST
            dve.wait_ge(mod_full, ADA_FIRST)
            V.tensor_tensor(mod[:, 0:NF], psum[:, 7, 0:NF], vcols("b_ada")[:, 0:NF], ALU.add).then_inc(mod_ready, 1)
            dve.wait_ge(mod_ready, 1)
            step(V.scalar_tensor_tensor(gs[:, 0:8], mod[:, 8:16], 1.0, vcols("norm1_g"), ALU.add, ALU.mult))
            after_step()
            low_part(2)
            scaled(1, hT, xT, lambda k: gs[:, k:k + 1], shift=lambda k: mod[:, k:k + 1])
            low_part(3)
            low_part(4)
            x_low_part("h1", 0)
            x_low_part("h1", 1)
            for c in range(6):
                low_part(5 + c)

            for s in range(HEADS + 2):
                if s < HEADS:
                    h = s
                    low_part(11 + s // 2, (2 * (s % 2), 2 * (s % 2) + 1))
                    ps = full(dve, f"z{h}")
                    dve.wait_ge(sb_abs, 3 * h + 1)
                    step(V.tensor_scalar(sc_lb[h % 2], ps[:, 0:W3], HD ** -0.5, 0.0, ALU.mult, ALU.min))
                    z = ps
                    ps = full(dve, f"s{h}")
                    if h == 0:
                        dve.wait_ge(bias_in, 16)
                    if h >= 2:
                        full(dve, f"pT{h - 2}")
                    p = sc_p[h % 2]
                    V.scalar_tensor_tensor(p[:, 0:P], ps[:, 0:P], HD ** -0.5, biasT[:, h, P:T], ALU.mult, ALU.add)
                    frees(V.scalar_tensor_tensor(p[:, P:W3], ps[:, P:W3], HD ** -0.5, biasT[:, h, :], ALU.mult, ALU.add), f"s{h}")
                    evacuated(dve, f"s{h}")
                    V.tensor_reduce(mx1[:, h % 2, 0:1], p[:, 0:P], AX, ALU.max, negate=True)
                    V.tensor_reduce(mx1[:, h % 2, 1:2], p[:, P:W3], AX, ALU.max, negate=True).then_inc(at_max, 1)
                    after_step()
                    dve.wait_ge(sb_abs, 3 * h + 3)
                    step(V.tensor_tensor(sc_lb[h % 2], sc_lb[h % 2], sc_L, ALU.subtract))
                    after_step()
                    if h >= 1:
                        full(dve, f"skip{h - 1}")
                    frees(V.scalar_tensor_tensor(sc_lr, z[:, 0:W3], -(HD ** -0.5), sc_lb[h % 2], ALU.mult, ALU.add), f"z{h}")
                    evacuated(dve, f"z{h}")
                    V.tensor_tensor(sc_lr, sc_lr, mask3, ALU.mult).then_inc(sb_rest, 1)
                if 1 <= s <= HEADS:
                    h = s - 1
                    ps = full(dve, f"skip{h}")
                    if h >= 2:
                        full(dve, f"av{h - 2}")
                    frees(V.tensor_tensor(sc_a[h % 2], sc_lb[h % 2], ps[:, 0:W3], ALU.add), f"skip{h}")
                    evacuated(dve, f"skip{h}")
                    dve.sem_inc(sb_arg, 1)
                if s < HEADS:
                    h = s
                    dve.wait_ge(at_exp, h + 1)
                    step(V.reciprocal(sm1[:, h % 2, :], sm1[:, h % 2, :]))
                    after_step()
                    p = sc_p[h % 2]
                    V.tensor_scalar(p[:, 0:P], p[:, 0:P], sm1[:, h % 2, 0:1], None, ALU.mult)
                    V.tensor_scalar(p[:, P:W3], p[:, P:W3], sm1[:, h % 2, 1:2], None, ALU.mult).then_inc(at_p_ready, 1)
                if 1 <= s <= HEADS:
                    h = s - 1
                    dve.wait_ge(sb_exp, h + 1)
                    V.tensor_tensor(sc_a[h % 2], sc_a[h % 2], mask3, ALU.mult).then_inc(sb_a, 1)
            low_part(15, (0, 1))
            x_low_part("O", 0)
            x_low_part("O", 1)
            low_part(15, (2, 3))
            dve.wait_ge(mod_full, ADA)
            step(V.tensor_tensor(mod[:, NF:48], psum[:, 7, NF:48], vcols("b_ada")[:, NF:48], ALU.add))
            after_step()
            step(V.scalar_tensor_tensor(gs[:, 8:16], mod[:, 32:40], 1.0, vcols("norm2_g"), ALU.add, ALU.mult))
            after_step()
            for j in range(4):
                dve.wait_ge(gates_ready, 2 + 2 * (j // 2))
                ps = full(dve, f"brs_{j}").rearrange("p (k t) -> p k t", t=T)
                frees(V.tensor_tensor(merged[:, 2 * j:2 * j + 2, :], ps, G1[:, 2 * j:2 * j + 2, :], ALU.mult), f"brs_{j}")
                ps = full(dve, f"brm_{j}").rearrange("p (k t) -> p k t", t=T)
                frees(V.tensor_tensor(G1[:, 8 + 2 * j:10 + 2 * j, :], ps, G1[:, 8 + 2 * j:10 + 2 * j, :], ALU.mult), f"brm_{j}")
                evacuated(dve, f"brs_{j}")
                evacuated(dve, f"brm_{j}")
                V.tensor_tensor(merged[:, 2 * j:2 * j + 2, :], merged[:, 2 * j:2 * j + 2, :], G1[:, 8 + 2 * j:10 + 2 * j, :],
                                ALU.add).then_inc(merged_ready, 1)
                if j == 1:
                    low_part(16)
                if j % 2:
                    x_low_part("merged", j // 2)
            low_part(17)
            for j in range(4):
                evacuated(dve, f"again{j}")

            def residual(name, m0, gate):
                ps = full(dve, name)
                for t in range(2):
                    ins = V.scalar_tensor_tensor(xT[:, m0 + t, :], ps[:, t * T:(t + 1) * T], gate(m0 + t), xT[:, m0 + t, :],
                                                 ALU.mult, ALU.add)
                frees(ins, name)

            for j in range(4):
                residual(f"out{j}", 2 * j, lambda m: mod[:, 16 + m:17 + m])
                evacuated(dve, f"out{j}")
                squares(xT, sq_g, j)
            mean(2)
            scaled(2, hT, xT, lambda k: gs[:, 8 + k:9 + k])

            def rows_low(j):
                t, half = j // 2, j % 2
                v = lambda ap: ap[:, t, :].rearrange("p (k c) -> p c k", k=KT)[:, 64 * half:64 * half + 64, :]
                ps = full(dve, f"hN{j}")
                dve.wait_ge(hn_high, j + 1)
                frees(V.tensor_tensor(v(hN_lo), ps.rearrange("p (c k) -> p c k", k=KT), v(hN_hi32), ALU.subtract), f"hN{j}")

            lg = rt[:, 0:P]
            sc = rt[:, P:2 * P]
            ch = rt[:, 2 * P:3 * P]
            gsc = rt[:, 3 * P:3 * P + 16]
            gtop = rt[:, 400:416]
            gm = rt[:, 416:432]
            mch = rt[:, 512:640]
            rep = rt[:, 640:768]
            top = rt[:, 768:784]
            sel = rt[:, 896:1024]
            wts = rt[:, 1024:1152]
            rk = rt[:, 1152:1280]
            t8 = rt[:, 1280:1408]
            den = rt[:, 1408:1412]
            frees(V.tensor_copy(partial, full(dve, "logit1")[:, 0:T]), "logit1")
            ps = full(dve, "route1")
            frees(V.tensor_copy(lg, ps[:, 0:P]), "route1")
            evacuated(dve, "route1")
            dve.sem_inc(route_ready, 1)
            dve.wait_ge(act_func, 9)
            step(V.tensor_scalar(lg, lg, 1.0, None, ALU.add))
            after_step()
            step(V.reciprocal(sc, lg))
            after_step()
            for t in range(TT):
                step(V.tensor_tensor(ch[:, t * E1:(t + 1) * E1], sc[:, t * E1:(t + 1) * E1], rbias[:, :], ALU.add))
            after_step()
            for g in range(TT * GROUPS):
                step(V.max(t8[:, 8 * g:8 * g + 8], ch[:, 8 * g:8 * g + 8]))
            after_step()
            tv = t8.rearrange("p (g i) -> p g i", i=8)
            step(V.tensor_tensor(gsc.rearrange("p (g i) -> p g i", i=1), tv[:, :, 0:1], tv[:, :, 1:2], ALU.add))
            after_step()
            for t in range(TT):
                step(V.max(gtop[:, 8 * t:8 * t + 8], gsc[:, 8 * t:8 * t + 8]))
            after_step()
            for t in range(TT):
                step(V.memset(gtop[:, 8 * t + 4:8 * t + 8], 3e38))
            after_step()
            for t in range(TT):
                step(V.match_replace(gm[:, 8 * t:8 * t + 8], gtop[:, 8 * t:8 * t + 8], gsc[:, 8 * t:8 * t + 8], -3e38))
            after_step()
            step(V.tensor_scalar(gm, gm, -3e38, None, ALU.is_equal))
            after_step()
            step(V.tensor_scalar(gsc, gm, -1.0, 1e30, ALU.add, ALU.mult))
            after_step()
            grouped = lambda ap: ap.rearrange("p (g i) -> p g i", i=8)
            spread = lambda ap: ap.unsqueeze(2).to_broadcast([P, 16, 8])
            step(V.tensor_tensor(grouped(mch), grouped(ch), spread(gm), ALU.mult))
            after_step()
            step(V.tensor_tensor(grouped(mch), grouped(mch), spread(gsc), ALU.add))
            after_step()
            for t in range(TT):
                step(V.max(top[:, 8 * t:8 * t + 8], mch[:, t * E1:(t + 1) * E1]))
            after_step()
            for t in range(TT):
                step(V.match_replace(rep[:, t * E1:(t + 1) * E1], top[:, 8 * t:8 * t + 8], mch[:, t * E1:(t + 1) * E1], -3e38))
            after_step()
            V.tensor_scalar(sel, rep, -3e38, None, ALU.is_equal).then_inc(route_ready, 1)
            dve.wait_ge(route_ready, 2)
            for t in range(TT):
                e = slice(t * E1, (t + 1) * E1)
                step(V.tensor_tensor(wts[:, e], sc[:, e], sel[:, e], ALU.mult))
            after_step()
            step(V.tensor_reduce(den[:, 0:2], wts.rearrange("p (t e) -> p t e", t=TT), AX, ALU.add))
            after_step()
            step(V.reciprocal(den[:, 2:4], den[:, 0:2]))
            after_step()
            for t in range(TT):
                e = slice(t * E1, (t + 1) * E1)
                step(V.tensor_scalar(wts[:, e], wts[:, e], den[:, 2 + t:3 + t], 2.5, ALU.mult, ALU.mult))
            for j in range(4):
                rows_low(j)
            ps = full(dve, "rank1")
            frees(V.scalar_tensor_tensor(rk, ps[:, 0:P], FAR, sel, ALU.add, ALU.mult), "rank1")
            evacuated(dve, "rank1")
            after_step()
            dve.sem_inc(route_ready, 1)
            for t in range(TT):
                step(V.tensor_scalar(items[:, 0, t, 0:E1], rk[:, t * E1:(t + 1) * E1], -FAR, None, ALU.add))
                step(V.tensor_copy(items[:, 1, t, 0:E1], wts[:, t * E1:(t + 1) * E1]))
            step(V.memset(items[:, 0, :, E1 + EXTRA:ITEMS], -FAR))
            step(V.memset(items[:, 1, :, E1 + EXTRA:ITEMS], 0.0))
            cnt, ex, tmp = (rt[0:64, 1416 + i:1417 + i] for i in range(3))
            st, en = (rt[0:64, 1420 + i:1421 + i] for i in range(2))
            OH, CH, ge = (rt[0:64, 1440 + 32 * i:1472 + 32 * i] for i in range(3))
            ps = full(dve, "count1")
            frees(V.tensor_copy(cnt, ps[0:64, 0:1]), "count1")
            evacuated(dve, "count1")
            step(V.tensor_scalar(ex, cnt, float(SLOTS1), None, ALU.is_gt))
            after_step()
            for j in range(2, T // SLOTS1):
                step(V.tensor_scalar(tmp, cnt, float(SLOTS1 * j), None, ALU.is_gt))
                after_step()
                step(V.tensor_tensor(ex, ex, tmp, ALU.add))
                after_step()
            dve.sem_inc(route_ready, 1)
            ps = full(dve, "start1")
            frees(V.tensor_copy(st, ps[0:64, 0:1]), "start1")
            evacuated(dve, "start1")
            step(V.tensor_tensor(en, st, ex, ALU.add))
            after_step()
            step(V.tensor_scalar(ge, iota[0:64, 0:32], en, None, ALU.is_ge))
            step(V.tensor_scalar(OH, iota[0:64, 0:32], st, None, ALU.is_ge))
            after_step()
            step(V.tensor_tensor(OH, OH, ge, ALU.subtract))
            step(V.tensor_scalar(CH, iota[0:64, 0:32], st, 1.0, ALU.subtract, ALU.add))
            after_step()
            step(V.scalar_tensor_tensor(CH, CH, -float(SLOTS1), OH, ALU.mult, ALU.mult))
            after_step()
            ps = full(dve, "tabT")
            rT = buf(8, 512, 512)
            frees(V.tensor_copy(rT[0:64, :], ps[0:64, :]), "tabT")
            evacuated(dve, "tabT")
            dve.sem_inc(route_ready, 1)
            ps = full(dve, "item")
            iv = ps[:, 0:128].rearrange("p (w t s) -> p w t s", w=2, t=TT)
            step(V.tensor_scalar(items[:, 0, :, E1:E1 + EXTRA], iv[:, 0], -FAR, None, ALU.add))
            frees(V.tensor_copy(items[:, 1, :, E1:E1 + EXTRA], iv[:, 1]), "item")
            after_step()
            evacuated(dve, "item")
            ps = full(dve, "eidx")
            frow = rt[0:1, 1600:1664]
            step(V.memset(frow, 0.0))
            after_step()
            step(V.tensor_copy(frow[:, 0:32], ps[0:1, 0:32]))
            frees(V.tensor_copy(rt[0:1, 1670:1671], ps[0:1, 32:33]), "eidx")
            evacuated(dve, "eidx")
            i4 = iota[0:1, 0:32].rearrange("p (a b) -> p a b", b=4)[:, :, 0:1]
            step(V.tensor_scalar(rt[0:1, 1680:1688].rearrange("p (a b) -> p a b", b=1), i4, rt[0:1, 1670:1671], None, ALU.is_lt))
            after_step()
            step(V.tensor_reduce(frow[:, 32:33], rt[0:1, 1680:1688], AX, ALU.add))
            after_step()
            V.tensor_copy(tab_i[:, :], frow).then_inc(table_ready, 1)
            ps = full(dve, "shu").rearrange("p (k t) -> p k t", t=T)
            evacuated(dve, "shg")
            frees(V.tensor_tensor(sha, shg_s, ps, ALU.mult), "shu")

            dve.wait_ge(table_ready, 1)
            extra = dve.value_load(tab_i[0:1, 32:33], min_val=0, max_val=EXTRA // 4)
            turns1 = dve.snap(extra + TURNS1)

            def onehots(col0):
                for t in range(TT):
                    for j in range(4):
                        r = items[:, 0, t, bass.ds(col0 + j, 1)]
                        w = items[:, 1, t, bass.ds(col0 + j, 1)]
                        c = slice(SLOTS1 * j, SLOTS1 * (j + 1))
                        V.tensor_scalar(Pg1[:, t, c], iota[:, 0:SLOTS1], r, None, ALU.is_equal)
                        ins = V.tensor_scalar(Pw1[:, t, c], iota[:, 0:SLOTS1], r, w, ALU.is_equal, ALU.mult)
                ins.then_inc(p_ready, 1)

            def gather_copy(quarter, count):
                dve.wait_ge(gathered, count)
                V.tensor_copy(xg1[:, 2 * quarter:2 * quarter + 2, :],
                              psum[:, 4 + 3 * (quarter % 2), :].rearrange("p (k c) -> p k c", k=2)).then_inc(g_copied, 1)

            def transposed_copy(pair, count):
                dve.wait_ge(pT_done, count)
                V.tensor_copy(wslot[:, pair:pair + 1], psum[:, 6, T:T + 1])
                V.tensor_copy(PT1[pair], psum[:, 6, 0:T]).then_inc(pT_copied, 1)

            V.memset(buf_r(6).bitcast(F32), 0.0)
            dve.sem_inc(aT_ready, 1)
            onehots(0)
            V.memset(PT1[1].bitcast(F32), 0.0).then_inc(y_copied, 1)
            for q in range(4):
                gather_copy(q, q + 1)
            transposed_copy(0, 1)
            with dve.Fori(0, turns1) as i:
                for j in range(PAIRS_PER_TURN):
                    if j == 1:
                        gather_copy(0, i * 4 + 5)
                        gather_copy(1, i * 4 + 6)
                    dve.wait_ge(sil_ready, i * 2 + (j + 1))
                    V.tensor_tensor(aT1, sil1, psum[:, 6, 256:512], ALU.mult).then_inc(aT_ready, 1)
                    if j == 1:
                        gather_copy(2, i * 4 + 7)
                        gather_copy(3, i * 4 + 8)
                    dve.wait_ge(y_high0, i * 2 + (j + 1))
                    V.scalar_tensor_tensor(y_lo[:, 0:512], psum[:, 4, :], wslot[:, j:j + 1], y_hi32[:, 0:512], ALU.mult, ALU.subtract)
                    transposed_copy((j + 1) % 2, i * 2 + (j + 2))
                    dve.wait_ge(y_high1, i * 2 + (j + 1))
                    V.scalar_tensor_tensor(y_lo[:, 512:D], psum[:, 7, :], wslot[:, j:j + 1], y_hi32[:, 512:D], ALU.mult, ALU.subtract)\
                     .then_inc(y_copied, 1)
                    if j == 0:
                        onehots(i * 4 + 4)
            dve.wait_ge(scattered, turns1 * 2 + 1)

            def add_accumulated(j, gate):
                for m in (2 * j, 2 * j + 1):
                    ps = psum[:, m // 2, (m % 2) * T:(m % 2) * T + T]
                    if gate is None:
                        ins = V.tensor_tensor(xT[:, m, :], ps, xT[:, m, :], ALU.add)
                    else:
                        ins = V.scalar_tensor_tensor(xT[:, m, :], ps, gate(m), xT[:, m, :], ALU.mult, ALU.add)
                ins.then_inc(acc_read, 1)

            for j in range(4):
                add_accumulated(j, lambda m: mod[:, 40 + m:41 + m])
                dve.wait_ge(acc_read, j + 1)
                squares(xT, sq_g, j, g_sq)
            kb = SPLIT_AT[("b", 0)]
            mean(3)
            low_part(kb)
            dve.wait_ge(rstd_ready, 4)
            r3, m4 = rstd_of(3), rstd_of(4)
            ps = full(dve, "ms4")
            step(V.scalar_tensor_tensor(m4, ps[:, 0:T], 1.0 / D, r3, ALU.mult, ALU.mult))
            after_step()
            step(V.tensor_tensor(m4, m4, r3, ALU.mult))
            after_step()
            frees(V.tensor_scalar(m4, m4, EPS, None, ALU.add), "ms4")
            evacuated(dve, "ms4")
            dve.sem_inc(mean_ready, 1)
            dve.wait_ge(rstd_ready, 5)
            step(V.tensor_tensor(m4, m4, r3, ALU.mult))
            after_step()
            dve.sem_inc(normed, 2)
            scaled(4, hT, xT, lambda k: g_both[:, k:k + 1])
            x_low_part("h4", 0)
            x_low_part("h4", 1)
            for k in range(KT):
                ins = V.scalar_tensor_tensor(xT[:, k, :], xT[:, k, :], vcol("final_g", k), r3, ALU.mult, ALU.mult)
            step(ins)
            after_step()
            low_part(kb + 1)

            evacuated(dve, "cq")
            evacuated(dve, "ckv")
            V.tensor_tensor(lsq, low[:, 0:3, :], low[:, 0:3, :], ALU.mult).then_inc(squares_ready, 1)
            low_part(kb + 2)
            ps = full(dve, "msq")
            step(V.tensor_scalar(rstd_lo[:, 0:T], ps[:, 0:T], 1.0 / QL, EPS, ALU.mult, ALU.add))
            frees(V.tensor_scalar(rstd_lo[:, T:2 * T], ps[:, T:2 * T], 1.0 / KVL, EPS, ALU.mult, ALU.add), "msq")
            after_step()
            evacuated(dve, "msq")
            dve.sem_inc(q_scaled, 1)
            dve.wait_ge(act_func, 11)
            for k in range(2):
                V.scalar_tensor_tensor(low[:, k, :], low[:, k, :], vcol("q_norm_g_2", k), rstd_lo[:, 0:T], ALU.mult, ALU.mult)
            V.scalar_tensor_tensor(low[:, 2, :], low[:, 2, :], vcol("kv_norm_g_2", 0), rstd_lo[:, T:2 * T],
                                   ALU.mult, ALU.mult).then_inc(q_scaled, 1)
            dve.wait_ge(rope_in, 16)
            cosT, sinT = rope[:, R_COS:R_COS + T], rope[:, R_SIN:R_SIN + T]
            for j in range(3):
                ps = full(dve, f"rot{j}")
                ms = (4 + 2 * j, 5 + 2 * j) if j < 2 else (3,)
                for n, m in enumerate(ms):
                    step(V.tensor_tensor(low[:, m, :], low[:, m, :], cosT, ALU.mult))
                    ins = V.tensor_tensor(spare[:, n * T:(n + 1) * T], ps[:, n * T:(n + 1) * T], sinT, ALU.mult)
                frees(ins, f"rot{j}")
                after_step()
                evacuated(dve, f"rot{j}")
                for n, m in enumerate(ms):
                    ins = V.tensor_tensor(low[:, m, :], low[:, m, :], spare[:, n * T:(n + 1) * T], ALU.add)
                ins.then_inc(rope_done, 1)
                dve.wait_ge(rope_done, j + 1)

            low_part(kb + 3)

            def softmax_max(name, h, scale):
                ps = full(dve, name)
                step(V.tensor_reduce(mx2[:, h % 2, :], ps.rearrange("p (t k) -> p t k", t=TT), AX, ALU.max, negate=True))
                after_step()
                V.tensor_scalar(mx2[:, h % 2, :], mx2[:, h % 2, :], scale, None, ALU.mult).then_inc(at_max, 1)

            def softmax_norm(name, h):
                evacuated(dve, name)
                step(V.reciprocal(sm2[:, h % 2, :], sm2[:, h % 2, :]))
                after_step()
                p = at_p[h % 2]
                V.tensor_scalar(p[:, 0:T], p[:, 0:T], sm2[:, h % 2, 0:1], None, ALU.mult)
                V.tensor_scalar(p[:, T:2 * T], p[:, T:2 * T], sm2[:, h % 2, 1:2], None, ALU.mult).then_inc(at_p_ready, 1)

            def conv_tile(k):
                y, v = low[:, k % 2, :], xcT[:, k, :]
                step(V.tensor_scalar(y, v, vcol("conv_w_2", 8 + k), vcol("conv_b_2", k), ALU.mult, ALU.add))
                after_step()
                step(V.scalar_tensor_tensor(y[:, 1:T], v[:, 0:T - 1], vcol("conv_w_2", k), y[:, 1:T], ALU.mult, ALU.add))
                after_step()
                step(V.scalar_tensor_tensor(y[:, 0:T - 1], v[:, 1:T], vcol("conv_w_2", 16 + k), y[:, 0:T - 1], ALU.mult, ALU.add))
                after_step()
                V.tensor_tensor(gbT[:, k, :], y, gbT[:, k, :], ALU.mult).then_inc(conv_ready, 1)

            for s in range(HEADS):
                softmax_max(f"ls{s}", s, (MLA_NOPE + MLA_ROPE) ** -0.5)
                softmax_norm(f"ls{s}", s)
                low_part(kb + 4 + s)
                for n in (2 * s, 2 * s + 1):
                    if 4 <= n < 8:
                        m = 2 * (n - 4)
                        ps = full(dve, f"fill{n}").rearrange("p (k t) -> p k t", t=T)
                        frees(V.tensor_tensor(xcT[:, m:m + 2, :], ps, xcT[:, m:m + 2, :], ALU.mult), f"fill{n}")
                        evacuated(dve, f"fill{n}")
                        evacuated(dve, f"fill{n - 4}")
                        conv_tile(m)
                        conv_tile(m + 1)
            x_low_part("conv", 0)
            x_low_part("conv", 1)
            low_part(kb + 12)
            x_low_part("mla", 0)
            x_low_part("mla", 1)
            low_part(kb + 13)
            dve.wait_ge(gates_ready, 8)
            for j in range(4):
                ps = full(dve, f"conv{j}").rearrange("p (k t) -> p k t", t=T)
                frees(V.tensor_tensor(yn[:, 2 * j:2 * j + 2, :], ps, g_conv[:, 2 * j:2 * j + 2, :], ALU.mult), f"conv{j}")
            low_part(kb + 14)
            for j in range(4):
                ps = full(dve, f"mla{j}").rearrange("p (k t) -> p k t", t=T)
                g = g_mla[:, 2 * j:2 * j + 2, :]
                frees(V.tensor_tensor(g, ps, g, ALU.mult), f"mla{j}")
                evacuated(dve, f"mla{j}")
                evacuated(dve, f"conv{j}")
                V.tensor_tensor(yn[:, 2 * j:2 * j + 2, :], yn[:, 2 * j:2 * j + 2, :], g, ALU.add).then_inc(merged_ready, 1)
                if j == 1:
                    x_low_part("yn", 0)
                    low_part(kb + 15)
            x_low_part("yn", 1)
            low_part(kb + 16)
            low_part(kb + 17)

            def plain_residual(name, m0):
                ps = full(dve, name).rearrange("p (k t) -> p k t", t=T)
                frees(V.tensor_tensor(xT[:, m0:m0 + 2, :], ps, xT[:, m0:m0 + 2, :], ALU.add), name)

            for j in range(4):
                plain_residual(f"mix{j}", 2 * j)
                evacuated(dve, f"mix{j}")
                if j == 0:
                    V.memset(wr2_flat[:, KT * E2:], 0.0)
                squares(xT, sq[1], j)
            mean(5)
            scaled(5, hT, xT, lambda k: vcol("norm_mem_g_2", k))
            x_low_part("h5", 0)
            x_low_part("h5", 1)
            low_part(kb + 18)
            low_part(kb + 19)
            for s in range(MEMH):
                softmax_max(f"mS{s}", s, T ** -0.5)
                softmax_norm(f"mS{s}", s)
            x_low_part("mo", 0)
            x_low_part("mo", 1)
            low_part(kb + 20)
            for j in range(4):
                plain_residual(f"mo{j}", 2 * j)
                evacuated(dve, f"mo{j}")
                squares(xT, sq_g, j)
            mean(6)
            scaled(6, hT, xT, lambda k: vcol("norm_moe_g_2", k))
            V.memset(zeros, 0.0).then_inc(zeros_ready, 1)
            frees(V.tensor_copy(partial, full(dve, "logit2")[:, 0:T]), "logit2")
            ps = full(dve, "route2")
            V.tensor_reduce(mx2[:, 0, :], ps[:, 0:TT * E2].rearrange("p (t e) -> p t e", t=TT), AX, ALU.max,
                            negate=True).then_inc(at_max, 1)
            evacuated(dve, "route2")
            step(V.reciprocal(sm2[:, 0, :], sm2[:, 0, :]))
            after_step()
            for t in range(TT):
                ins = V.tensor_scalar(rt2[:, t, :], rt2[:, t, :], sm2[:, 0, t:t + 1], None, ALU.mult)
            ins.then_inc(route_ready, 1)
            dve.wait_ge(route_ready, 6)
            ps = full(dve, "affT")
            aff = [rt[0:E2, 256:512], rt[0:E2, 512:768]]
            t8b = rt[0:E2, 768:776]
            frees(V.tensor_copy(aff[0], ps[0:E2, 0:T]), "affT")
            evacuated(dve, "affT")
            for r in range(CAP2 // 8):
                step(V.max(t8b, aff[r % 2]))
                after_step()
                step(V.match_replace(aff[(r + 1) % 2], t8b, aff[r % 2], -1.0))
                after_step()
            V.tensor_scalar(aff[1], aff[0], 0.0, None, ALU.is_lt).then_inc(route_ready, 1)
            ps = full(dve, "selT")
            frees(V.tensor_copy(sel2, ps[:, 0:TT * E2]), "selT")
            evacuated(dve, "selT")
            dve.sem_inc(route_ready, 1)
            step(V.tensor_tensor(items[:, 1, :, 0:E2], rt2, sel2.rearrange("p (t e) -> p t e", t=TT), ALU.mult))
            ps = full(dve, "rank2")
            frees(V.scalar_tensor_tensor(rk[:, 0:TT * E2], ps[:, 0:TT * E2], FAR, sel2, ALU.add, ALU.mult), "rank2")
            evacuated(dve, "rank2")
            after_step()
            step(V.tensor_scalar(items[:, 0, :, 0:E2], rk[:, 0:TT * E2].rearrange("p (t e) -> p t e", t=TT), -FAR, None, ALU.add))
            after_step()
            for ahead in (g2_copied, aT2_ready, y21_copied):
                dve.sem_inc(ahead, 1)
            with dve.Fori(0, TURNS2) as i:
                dve.wait_ge(pwT2_done, i + 1)
                for t in range(TT):
                    for j in range(4):
                        r = items[:, 0, t, bass.ds(i * 4 + j, 1)]
                        w = items[:, 1, t, bass.ds(i * 4 + j, 1)]
                        c = slice(CAP2 * j, CAP2 * (j + 1))
                        V.tensor_scalar(Pg[:, t, c], iota[:, 0:CAP2], r, None, ALU.is_equal)
                        ins = V.tensor_scalar(Pw[:, t, c], iota[:, 0:CAP2], r, w, ALU.is_equal, ALU.mult)
                ins.then_inc(p2_ready, 1)
                for half in range(2):
                    dve.wait_ge(gathered2, i * 2 + (half + 1))
                    V.tensor_copy(xg[:, 4 * half:4 * half + 4, :], psum[:, 4, :].rearrange("p (k c) -> p k c", k=4))\
                     .then_inc(g2_copied, 1)
                dve.wait_ge(pwT2_done, i + 2)
                V.tensor_copy(PwT, psum[:, 6, 0:T]).then_inc(pwT2_copied, 1)
                for e in range(4):
                    dve.wait_ge(sil2_ready, i * 4 + (e + 1))
                    V.tensor_tensor(aT2[e].rearrange("p (h f) c -> p f h c", h=2),
                                    sil2.rearrange("p (f h c) -> p f h c", f=4, h=2),
                                    psum[:, 6, :].rearrange("p (f g h c) -> p f g h c", f=4, g=2, h=2)[:, :, 1], ALU.mult)\
                     .then_inc(aT2_ready, 1)
                dve.wait_ge(used_b, i * 24 + (NB + 24))
                dve.wait_ge(scattered2, i + 1)
                V.tensor_copy(y_s[:, 512:D], psum[:, 7, :]).then_inc(y21_copied, 1)
            dve.wait_ge(scattered2, TURNS2 + 1)
            for j in range(4):
                add_accumulated(j, None)
            dve.wait_ge(acc_read, 8)
            for k in range(4, KT):
                ins = V.tensor_scalar(hT[:, k, :], xT[:, k, :], vcol("norm_final_g_2", k), None, ALU.mult)
            ins.then_inc(dve_gained, 1)
            mean(7)
            evacuated(dve, "rstdT")
            for j in (0, 2):
                ps = full(dve, f"oN{j}")
                frees(V.tensor_scalar(oN[:, j // 2, 0:512], ps, rstd_col[:, j // 2:j // 2 + 1], None, ALU.mult), f"oN{j}")

        @block.tensor
        def _(pe):
            mm = nc.tensor.matmul
            turn = nc.tensor.transpose
            opened = []

            def start(name):
                opened.append(name)
                b, use = AT[name]
                if use:
                    pe.wait_ge(bank_free[b], use)
                return bank(name)

            def done(ins, name):
                ins.then_inc(bank_full[AT[name][0]], 1)

            def product(ps_of, w, x, rows=None):
                name, k0 = x
                hi, lo = (part[:, k0:k0 + w[0].shape[1], :] for part in PARTS[name])
                nk = w[0].shape[1]
                for k in range(nk):
                    if (k0 + k) % 2 == 0:
                        pe.wait_ge(x_low, 4 * PART_AT[name] + (k0 + k) // 2 + 1)
                    for i, (a_, b_) in enumerate(((w[0], hi), (w[0], lo), (w[1], hi))):
                        ins = ps_of(a_, b_, k, k == 0 and i == 0, k == nk - 1 and i == 2)
                return ins

            def project(name, w, x, m):
                ps = start(name)
                for t in range(2):
                    c = slice((m + t) * P, (m + t + 1) * P)
                    ins = product(lambda a_, b_, k, first, last: mm(ps[:, t * T:(t + 1) * T], a_[:, k, c], b_[:, k, :],
                                                                    start=first, stop=last), w, x)
                done(ins, name)

            def project_rows(name, w, x, t):
                ps = start(name)
                done(product(lambda a_, b_, k, first, last: mm(ps, b_[:, k, t * P:(t + 1) * P], a_[:, k, :],
                                                               start=first, stop=last), w, x), name)

            def project_whole(name, w, src, m):
                ps = start(name)
                nk = w.shape[1]
                for t in range(2):
                    for k in range(nk):
                        ins = mm(ps[:, t * T:(t + 1) * T], w[:, k, (m + t) * P:(m + t + 1) * P], src[:, k, :],
                                 start=(k == 0), stop=(k == nk - 1))
                done(ins, name)

            def mean_square(n, sqb, ks=range(KT)):
                ps = start(f"ms{n}") if ks[0] == 0 else bank(f"ms{n}")
                base = 4 * n + (1 - 4) * (n > 4)
                for k in ks:
                    if k % 2 == 0:
                        pe.wait_ge(squares_ready, base + k // 2 + 1)
                    ins = mm(ps[:, 0:T], ones, sqb[:, k, :], start=(k == 0), stop=(k == KT - 1))
                if k == KT - 1:
                    done(ins, f"ms{n}")

            def chunk(part, n):
                name, _, cols, k = (CHUNKS_A if part == "a" else CHUNKS_B)[n]
                s = where((part, n))[0]
                v = lambda ap: ap[:, 0:k * cols].rearrange("p (k c) -> p k c", k=k)
                if name in WHOLE:
                    arrived(pe, (part, n))
                    return v(ring[:, s, :])
                pe.wait_ge(w_low, 4 * SPLIT_AT[(part, n)] + 4)
                return v(ring_r[:, (s + 1) % RING, :]), v(ring_r[:, s, :])

            chunk_a = lambda n, cols=None: chunk("a", n)
            chunk_b = lambda n, cols=None: chunk("b", n)

            def used(sem_, slots=2):
                pe.sem_inc(sem_, slots)

            pe.wait_ge(cst_in, 48)
            pe.wait_ge(rows_in, 16 * (len(VEC) + len(VEC2)))
            pe.wait_ge(rows_zeroed, 1)
            ps = start("vec")
            for h in range(2):
                ins = turn(ps[:, h * P:(h + 1) * P], vec_rows[:, h, :], ident)
            done(ins, "vec")
            for src, arrival, nm in ((memN, mem_in, "memT"), (xN, x_in, "xT")):
                pe.wait_ge(arrival, 16)
                for j in range(4):
                    ps = start(f"{nm}{j}")
                    for k in range(2):
                        for t in range(TT):
                            ins = turn(ps[:, k * T + t * P:k * T + (t + 1) * P], src[:, t, (2 * j + k) * P:(2 * j + k + 1) * P], ident)
                    done(ins, f"{nm}{j}")
            mean_square(0, sq[0])
            mean_square(1, sq[1])
            pe.wait_ge(cs32_ready, 1)
            sel_col = cst[:, C_SEL:C_SEL + 1]

            def columns(n):
                evacuated(pe, f"ada{n}")
                for b in range(4):
                    m = 4 * n + b
                    ins = mm(psum[:, 7, m:m + 1], ada_rows[n % 2][:, b * P:(b + 1) * P], sel_col, start=True, stop=True)
                ins.then_inc(mod_full, 1)

            def modulation(n, place):
                w = chunk_a(place, 512)
                ps = start(f"ada{n}")
                for k in range(2):
                    for q in range(4):
                        ins = mm(ps[32 * q:32 * q + 32, :], cs32[:, 2 * q + k, :], w[:, 2 * q + k, :],
                                 start=(k == 0), stop=(k == 1))
                done(ins, f"ada{n}")
                full(pe, f"ada{n}")
                used(used_a, 1)
                if n == ADA_FIRST:
                    pe.wait_ge(mod_ready, 1)
                elif n >= 1:
                    columns(n - 1)

            for i, x in enumerate(START):
                g = START[:i].count(x)
                if x == "a":
                    modulation(g, i)
                    continue
                w = chunk_a(i)
                for j in range(2):
                    if g < 2:
                        project(f"memkv{g}_{j}", w, ("mem", 0), 2 * j)
                    else:
                        project_rows(f"memkv{g}_{j}", w, ("mem", 0), j)
                    if g == 1 and j == 0:
                        columns(ADA_FIRST - 1)
                full(pe, f"memkv{g}_1")
                used(used_a)
                if g == 0:
                    pe.wait_ge(relb_ready, 1)
                for h in (2 * g, 2 * g + 1):
                    ps = start(f"rel{h}")
                    done(mm(ps[:, 0:T], relb[0:32, h, :], onehot[0:32, :], start=True, stop=True), f"rel{h}")

            n0 = IN_A[9] - 9
            for c in range(6):
                w = chunk_a(IN_A[c], 512)
                for j in range(2):
                    if c in (2, 5):
                        project_rows(f"in{c}_{j}", w, ("h1", 0), j)
                    else:
                        project(f"in{c}_{j}", w, ("h1", 0), 2 * j)
                full(pe, f"in{c}_1")
                used(used_a)
                modulation(ADA_FIRST + c, IN_A[c] + 1)
            for j in range(2):
                for c in range(6):
                    evacuated(pe, f"in{c}_{j}")
            for s in range(HEADS + 2):
                if s < HEADS:
                    h, r = s, 64 * (s % 2)
                    ps = start(f"z{h}")
                    q, k = QK[r:r + 64, h // 2, :], QK[r:r + 64, 4 + h // 2, :]
                    mm(ps[:, 0:T], k[:, 0:P], q, start=True, stop=True)
                    done(mm(ps[:, T:T + P], k[:, P:T], q[:, P:T], start=True, stop=True), f"z{h}")
                    ps = start(f"s{h}")
                    q, k = QK[r:r + 64, 8 + h // 2, :], QK[r:r + 64, 12 + h // 2, :]
                    mm(ps[:, 0:P], q[:, 0:P], k[:, 0:P], start=True, stop=True)
                    done(mm(ps[:, P:W3], q[:, P:T], k, start=True, stop=True), f"s{h}")
                    c = 6 + s // 2
                    if s % 2 == 0:
                        w_g = chunk_a(IN_A[c], 512)
                    project(f"in{c}_{s % 2}", w_g, ("h1", 0), 2 * (s % 2))
                    if s % 2:
                        full(pe, f"in{c}_1")
                        used(used_a)
                    if s in (1, 3):
                        modulation(ADA_FIRST + 6 + s // 2, IN_A[c] + 1)
                if 1 <= s <= HEADS:
                    h = s - 1
                    pe.wait_ge(sb_rest, h + 1)
                    ps = start(f"skip{h}")
                    mm(ps[:, 0:T], after, sc_lr[:, 0:T], start=True, stop=False, skip_group_check=True)
                    mm(ps[:, P:T], ones, sc_lr[:, T:W3], start=False, stop=False, skip_group_check=True)
                    done(mm(ps[:, T:W3], after, sc_lr[:, T:W3], start=False, stop=True, skip_group_check=True), f"skip{h}")
                    pe.wait_ge(at_p_ready, h + 1)
                    ps = start(f"pT{h}")
                    p = sc_p[h % 2]
                    turn(ps[:, 0:P], p[:, 0:P], ident)
                    turn(ps[:, P:T], p[:, P:T], ident)
                    done(turn(ps[:, T:W3], p[:, T:W3], ident), f"pT{h}")
                if s == 4:
                    columns(ADA - 1)
                if s >= 2:
                    h, r = s - 2, 64 * (s % 2)
                    ps = start(f"av{h}")
                    pe.wait_ge(sb_a, h + 1)
                    evacuated(pe, f"pT{h}")
                    for b, pr in ((0, sc_a[h % 2]), (1, sc_pT[h % 2])):
                        o = b * T
                        v = V1[:, :, b * 512 + h * HD:b * 512 + (h + 1) * HD]
                        mm(ps[r:r + 64, o:o + T], v[:, 0, :], pr[:, 0:T], start=True, stop=False, skip_group_check=True)
                        ins = mm(ps[r:r + 64, o + P:o + T], v[:, 1, :], pr[:, T:W3], start=False, stop=True, skip_group_check=True)
                    done(ins, f"av{h}")
            ws = chunk_a(n0 + 10)
            for j in range(4):
                project(f"brs_{j}", ws, ("O", 0), 2 * j)
                if j == 0:
                    wm = chunk_a(n0 + 11)
                project(f"brm_{j}", wm, ("O", 4), 2 * j)
            full(pe, "brm_3")
            used(used_a, 4)
            pe.wait_ge(again_in, 16)
            for j in range(4):
                ps = start(f"again{j}")
                for k in range(2):
                    for t in range(TT):
                        ins = turn(ps[:, k * T + t * P:k * T + (t + 1) * P], xN[:, t, (2 * j + k) * P:(2 * j + k + 1) * P], ident)
                done(ins, f"again{j}")
            for j in range(4):
                if j % 2 == 0:
                    w = chunk_a(n0 + 12 + j // 2)
                project(f"out{j}", w, ("merged", 0), 2 * (j % 2))
                if j == 2:
                    mean_square(2, sq_g, range(4))
                if j % 2:
                    full(pe, f"out{j}")
                    used(used_a)
            mean_square(2, sq_g, range(4, KT))
            pe.wait_ge(wr1_in, 16)
            ps = start("logit1")
            for k in range(KT):
                pe.wait_ge(act_func, k + 1)
                r = E1 * (k % 2)
                ins = mm(ps[r:r + E1, 0:T], wr1[:, k, :], hT[:, k, :], start=(k < 2), stop=(k >= KT - 2))
            done(ins, "logit1")

            def logits(name, parts, n, col):
                evacuated(pe, parts)
                ps = start(name)
                for t in range(TT):
                    ins = mm(ps[:, t * n:(t + 1) * n], partial[:, t * P:(t + 1) * P], cst[:, col:col + n], start=True, stop=True)
                done(ins, name)

            def rows_of_h(prefix, after_first):
                for j in range(4):
                    ps = start(f"{prefix}{j}")
                    t, half = j // 2, j % 2
                    for k in range(4):
                        ins = turn(ps[:, k * P:(k + 1) * P], hT[:, 4 * half + k, t * P:(t + 1) * P], ident)
                    done(ins, f"{prefix}{j}")
                    if j == 0:
                        after_first()

            rows_of_h("hN", lambda: logits("route1", "logit1", E1, C_SUM1))
            arrived(pe, ("a", n0 + 14))
            w = ring[:, SLOT_A[n0 + 14] % RING, :].rearrange("p (g k f) -> p g k f", g=2, k=KT)
            project_whole("shg", w[:, 0], hT, 0)
            project_whole("shu", w[:, 1], hT, 0)
            full(pe, "shu")
            used(used_a, 1)
            pe.wait_ge(route_ready, 2)
            sel = rt[:, 896:1024]
            ps = start("rank1")
            mm(ps[:, 0:E1], before, sel[:, 0:E1], start=True, stop=True)
            mm(ps[:, E1:2 * E1], ones, sel[:, 0:E1], start=True, stop=False)
            done(mm(ps[:, E1:2 * E1], before, sel[:, E1:2 * E1], start=False, stop=True), "rank1")
            ps = start("count1")
            mm(ps[0:64, 0:1], sel[:, 0:E1], ones[:, 0:1], start=True, stop=False)
            done(mm(ps[0:64, 0:1], sel[:, E1:2 * E1], ones[:, 0:1], start=False, stop=True), "count1")
            pe.wait_ge(route_ready, 4)
            ps = start("start1")
            done(mm(ps[0:64, 0:1], before[0:64, 0:64], rt[0:64, 1417:1418], start=True, stop=True), "start1")
            ps = start("tabT")
            rk, wts = rt[:, 1152:1280], rt[:, 1024:1152]
            for i, src in enumerate((rk, wts)):
                for t in range(TT):
                    ins = turn(ps[0:64, i * T + t * P:i * T + (t + 1) * P], src[:, t * E1:(t + 1) * E1], ident)
            done(ins, "tabT")
            pe.wait_ge(route_ready, 5)
            rT = buf(8, 512, 512)
            OH, CH = rt[0:64, 1440:1472], rt[0:64, 1472:1504]
            ps = start("item")
            for t in range(TT):
                mm(ps[:, t * 32:(t + 1) * 32], rT[0:64, t * P:(t + 1) * P], OH, start=True, stop=False)
                mm(ps[:, t * 32:(t + 1) * 32], ones[0:64, :], CH, start=False, stop=True)
            for t in range(TT):
                ins = mm(ps[:, 64 + t * 32:64 + (t + 1) * 32], rT[0:64, T + t * P:T + (t + 1) * P], OH, start=True, stop=True)
            done(ins, "item")
            ps = start("eidx")
            mm(ps[0:1, 0:32], cst[0:64, C_PIDX:C_PIDX + 1], OH, start=True, stop=True)
            done(mm(ps[0:1, 32:33], rt[0:64, 1417:1418], ones[0:64, 0:1], start=True, stop=True), "eidx")

            wd = chunk_a(n0 + 15, 1024)
            for nm in last_uses(opened):
                evacuated(pe, nm)
            acc = lambda m: psum[:, m // 2, (m % 2) * T:(m % 2) * T + T]
            for m in range(KT):
                for k in range(2):
                    ins = mm(acc(m), wd[:, k, m * P:(m + 1) * P], sha[:, k, :], start=(k == 0 and m % 2 == 0), stop=False,
                             skip_group_check=True)
            ins.then_inc(acc_ready, 1)
            pe.wait_ge(acc_ready, 1)
            used(used_a, 1)

            for nm in ("hN0", "hN1", "hN2", "hN3"):
                evacuated(pe, nm)
            pe.wait_ge(table_ready, 1)
            extra = pe.value_load(tab_i[0:1, 32:33], min_val=0, max_val=EXTRA // 4)
            turns1 = pe.snap(extra + TURNS1)

            def scatter1(pair, m0, m1):
                for m in range(m0, m1):
                    for y in (y_hi, y_lo):
                        ins = mm(acc(m), y[:, m * P:(m + 1) * P], PT1[pair], start=False, stop=False, skip_group_check=True)
                return ins

            def gather1(quarter):
                for k in range(2):
                    for t in range(TT):
                        for h in (hN_hi, hN_lo):
                            kk = 2 * quarter + k
                            ins = mm(psum[:, 4 + 3 * (quarter % 2), k * T:(k + 1) * T], h[:, t, kk * P:(kk + 1) * P], Pg1[:, t, :],
                                     start=(t == 0 and h is hN_hi), stop=(t == TT - 1 and h is hN_lo))
                ins.then_inc(gathered, 1)

            def onehot_turn(pair):
                for t in range(TT):
                    turn(psum[:, 6, t * P:(t + 1) * P], Pg1_32[:, t, pair * P:(pair + 1) * P], ident)
                for t in range(TT):
                    ins = mm(psum[:, 6, T:T + 1], Pw1[:, t, pair * P:(pair + 1) * P], ones[:, 0:1], start=(t == 0), stop=(t == TT - 1))
                ins.then_inc(pT_done, 1)

            pe.wait_ge(p_ready, 1)
            gather1(0)
            gather1(1)
            for q in (2, 3):
                pe.wait_ge(g_copied, q - 1)
                gather1(q)
            onehot_turn(0)
            with pe.Fori(0, turns1) as i:
                for j in range(PAIRS_PER_TURN):
                    c = 3 * j
                    arrived_moe1(pe, i, c)
                    arrived_moe1(pe, i, c + 1)
                    pe.wait_ge(g_copied, i * 4 + 4)
                    ws = [ring[:, (NA + c + e) % RING, :].rearrange("p (g k f) -> p g k f", g=2, k=KT) for e in range(2)]
                    for k in range(KT):
                        for e in range(2):
                            ins = mm(psum[64 * e:64 * e + 64, 5, :], xg1[:, k, P * j + 64 * e:P * j + 64 * e + 64], ws[e][:, :, k, :],
                                     start=(k == 0), stop=(k == KT - 1))
                    ins.then_inc(used_a, 2)
                    pe.wait_ge(y_copied, i * 2 + (j + 1))
                    if j == 0:
                        scatter1(1, 0, 4)
                    else:
                        pe.wait_ge(p_ready, i + 2)
                        gather1(0)
                    pe.wait_ge(gu_copied, i * 2 + (j + 1))
                    pe.wait_ge(pT_copied, i * 2 + (j + 1))
                    for b in range(4):
                        src = gu_s[:, 256 * (b // 2) + b % 2:256 * (b // 2) + 256:2]
                        ins = turn(psum[:, 6, b * P:(b + 1) * P], src, ident)
                    ins.then_inc(turned, 1)
                    if j == 0:
                        scatter1(1, 4, 8).then_inc(scattered, 1)
                    else:
                        gather1(1)
                        pe.wait_ge(g_copied, i * 4 + 5)
                        gather1(2)
                        scatter1(0, 0, 8).then_inc(scattered, 1)
                        pe.wait_ge(g_copied, i * 4 + 6)
                        gather1(3)
                    pe.wait_ge(aT_ready, i * 2 + (j + 2))
                    arrived_moe1(pe, i, c + 2)
                    wd = ring[:, (NA + c + 2) % RING, :].rearrange("p (e k f) -> p e k f", e=2, k=2)
                    for half in range(2):
                        if j == 1:
                            pe.wait_ge(g_copied, i * 4 + (7 + half))
                        b = 4 + 3 * half
                        for k in range(2):
                            for e in range(2):
                                ins = mm(psum[64 * e:64 * e + 64, b, :], aT1[:, k * P + 64 * e:k * P + 64 * e + 64],
                                         wd[:, e, k, half * 512:(half + 1) * 512], start=(k == 0), stop=(k == 1))
                        ins.then_inc(used_a if half else y0_done, 1)
                    onehot_turn((j + 1) % 2)
            pe.wait_ge(y_copied, turns1 * 2 + 1)
            scatter1(1, 0, 8).then_inc(scattered, 1)

            p3, p4 = start("ms3"), start("ms4")
            assert AT["ms3"][0] > 3 and AT["ms4"][0] > 3
            for ps, sqb, ready, base in ((p3, sq[1], act_squares, 0), (p4, sq_g, squares_ready, 12)):
                for k in range(KT):
                    if k % 2 == 0:
                        pe.wait_ge(ready, base + k // 2 + 1)
                    ins = mm(ps[:, 0:T], ones, sqb[:, k, :], start=(k == 0), stop=(k == KT - 1))
                done(ins, "ms3" if ready is act_squares else "ms4")
            pe.wait_ge(acc_read, 4)
            w = chunk_b(0)
            project("cq", w, ("h4", 0), 0)
            project("ckv", w, ("h4", 0), 2)
            full(pe, "ckv")
            used(used_b)
            for c in range(2):
                w = chunk_b(1 + c, 512)
                for j in range(2):
                    project(f"xc{2 * c + j}", w, ("h4", 0), 2 * j)
                full(pe, f"xc{2 * c + 1}")
                used(used_b)
                if c == 0:
                    pe.wait_ge(squares_ready, 17)
                    ps = start("msq")
                    for k in range(2):
                        mm(ps[:, 0:T], ones, lsq[:, k, :], start=(k == 0), stop=(k == 1))
                    done(mm(ps[:, T:2 * T], ones, lsq[:, 2, :], start=True, stop=True), "msq")
            pe.wait_ge(q_scaled, 2)
            w = chunk_b(3, 1536)
            HQ = MLA_NOPE + MLA_ROPE
            for j in range(4):
                ps = start(f"qn{j}")
                for t in range(2):
                    for k in range(2):
                        c0 = (2 * j + t) * HQ
                        ins = mm(ps[:, t * T:(t + 1) * T], w[:, k, c0:c0 + MLA_NOPE], low[:, k, :], start=(k == 0), stop=(k == 1))
                done(ins, f"qn{j}")
            for j in range(2):
                ps = start(f"qr{j}")
                for t in range(2):
                    for k in range(2):
                        for r in range(2):
                            c0 = (4 * j + 2 * t + r) * HQ + MLA_NOPE
                            ins = mm(ps[64 * r:64 * r + 64, t * T:(t + 1) * T], w[:, k, c0:c0 + MLA_ROPE], low[:, k, :],
                                     start=(k == 0), stop=(k == 1))
                done(ins, f"qr{j}")
            full(pe, "qr1")
            used(used_b, 1)
            w = chunk_b(4, 2048)
            HK = MLA_NOPE + MLA_V
            for j in range(4):
                ps = start(f"kn{j}")
                for t in range(2):
                    c0 = (2 * j + t) * HK
                    ins = mm(ps[:, t * T:(t + 1) * T], w[:, 0, c0:c0 + MLA_NOPE], low[:, 2, :], start=True, stop=True)
                done(ins, f"kn{j}")
            wv = w[:, 0, :].rearrange("p (h c) -> p h c", c=HK)
            for j in range(4):
                ps = start(f"v{j}")
                done(mm(ps, low[:, 2, (j // 2) * P:(j // 2 + 1) * P], wv[:, 4 * (j % 2):4 * (j % 2) + 4, MLA_NOPE:HK],
                        start=True, stop=True), f"v{j}")
            full(pe, "v3")
            used(used_b, 1)
            pe.wait_ge(rope_in, 16)
            perm = rope[:, R_PERM:R_PERM + P]
            for j in range(3):
                ps = start(f"rot{j}")
                if j < 2:
                    evacuated(pe, f"qr{j}")
                for n, m in enumerate((4 + 2 * j, 5 + 2 * j) if j < 2 else (3,)):
                    ins = mm(ps[:, n * T:(n + 1) * T], perm, low[:, m, :], start=True, stop=True)
                done(ins, f"rot{j}")
            pe.wait_ge(rope_done, 3)
            for j in range(4):
                evacuated(pe, f"qn{j}")
                evacuated(pe, f"kn{j}")
                evacuated(pe, f"v{j}")

            def fill(n):
                nonlocal w_f
                if n % 2 == 0:
                    w_f = chunk_b(5 + n // 2, 512)
                project(f"fill{n}", w_f, ("h4", 0), 2 * (n % 2))
                if n % 2:
                    full(pe, f"fill{n}")
                    used(used_b)

            w_f = None
            for s in range(HEADS + 2):
                if s < HEADS:
                    ps = start(f"ls{s}")
                    r = 64 * (s % 2)
                    for t in range(TT):
                        mm(ps[:, t * T:(t + 1) * T], qnT[:, s, t * P:(t + 1) * P], knT[:, s, :], start=True, stop=False)
                        ins = mm(ps[:, t * T:(t + 1) * T], low[r:r + 64, 4 + s // 2, t * P:(t + 1) * P], low[r:r + 64, 3, :],
                                 start=False, stop=True)
                    done(ins, f"ls{s}")
                    fill(2 * s)
                if 1 <= s <= HEADS:
                    h = s - 1
                    pe.wait_ge(at_p_ready, HEADS + h + 1)
                    ps = start(f"lp{h}")
                    for k in range(TT):
                        for t in range(TT):
                            ins = turn(ps[:, k * T + t * P:k * T + (t + 1) * P], at_p[h % 2][:, t * T + k * P:t * T + (k + 1) * P], ident)
                    done(ins, f"lp{h}")
                if s < HEADS:
                    fill(2 * s + 1)
                if s >= 2:
                    h = s - 2
                    ps = start(f"lo{h}")
                    evacuated(pe, f"lp{h}")
                    for k in range(TT):
                        ins = mm(ps[:, 0:T], vN[:, k, h * MLA_V:(h + 1) * MLA_V], at_pT[h % 2][:, k * T:(k + 1) * T],
                                 start=(k == 0), stop=(k == TT - 1))
                    done(ins, f"lo{h}")
            n = 13
            for nm, x in (("conv", "conv"), ("mla", "mla"), ("mix", "yn")):
                for j in range(4):
                    if j % 2 == 0:
                        w = chunk_b(n, 512)
                        n += 1
                    project(f"{nm}{j}", w, (x, 0), 2 * (j % 2))
                    if nm == "mix" and j == 2:
                        mean_square(5, sq[1], range(4))
                    if j % 2:
                        full(pe, f"{nm}{j}")
                        used(used_b)
            mean_square(5, sq[1], range(4, KT))
            for j in range(4):
                if j % 2 == 0:
                    w = chunk_b(n, 512)
                    n += 1
                project(f"mq{j}", w, ("h5", 0), 2 * (j % 2))
                if j % 2:
                    full(pe, f"mq{j}")
                    used(used_b)
            for j in range(4):
                evacuated(pe, f"mq{j}")
            def memory_scores(s):
                ps = start(f"mS{s}")
                for t in range(TT):
                    for k in range(2):
                        ins = mm(ps[:, t * T:(t + 1) * T], mqT[:, 2 * s + k, t * P:(t + 1) * P], memK[:, 2 * s + k, :],
                                 start=(k == 0), stop=(k == 1))
                done(ins, f"mS{s}")

            memory_scores(0)
            memory_scores(1)
            for h in range(MEMH):
                pe.wait_ge(at_p_ready, 2 * HEADS + h + 1)
                ps = start(f"mP{h}")
                for k in range(TT):
                    for t in range(TT):
                        ins = turn(ps[:, k * T + t * P:k * T + (t + 1) * P], at_p[h % 2][:, t * T + k * P:t * T + (k + 1) * P], ident)
                done(ins, f"mP{h}")
                if h + 2 < MEMH:
                    memory_scores(h + 2)
                ps = start(f"mO{h}")
                evacuated(pe, f"mP{h}")
                for m in range(2):
                    for k in range(TT):
                        ins = mm(ps[:, m * T:(m + 1) * T], memV[:, k, (2 * h + m) * P:(2 * h + m + 1) * P],
                                 at_pT[h % 2][:, k * T:(k + 1) * T], start=(k == 0), stop=(k == TT - 1))
                done(ins, f"mO{h}")
            for j in range(4):
                if j % 2 == 0:
                    w = chunk_b(n, 512)
                    n += 1
                project(f"mo{j}", w, ("mo", 0), 2 * (j % 2))
                if j == 2:
                    mean_square(6, sq_g, range(4))
                if j % 2:
                    full(pe, f"mo{j}")
                    used(used_b)
            assert n == len(CHUNKS_B)
            mean_square(6, sq_g, range(4, KT))
            pe.wait_ge(wr2_in, 16)
            pe.wait_ge(normed, 14)
            ps = start("logit2")
            for k in range(KT):
                r = 32 * (k % 4)
                ins = mm(ps[r:r + 32, 0:T], wr2_flat[:, k * E2:k * E2 + 32], hT[:, k, :], start=(k < 4), stop=(k >= 4))
            done(ins, "logit2")
            rows_of_h("gN", lambda: logits("route2", "logit2", E2, C_SUM2))
            pe.wait_ge(route_ready, 6)
            ps = start("affT")
            for t in range(TT):
                ins = turn(ps[0:E2, t * P:(t + 1) * P], rt2[:, t, :], ident)
            done(ins, "affT")
            pe.wait_ge(route_ready, 7)
            ps = start("selT")
            for t in range(TT):
                ins = turn(ps[:, t * E2:(t + 1) * E2], rt[0:E2, 512 + t * P:512 + (t + 1) * P], ident[0:E2, 0:E2])
            done(ins, "selT")
            pe.wait_ge(route_ready, 8)
            ps = start("rank2")
            mm(ps[:, 0:E2], before, sel2[:, 0:E2], start=True, stop=True)
            mm(ps[:, E2:2 * E2], ones, sel2[:, 0:E2], start=True, stop=False)
            done(mm(ps[:, E2:2 * E2], before, sel2[:, E2:2 * E2], start=False, stop=True), "rank2")
            for nm in last_uses(opened):
                evacuated(pe, nm)
            for nm in ("gN0", "gN1", "gN2", "gN3"):
                evacuated(pe, nm)
            pe.wait_ge(zeros_ready, 1)

            def gather(half, done_sem):
                for k in range(4):
                    for t in range(TT):
                        kk = 4 * half + k
                        ins = mm(psum[:, 4, k * P:(k + 1) * P], hN[:, t, kk * P:(kk + 1) * P], Pg[:, t, :],
                                 start=(t == 0), stop=(t == TT - 1))
                ins.then_inc(done_sem, 1)

            def weights_turn(done_sem):
                for t in range(TT):
                    ins = turn(psum[:, 6, t * P:(t + 1) * P], Pw[:, t, :], ident)
                ins.then_inc(done_sem, 1)

            def scatter(m0, wT):
                for m in range(m0, m0 + 4):
                    ins = mm(acc(m), y_s[:, m * P:(m + 1) * P], wT, start=False, stop=False, skip_group_check=True)
                return ins

            pe.sem_inc(pwT2_done, 1)
            pe.sem_inc(scattered2, 1)
            for m in range(0, KT, 2):
                mm(psum[:, m // 2, :], zeros, cst[:, 0:512], start=True, stop=False, skip_group_check=True)
            with pe.Fori(0, TURNS2) as i:
                pe.wait_ge(p2_ready, i + 1)
                pe.wait_ge(g2_copied, i * 2 + 1)
                gather(0, gathered2)
                pe.wait_ge(g2_copied, i * 2 + 2)
                gather(1, gathered2)
                weights_turn(pwT2_done)
                pe.wait_ge(g2_copied, i * 2 + 3)
                for e in range(4):
                    b = 5 + 2 * (e % 2)
                    if e == 0:
                        pe.wait_ge(y20_copied, i + 1)
                    if e == 1:
                        pe.wait_ge(y21_copied, i + 1)
                    for c in range(4 * e, 4 * e + 4):
                        arrived_moe2(pe, i, c)
                        w = ring[:, (NA + NB + c) % RING, :].rearrange("p (g k f) -> p g k f", g=2, k=2)
                        for k in range(2):
                            for q in range(4):
                                kk = 2 * (c % 4) + k
                                ins = mm(psum[32 * q:32 * q + 32, b, :], xg[:, kk, CAP2 * e:CAP2 * (e + 1)],
                                         w[:, q // 2, k, (q % 2) * 512:(q % 2 + 1) * 512], start=(kk == 0), stop=(kk == KT - 1))
                        ins.then_inc(used_b, 1)
                    pe.wait_ge(gu2_copied, i * 4 + (e + 1))
                    if e == 0:
                        pe.wait_ge(pwT2_copied, i + 1)
                    else:
                        pe.wait_ge(aT2_ready, i * 4 + (e + 1))
                    for f in range(4):
                        ins = turn(psum[:, 6, f * P:(f + 1) * P], gu_s[:, f * P:(f + 1) * P], ident)
                    ins.then_inc(turned2, 1)
                pe.wait_ge(aT2_ready, i * 4 + 5)
                for c in range(16, 24):
                    arrived_moe2(pe, i, c)
                    w = ring[:, (NA + NB + c) % RING, :].rearrange("p (e f) -> p e f", e=4)
                    k = c - 16
                    for half in range(2):
                        for e in range(4):
                            ins = mm(psum[32 * e:32 * e + 32, 5 + 2 * half, :], aT2[e][:, k, :],
                                     w[:, e, half * 512:(half + 1) * 512], start=(k == 0), stop=(k == KT - 1))
                    ins.then_inc(used_b, 1)
                pe.wait_ge(y20_copied, i + 2)
                scatter(0, PwT)
                pe.wait_ge(y21_copied, i + 2)
                scatter(4, PwT).then_inc(scattered2, 1)
            ps = start("ms7")
            for k in range(KT):
                if k % 2 == 0:
                    pe.wait_ge(act_squares, 4 + k // 2 + 1)
                ins = mm(ps[:, 0:T], ones, sq[1][:, k, :], start=(k == 0), stop=(k == KT - 1))
            done(ins, "ms7")
            for j in range(4):
                if j < 2:
                    pe.wait_ge((gained, dve_gained)[j], 1)
                ps = start(f"oN{j}")
                t, half = j // 2, j % 2
                for k in range(4):
                    ins = turn(ps[:, k * P:(k + 1) * P], hT[:, 4 * half + k, t * P:(t + 1) * P], ident)
                done(ins, f"oN{j}")
                if j == 0:
                    pe.wait_ge(mean_ready, 8)
                    ps = start("rstdT")
                    for t in range(TT):
                        ins = turn(ps[:, t * P:(t + 1) * P], rstd_of(7)[:, t * P:(t + 1) * P], ident)
                    done(ins, "rstdT")
            assert opened == JOBS + JOBS2, [x for x in zip(opened, JOBS + JOBS2) if x[0] != x[1]][:3]


_OUTS = [((1, T, D), "float32")]


def kernel(**inputs):
    import numpy as _np
    import concourse.bacc as _bacc
    from concourse import mybir as _mybir
    from concourse.bass_utils import run_bass_kernel_spmd as _run

    nc = _bacc.Bacc("TRN2", target_bir_lowering=False, num_devices=1)
    arrays, aps = {}, {}
    for name, value in {**inputs, **shape_tables()}.items():
        x = _np.ascontiguousarray(value)
        arrays[f"in_{name}_dram"] = x
        aps[name] = nc.dram_tensor(f"in_{name}_dram", x.shape, _mybir.dt.from_np(x.dtype), kind="ExternalInput").ap()
    out = nc.dram_tensor("out_0_dram", _OUTS[0][0], _mybir.dt.from_np(_np.dtype(_OUTS[0][1])), kind="ExternalOutput").ap()
    build(nc, aps, out)
    r = _run(nc, [arrays], core_ids=[0])
    return r.results[0]["out_0_dram"]
```
